# Optimizing a Trainium2 kernel written in Bass

```python
import math
import jax, jax.numpy as jnp
from jax import lax
import numpy as np

D_MODEL = 1024
BATCH = 1
SEQ = 512
DEPTH = 1
DEC_BATCH = 8
DEC_SEQ = 1
PAST_LEN = 4096
PAGE_SIZE = 128

N_META = 16
MIX_WIDTH = D_MODEL
SSM_WIDTH = MIX_WIDTH // 2
CONV_WIDTH = MIX_WIDTH - SSM_WIDTH
SSM_GROUP_CH = 16
SSM_GROUPS = SSM_WIDTH // SSM_GROUP_CH
SSM_STATE = 64
CONV_HEADS = 8
CONV_HEAD_DIM = CONV_WIDTH // CONV_HEADS
CONV_K = 3
N_EXPERTS = 32
TOP_K = 4
D_FF = D_MODEL
SWIGLU_LIMIT = 7.0
SWIGLU_ALPHA = 1.702
MOE_BLOCK = 128
EPS = 1e-5
DT_MIN = 1e-3
DT_MAX = 1e-1

kernel_name = "hymba_s5_shortconv_moe_step"

def rmsnorm(x, g):
    xf = x.astype(jnp.float32)
    xf = xf * lax.rsqrt(jnp.mean(xf * xf, axis=-1, keepdims=True) + EPS)
    return xf.astype(x.dtype) * g

def _lin_combine(left, right):
    a_l, b_l = left
    a_r, b_r = right
    return a_r * a_l, a_r * b_l + b_r

def ssm_mixer(u, s0_re, s0_im, a_re, a_im, log_dt, b_re, b_im, c_re, c_im, d_skip, w_glu, b_glu):
    bt, L, _ = u.shape
    f32 = jnp.float32
    uf = u.astype(f32).reshape(bt, L, SSM_GROUPS, SSM_GROUP_CH)
    A = lax.complex(a_re.astype(f32), a_im.astype(f32))
    dtA = A * jnp.exp(log_dt.astype(f32))[:, None]
    a_bar = jnp.exp(dtA)
    b_bar = ((a_bar - 1.0) / A)[:, :, None] * lax.complex(b_re.astype(f32), b_im.astype(f32))
    bu = jnp.einsum('gnh,blgh->blgn', b_bar, uf.astype(jnp.complex64))
    decay = jnp.broadcast_to(a_bar, bu.shape)
    _, s = lax.associative_scan(_lin_combine, (decay, bu), axis=1)
    steps = jnp.arange(1, L + 1, dtype=f32)[:, None, None]
    s0 = lax.complex(s0_re.astype(f32), s0_im.astype(f32))
    s = s + jnp.exp(dtA[None] * steps)[None] * s0[:, None]
    Cc = lax.complex(c_re.astype(f32), c_im.astype(f32))
    y = jnp.einsum('ghn,blgn->blgh', Cc, s).real + d_skip.astype(f32).reshape(SSM_GROUPS, SSM_GROUP_CH) * uf
    y = jax.nn.gelu(y.reshape(bt, L, SSM_WIDTH))
    out = y * jax.nn.sigmoid(y @ w_glu.astype(f32) + b_glu.astype(f32))
    last = s[:, -1]
    return out.astype(u.dtype), jnp.real(last), jnp.imag(last)

def causal_conv(z, buf, w):
    L = z.shape[1]
    z_ext = jnp.concatenate([buf.astype(z.dtype), z], axis=1)
    y = w[0] * z_ext[:, 0:L]
    for k in range(1, CONV_K):
        y = y + w[k] * z_ext[:, k:k + L]
    return y, z_ext[:, L:]

def moe(x2, w_router, b_router, w_gate_up, b_gate_up, w_down, b_down):
    T = x2.shape[0]
    logits = (x2 @ w_router + b_router).astype(jnp.float32)
    top_v, top_i = lax.top_k(logits, TOP_K)
    gates = jax.nn.softmax(top_v, axis=-1)
    n_assign = T * TOP_K
    flat_e = top_i.reshape(-1).astype(jnp.int32)
    order = jnp.argsort(flat_e)
    sorted_e = flat_e[order]
    counts = jnp.bincount(flat_e, length=N_EXPERTS)
    start = jnp.cumsum(counts) - counts
    padded = ((counts + MOE_BLOCK - 1) // MOE_BLOCK) * MOE_BLOCK
    pend = jnp.cumsum(padded)
    pstart = pend - padded
    rank = jnp.arange(n_assign, dtype=jnp.int32) - start[sorted_e]
    dest_sorted = (pstart[sorted_e] + rank).astype(jnp.int32)
    n_blocks = (n_assign + N_EXPERTS * (MOE_BLOCK - 1) + MOE_BLOCK - 1) // MOE_BLOCK
    cap = n_blocks * MOE_BLOCK
    tok_sorted = (order // TOP_K).astype(jnp.int32)
    slot_tok = jnp.full((cap,), T, jnp.int32).at[dest_sorted].set(tok_sorted)
    blk_e = jnp.minimum(jnp.searchsorted(pend, jnp.arange(n_blocks) * MOE_BLOCK, side='right'), N_EXPERTS - 1)
    x_pad = jnp.concatenate([x2, jnp.zeros((1, x2.shape[1]), x2.dtype)], axis=0)
    xb = x_pad[slot_tok].reshape(n_blocks, MOE_BLOCK, x2.shape[1])

    def expert_block(args):
        xe, e = args
        gu = xe @ w_gate_up[e] + b_gate_up[e]
        gate, up = gu[:, :D_FF], gu[:, D_FF:]
        gate = jnp.minimum(gate, SWIGLU_LIMIT)
        up = jnp.clip(up, -SWIGLU_LIMIT, SWIGLU_LIMIT)
        h = gate * jax.nn.sigmoid(SWIGLU_ALPHA * gate) * (up + 1.0)
        return h @ w_down[e] + b_down[e]

    yb = lax.map(expert_block, (xb, blk_e)).reshape(cap, x2.shape[1])
    dest = jnp.zeros((n_assign,), jnp.int32).at[order].set(dest_sorted)
    y = yb[dest].reshape(T, TOP_K, x2.shape[1])
    return jnp.sum(y * gates[..., None].astype(y.dtype), axis=1)

def trunk(x, s_re, s_im, conv_buf, norm_mix, w_in, ssm_a_re, ssm_a_im, ssm_log_dt, ssm_b_re, ssm_b_im,
          ssm_c_re, ssm_c_im, ssm_d, w_glu, b_glu, conv_w, norm_out_ssm, norm_out_conv, w_out,
          norm_ffn, w_router, b_router, w_gate_up, b_gate_up, w_down, b_down, norm_final):
    new_re, new_im, new_buf = [], [], []
    for l in range(DEPTH):
        h = rmsnorm(x, norm_mix[l])
        proj = h @ w_in[l]
        u = proj[..., :SSM_WIDTH]
        zc = proj[..., SSM_WIDTH:SSM_WIDTH + CONV_WIDTH]
        gb = proj[..., SSM_WIDTH + CONV_WIDTH:SSM_WIDTH + 2 * CONV_WIDTH]
        gc = proj[..., SSM_WIDTH + 2 * CONV_WIDTH:]
        y_ssm, r_re, r_im = ssm_mixer(u, s_re[l], s_im[l], ssm_a_re[l], ssm_a_im[l], ssm_log_dt[l],
                                      ssm_b_re[l], ssm_b_im[l], ssm_c_re[l], ssm_c_im[l], ssm_d[l],
                                      w_glu[l], b_glu[l])
        y_conv, r_buf = causal_conv(gc * zc, conv_buf[l], conv_w[l])
        y_conv = gb * y_conv
        mix = jnp.concatenate([rmsnorm(y_ssm, norm_out_ssm[l]), rmsnorm(y_conv, norm_out_conv[l])], axis=-1)
        x = x + mix @ w_out[l]
        hf = rmsnorm(x, norm_ffn[l])
        bt, L, D = hf.shape
        x = x + moe(hf.reshape(bt * L, D), w_router[l], b_router[l], w_gate_up[l], b_gate_up[l],
                    w_down[l], b_down[l]).reshape(bt, L, D)
        new_re.append(r_re)
        new_im.append(r_im)
        new_buf.append(r_buf)
    return rmsnorm(x, norm_final), jnp.stack(new_re), jnp.stack(new_im), jnp.stack(new_buf)

def setup_inputs(seed: int = 0) -> dict:
    key = jax.random.key(seed)
    ks = jax.random.split(key, 32)
    f32 = jnp.float32
    nrm = lambda k, shape, s: (jax.random.normal(k, shape, f32) * s)
    n_idx = jnp.arange(SSM_STATE, dtype=f32)
    a_re = -0.5 + nrm(ks[5], (DEPTH, SSM_GROUPS, SSM_STATE), 0.01)
    a_im = math.pi * n_idx[None, None] + nrm(ks[6], (DEPTH, SSM_GROUPS, SSM_STATE), 0.01)
    log_dt = jax.random.uniform(ks[7], (DEPTH, SSM_GROUPS), f32, math.log(DT_MIN), math.log(DT_MAX))
    return {
        "x_prompt": nrm(ks[0], (BATCH, SEQ, D_MODEL), 1.0),
        "x_sample": nrm(ks[1], (DEC_BATCH, DEC_SEQ, D_MODEL), 1.0),
        "state_ssm_re": nrm(ks[2], (DEPTH, DEC_BATCH, SSM_GROUPS, SSM_STATE), 0.5),
        "state_ssm_im": nrm(ks[3], (DEPTH, DEC_BATCH, SSM_GROUPS, SSM_STATE), 0.5),
        "state_conv": nrm(ks[4], (DEPTH, DEC_BATCH, CONV_K - 1, CONV_WIDTH), 1.0),
        "meta_tokens": nrm(ks[8], (N_META, D_MODEL), 1.0),
        "norm_mix": 1.0 + nrm(ks[9], (DEPTH, D_MODEL), 0.02),
        "w_in": nrm(ks[10], (DEPTH, D_MODEL, SSM_WIDTH + 3 * CONV_WIDTH), D_MODEL ** -0.5),
        "ssm_a_re": a_re,
        "ssm_a_im": a_im,
        "ssm_log_dt": log_dt,
        "ssm_b_re": nrm(ks[11], (DEPTH, SSM_GROUPS, SSM_STATE, SSM_GROUP_CH), (2 * SSM_GROUP_CH) ** -0.5),
        "ssm_b_im": nrm(ks[12], (DEPTH, SSM_GROUPS, SSM_STATE, SSM_GROUP_CH), (2 * SSM_GROUP_CH) ** -0.5),
        "ssm_c_re": nrm(ks[13], (DEPTH, SSM_GROUPS, SSM_GROUP_CH, SSM_STATE), (2 * SSM_STATE) ** -0.5),
        "ssm_c_im": nrm(ks[14], (DEPTH, SSM_GROUPS, SSM_GROUP_CH, SSM_STATE), (2 * SSM_STATE) ** -0.5),
        "ssm_d": nrm(ks[15], (DEPTH, SSM_WIDTH), 1.0),
        "w_glu": nrm(ks[16], (DEPTH, SSM_WIDTH, SSM_WIDTH), SSM_WIDTH ** -0.5),
        "b_glu": nrm(ks[17], (DEPTH, SSM_WIDTH), 0.01),
        "conv_w": nrm(ks[18], (DEPTH, CONV_K, CONV_WIDTH), CONV_K ** -0.5),
        "norm_out_ssm": 1.0 + nrm(ks[19], (DEPTH, SSM_WIDTH), 0.02),
        "norm_out_conv": 1.0 + nrm(ks[20], (DEPTH, CONV_WIDTH), 0.02),
        "w_out": nrm(ks[21], (DEPTH, MIX_WIDTH, D_MODEL), MIX_WIDTH ** -0.5),
        "norm_ffn": 1.0 + nrm(ks[22], (DEPTH, D_MODEL), 0.02),
        "w_router": nrm(ks[23], (DEPTH, D_MODEL, N_EXPERTS), D_MODEL ** -0.5),
        "b_router": nrm(ks[24], (DEPTH, N_EXPERTS), 0.01),
        "w_gate_up": nrm(ks[25], (DEPTH, N_EXPERTS, D_MODEL, 2 * D_FF), D_MODEL ** -0.5),
        "b_gate_up": nrm(ks[26], (DEPTH, N_EXPERTS, 2 * D_FF), 0.01),
        "w_down": nrm(ks[27], (DEPTH, N_EXPERTS, D_FF, D_MODEL), D_FF ** -0.5),
        "b_down": nrm(ks[28], (DEPTH, N_EXPERTS, D_MODEL), 0.01),
        "norm_final": 1.0 + nrm(ks[29], (D_MODEL,), 0.02),
    }

def reference(x_prompt, x_sample, state_ssm_re, state_ssm_im, state_conv, meta_tokens, norm_mix, w_in,
              ssm_a_re, ssm_a_im, ssm_log_dt, ssm_b_re, ssm_b_im, ssm_c_re, ssm_c_im, ssm_d, w_glu, b_glu,
              conv_w, norm_out_ssm, norm_out_conv, w_out, norm_ffn, w_router, b_router, w_gate_up,
              b_gate_up, w_down, b_down, norm_final):
    bp = x_prompt.shape[0]
    meta = jnp.broadcast_to(meta_tokens[None].astype(x_prompt.dtype), (bp, N_META, D_MODEL))
    xp = jnp.concatenate([meta, x_prompt], axis=1)
    zeros_re = jnp.zeros((DEPTH, bp, SSM_GROUPS, SSM_STATE), jnp.float32)
    zeros_buf = jnp.zeros((DEPTH, bp, CONV_K - 1, CONV_WIDTH), x_prompt.dtype)
    y_p, p_re, p_im, p_conv = trunk(xp, zeros_re, zeros_re, zeros_buf, norm_mix, w_in, ssm_a_re, ssm_a_im,
                                    ssm_log_dt, ssm_b_re, ssm_b_im, ssm_c_re, ssm_c_im, ssm_d, w_glu, b_glu,
                                    conv_w, norm_out_ssm, norm_out_conv, w_out, norm_ffn, w_router, b_router,
                                    w_gate_up, b_gate_up, w_down, b_down, norm_final)
    y_prompt = y_p[:, N_META:]
    y_sample, s_re, s_im, s_conv = trunk(x_sample, state_ssm_re, state_ssm_im, state_conv, norm_mix, w_in,
                                         ssm_a_re, ssm_a_im, ssm_log_dt, ssm_b_re, ssm_b_im, ssm_c_re,
                                         ssm_c_im, ssm_d, w_glu, b_glu, conv_w, norm_out_ssm, norm_out_conv,
                                         w_out, norm_ffn, w_router, b_router, w_gate_up, b_gate_up, w_down,
                                         b_down, norm_final)
    return (y_prompt, y_sample, p_re, p_im, p_conv, s_re, s_im, s_conv)


_drawn_inputs = setup_inputs


def setup_inputs(seed=0):
    import zlib

    import numpy as np

    out = dict(_drawn_inputs(seed))
    spreads = {}
    factors = {'ssm_a_re': 56.207,
     'b_glu': 8.0,
     'norm_out_ssm': 10.651,
     'b_gate_up': 22.482,
     'b_down': 25.703,
     'norm_final': 24.419,
     'meta_tokens': 3.475,
     'norm_out_conv': 11.393,
     'b_router': 10.726,
     'norm_ffn': 3.614}
    for name, (base, spread) in spreads.items():
        noise = np.random.default_rng([zlib.crc32(name.encode()), seed]).standard_normal(out[name].shape)
        drawn = base * np.exp(spread * noise) if base else spread * noise
        out[name] = __import__('jax').numpy.asarray(drawn.astype(out[name].dtype))
    for name, factor in factors.items():
        out[name] = (out[name] * factor).astype(out[name].dtype)
    return out
```

```python
import math
from contextlib import ExitStack

import concourse.bass as bass
from concourse import mybir

F32 = mybir.dt.float32
BF16 = mybir.dt.bfloat16
I32 = mybir.dt.int32
U32 = mybir.dt.uint32
ALU = mybir.AluOpType
ACT = mybir.ActivationFunctionType
AX_X = mybir.AxisListType.X

P = 128
D = 1024
KD = D // P
NMETA, SEQ, NDEC = 16, 512, 8
NPROMPT = NMETA + SEQ
TOK = NPROMPT + NDEC
NT = (TOK + P - 1) // P
LAST = TOK - (NT - 1) * P
W = 512
MT = W // P
GROUPS, GCH, NS = 32, 16, 64
GP = GROUPS // 2
CH = 8
NCH = NPROMPT // CH
YC = NCH + 1 + NDEC
DEC0 = NCH + 1
UC = YC + NDEC
E = 32
TOPK = 4
FF = D
EPS = 1e-5
LIMIT = 7.0
ALPHA = 1.702
NOVER = (TOK * TOPK + E * (P - 1)) // P - E + 1
UNITS = 24
PAIRS = UNITS // 2
MISS = 4096.0
HALF = 264
REST = TOK - HALF


def rows(i):
    return P if i < NT - 1 else LAST


def refine_rsqrt(nc, done, r, t, v):
    done(nc.vector.reciprocal(r, r))
    done(nc.vector.tensor_tensor(t, r, r, ALU.mult))
    done(nc.vector.tensor_tensor(t, t, v, ALU.mult))
    done(nc.vector.tensor_scalar(t, t, -0.5, 1.5, ALU.mult, ALU.add))
    return nc.vector.tensor_tensor(r, r, t, ALU.mult)


def hybrid_step(nc, a, out):
    scratch = {
        "u": nc.dram_tensor("u_shuffle", [W, CH, YC], F32).ap(),
        "hf": nc.dram_tensor("ffn_in", [TOK, D], F32).ap(),
        "picked": nc.dram_tensor("expert_rows", [TOK * TOPK, D], F32).ap(),
    }
    with ExitStack() as ctx:
        def sb(stack, name, shape, dt=F32):
            return stack.enter_context(nc.sbuf_tensor(name, shape, dt))

        def sem(name):
            return ctx.enter_context(nc.semaphore(name))

        bank = [ctx.enter_context(nc.psum_tensor(f"bank{i}", [P, 512], F32)) for i in range(8)]
        keep = {
            "x": sb(ctx, "x", [P, NT, D]),
            "ident": sb(ctx, "ident", [P, P]),
            "pcol": sb(ctx, "pcol", [P, 36]),
            "ring_lo": sb(ctx, "ring_lo", [P, 16, 1024]),
        }
        with ExitStack() as st:
            mid = {
                "ymix": sb(st, "ymix", [P, MT, TOK]),
                "cmix": sb(st, "cmix", [P, MT, TOK]),
                "w_out": sb(st, "w_out", [P, KD, D]),
            }
            with ExitStack() as s1:
                mixer(nc, a, out, scratch, s1, sb, sem, bank, keep, mid)
            with ExitStack() as s2:
                tables = loop_tables(s2, sb)
                with ExitStack() as s3:
                    router(nc, a, scratch, s3, sb, sem, bank, keep, mid, tables)
                landed = keep["landed"]
                experts(nc, a, scratch, s2, sb, sem, bank, keep, mid, tables, landed)
        with ExitStack() as s4:
            combine(nc, a, out, scratch, s4, sb, sem, keep)


def mixer(nc, a, out, scratch, stack, sb, sem, bank, keep, mid):
    def buf(name, shape, dt=F32):
        return sb(stack, name, shape, dt)

    x, ident, pcol = keep["x"], keep["ident"], keep["pcol"]
    flat = keep["ring_lo"][:, :, :].rearrange("p a b -> p (a b)")
    BLK = KD * W
    w_in = flat.rearrange("p (blk k n) -> p blk k n", blk=4, k=KD)
    carve = [0]

    def late(n):
        v = flat[:, carve[0]:carve[0] + n]
        carve[0] += n
        return v

    toep = late(CH * W).rearrange("p (t n) -> p t n", t=CH)
    v_sb = late(2 * GP * UC).rearrange("p (r g c) -> p r g c", r=2, g=GP)
    s_sb = late(2 * GP * YC).rearrange("p (r g c) -> p r g c", r=2, g=GP)
    ZN = GP * NCH
    z0 = carve[0]
    y_ch = late(4 * ZN)[:, 0:MT * CH * YC]
    wz = [flat[:, z0 + i * ZN:z0 + (i + 1) * ZN] for i in range(4)]
    w_glu = late(MT * W).rearrange("p (k n) -> p k n", k=MT)
    wo_flat = mid["w_out"][:, :, :].rearrange("p a b -> p (a b)")
    PW = 2 * GP * CH * GCH
    p_sb = wo_flat[:, 0:PW].rearrange("p (r g i h) -> p r g i h", r=2, g=GP, i=CH)
    q_sb = wo_flat[:, PW:2 * PW].rearrange("p (r g t h) -> p r g t h", r=2, g=GP, t=CH)
    y_blk = wo_flat[0:YC, 0:PW].rearrange("c (t n) -> c t n", t=CH)
    rot = mid["ymix"][:, :, :].rearrange("p m t -> p (m t)")[:, 0:2 * ZN].rearrange("p (r g c) -> p r g c", r=2, g=GP)

    hT = buf("hT", [P, KD, TOK])
    hflat = hT[:, :, :].rearrange("p k t -> p (k t)")
    wb = hflat[:, 0:2 * GP * P].rearrange("p (r g n) -> p r g n", r=2, g=GP)
    YN = MT * CH * YC
    gel = hflat[:, 0:YN]
    u_ch = buf("u_ch", [P, MT, CH, YC])
    u_flat = u_ch[:, :, :, :].rearrange("p m t c -> p (m t c)")
    zg = buf("zg", [P, MT, TOK + 2])
    u_blk = buf("u_blk", [P, GROUPS, UC])
    ublk_flat = u_blk[:, :, :].rearrange("p g c -> p (g c)")
    xs0 = buf("xs0", [P, ZN])
    xs = [xs0[:, 0:D], ublk_flat[:, 0:D]]
    junk = ublk_flat[:, D:2 * D]
    rho_t = xs0[:, :]
    prow = buf("prow", [36, P])
    arow = buf("arow", [GP, 4, P])
    dtrow = buf("dtrow", [GP, 2])
    par = buf("par", [P, 4, GP])
    bt = buf("bt", [P, 2, GP, GCH])
    bbar = buf("bbar", [P, 2, GP, GCH])
    ctl = buf("ctl", [P, 2, 2, P])
    ct = buf("ct", [P, 2, GP, GCH])
    cz = buf("cz", [P, 2, GP, 2, GCH])
    apow = buf("apow", [P, 2, CH + 1, GP])
    sm = buf("sm", [P, 24, GP])
    tmp = buf("tmp", [P, 2 * TOK])
    tpool = buf("tpool", [P, 2, GP, GCH])
    ss = buf("ss", [P, 3 * NT])
    s0l = buf("s0l", [P, 2, P])
    stout = bt[:, :, :, :].rearrange("p r g h -> p (r g h)")[:, 0:2 * GP + 2 * P]
    sttr = ctl[:, :, :, :].rearrange("p a b c -> p (a b) c")[:, 0:3, :]
    cbl = ublk_flat[0:2 * NDEC, 2 * D:2 * D + W]
    cbt = buf("cbt", [P, MT, 2 * NDEC])
    crow = ct[:, :, :, :].rearrange("p r g h -> p (r g h)")[0:2 + NDEC, :]
    tkern = bbar[:, :, :, :].rearrange("p r g h -> p (r g h)")
    NM, CW, NOS, NOC, DS, BG = 0, 8, 20, 24, 28, 32
    ORDER = [0, 1, 2, 3, 4, 5, 6, 7, 12, 13, 14, 15, 8, 9, 10, 11]

    names = ("ident zeroed prow_in prow_psum pcol a_in dt_exp arow a_psum par exps b_in c_in c_psum ct "
             "s0_psum s0_done cb_in cb_psum cbt ss var root rstd xs xT_psum hT proj u_stored u_blk_in apow "
             "p_ready q_ready pt_psum wb k_psum k_sb toep_zero toep v_psum v ublk_zero "
             "state_in y_psum y_blk yt_psum y_ch st_ready st_psum sttr conv_z crow_psum crow "
             "gel_in gel_sig y_gelu glu_psum glu_sig out_done cz").split()
    s = {n: sem("m_" + n) for n in names}
    x_in = [sem(f"m_x_in{i}") for i in range(NT)]
    w_in_in = [sem(f"m_w_in{i}") for i in range(4)]
    wglu_in = sem("m_wglu")
    proj_free = [sem("m_proj_free0"), sem("m_proj_free1")]
    dve_step, pool_step = sem("m_dve_step"), sem("m_pool_step")
    keep["wout_in"] = sem("wout_in")

    def taken(eng, n):
        eng.wait_ge(proj_free[n % 2], n // 2 + 1)

    def gel_v(v):
        return v.rearrange("p (m t c) -> p m t c", m=MT, t=CH)

    block = stack.enter_context(nc.Block())

    @block.sync
    def _(sp):
        for i in range(NT):
            if i == 0:
                sp.dma_start(x[0:NMETA, 0, :], a["meta_tokens"]).then_inc(x_in[0], 16)
                sp.dma_start(x[NMETA:P, 0, :], a["x_prompt"][0, 0:P - NMETA, :]).then_inc(x_in[0], 16)
            elif i < NT - 1:
                sp.dma_start(x[:, i, :], a["x_prompt"][0, i * P - NMETA:(i + 1) * P - NMETA, :]).then_inc(x_in[i], 16)
            else:
                n = LAST - NDEC
                sp.dma_start(x[0:n, i, :], a["x_prompt"][0, SEQ - n:SEQ, :]).then_inc(x_in[i], 16)
                sp.dma_start(x[n:LAST, i, :], a["x_sample"][:, 0, :]).then_inc(x_in[i], 16)
        w_src = a["w_in"][0].rearrange("(k p) (b n) -> b p k n", p=P, b=4)
        for blk in (0, 1, 3, 2):
            sp.dma_start(w_in[:, blk], w_src[blk]).then_inc(w_in_in[blk], 16)
        for n in range(MT):
            taken(sp, n)
        sp.dma_start(scratch["u"].rearrange("(m p) t c -> p m (t c)", p=P),
                     u_ch[:, :, :, :].rearrange("p m t c -> p m (t c)")).then_inc(s["u_stored"], 16)
        sp.wait_ge(s["u_stored"], 16)
        sp.wait_ge(s["ublk_zero"], 1)
        u_src = scratch["u"].rearrange("(g h) t c -> t h g c", h=GCH)
        for t in range(CH):
            sp.dma_start(u_blk[t * GCH:(t + 1) * GCH, :, 0:YC], u_src[t]).then_inc(s["u_blk_in"], 16)
        sp.dma_start(u_blk[(CH - 1) * GCH:P, :, YC:UC], u_src[0, :, :, DEC0:YC]).then_inc(s["u_blk_in"], 16)
        sp.wait_ge(s["proj"], 16)
        sp.dma_start(w_glu, a["w_glu"][0].rearrange("(k p) n -> p k n", p=P)).then_inc(wglu_in, 16)
        sp.wait_ge(s["k_sb"], 1)
        sp.wait_ge(s["toep_zero"], 1)
        for t in range(CH):
            sp.dma_start(toep[0:(t + 1) * GCH, t, :], tkern[(CH - 1 - t) * GCH:P, :]).then_inc(s["toep"], 16)
        sp.wait_ge(s["y_ch"], 6)
        sp.dma_start(mid["w_out"][:], a["w_out"][0].rearrange("(k p) n -> p k n", p=P)).then_inc(keep["wout_in"], 16)
        sp.wait_ge(s["sttr"], 1)
        for r, (p_out, s_out) in enumerate((("re_p", "re_s"), ("im_p", "im_s"))):
            sp.dma_start(out[p_out][0, 0].rearrange("(g a) n -> g (a n)", a=2), sttr[r * GP:(r + 1) * GP, 0, :]).then_inc(s["out_done"], 16)
            sp.dma_start(out[s_out][0].rearrange("b (g a) n -> (b g) (a n)", a=2), sttr[:, 1 + r, :]).then_inc(s["out_done"], 16)
        sp.wait_ge(s["crow"], 1)
        sp.dma_start(out["conv_p"][0, 0], crow[0:2, :]).then_inc(s["out_done"], 16)
        sp.dma_start(out["conv_s"][0, :, 1, :], crow[2:2 + NDEC, :]).then_inc(s["out_done"], 16)
        sp.dma_start(out["conv_s"][0, :, 0, :], a["state_conv"][0, :, 1, :]).then_inc(s["out_done"], 16)
        sp.wait_ge(s["out_done"], 7 * 16)

    @block.scalar
    def _(act):
        act.dma_start(prow[NM:NM + 8, :], a["norm_mix"][0].rearrange("(k p) -> k p", p=P)).then_inc(s["prow_in"], 16)
        for k in range(3):
            act.dma_start(prow[CW + 4 * k:CW + 4 * k + 4, :], a["conv_w"][0, k].rearrange("(m p) -> m p", p=P)).then_inc(s["prow_in"], 16)
        for o, n in ((NOS, "norm_out_ssm"), (NOC, "norm_out_conv"), (DS, "ssm_d"), (BG, "b_glu")):
            act.dma_start(prow[o:o + 4, :], a[n][0].rearrange("(m p) -> m p", p=P)).then_inc(s["prow_in"], 16)
        act.dma_start(arow[:, 0, :], a["ssm_a_re"][0].rearrange("(g a) n -> g (a n)", a=2)).then_inc(s["a_in"], 16)
        act.dma_start(arow[:, 1, :], a["ssm_a_im"][0].rearrange("(g a) n -> g (a n)", a=2)).then_inc(s["a_in"], 16)
        act.dma_start(dtrow[:], a["ssm_log_dt"][0].rearrange("(g a) -> g a", a=2)).then_inc(s["a_in"], 16)
        act.wait_ge(s["a_in"], 48)
        nc.scalar.activation(dtrow[:], dtrow[:], ACT.Exp).then_inc(s["dt_exp"], 1)
        for i in range(NT):
            n = rows(i)
            act.wait_ge(x_in[i], 32 if i in (0, NT - 1) else 16)
            nc.scalar.activation(junk[0:n], x[0:n, i, :], ACT.Square, accum_out=ss[0:n, i:i + 1]).then_inc(s["ss"], 1)
            act.wait_ge(s["var"], i + 1)
            nc.scalar.activation(ss[0:n, NT + i:NT + i + 1], ss[0:n, i:i + 1], ACT.Sqrt).then_inc(s["root"], 1)
            act.wait_ge(s["rstd"], i + 1)
            if i >= 2:
                act.wait_ge(s["xT_psum"], i - 1)
            nc.scalar.activation(xs[i % 2][0:n], x[0:n, i, :], ACT.Copy, scale=ss[0:n, NT + i:NT + i + 1]).then_inc(s["xs"], 1)
        act.wait_ge(s["par"], 1)
        nc.scalar.activation(sm[:, 0, :], par[:, 2, :], ACT.Exp)
        nc.scalar.activation(sm[:, 1, :], par[:, 2, :], ACT.Exp, scale=float(CH)).then_inc(s["exps"], 1)
        act.wait_ge(s["zeroed"], 1)
        for n, m in enumerate(ORDER):
            if m >= 12:
                continue
            act.wait_ge(s["proj"], n + 1)
            b0, b1 = bank[2 * (n % 2)], bank[2 * (n % 2) + 1]
            if m < MT:
                c0 = HALF // CH
                nc.scalar.activation(u_ch[:, m, :, 0:c0], b0[:, 0:HALF].rearrange("p (c t) -> p t c", t=CH), ACT.Copy)
                nc.scalar.activation(u_ch[:, m, :, c0:NCH], b1[:, 0:NPROMPT - HALF].rearrange("p (c t) -> p t c", t=CH), ACT.Copy)
                nc.scalar.activation(u_ch[:, m, 0, DEC0:YC], b1[:, NPROMPT - HALF:REST], ACT.Copy).then_inc(proj_free[n % 2], 1)
            else:
                dst = zg[:, m - 4, 2:2 + TOK] if m < 8 else mid["cmix"][:, m - 8, :]
                nc.scalar.activation(dst[:, 0:HALF], b0[:, 0:HALF], ACT.Copy)
                nc.scalar.activation(dst[:, HALF:TOK], b1[:, 0:REST], ACT.Copy).then_inc(proj_free[n % 2], 1)
        act.wait_ge(s["k_psum"], 1)
        nc.scalar.activation(tkern, bank[6][:], ACT.Copy).then_inc(s["k_sb"], 1)
        for j in range(8):
            act.wait_ge(s["pt_psum"], j + 1)
            r, q = j // 4, j % 4
            nc.scalar.activation(wb[:, r, 4 * q:4 * q + 4, :], bank[4 + j % 2][:].rearrange("p (g n) -> p g n", g=4), ACT.Copy).then_inc(s["wb"], 1)
        for j in range(8):
            act.wait_ge(s["v_psum"], j + 1)
            nc.scalar.activation(v_sb[:, :, 2 * j:2 * j + 2, :],
                                 bank[4 + j % 2][:, 0:4 * UC].rearrange("p (g r c) -> p r g c", g=2, r=2), ACT.Copy).then_inc(s["v"], 1)
        for j in range(8):
            g0 = j % 2 + 8 * (j // 2)
            act.wait_ge(s["y_psum"], j + 1)
            nc.scalar.activation(y_blk[:, :, :].rearrange("c t (g h) -> c g t h", h=GCH)[:, g0:g0 + 7:2],
                                 bank[4 + j % 2][0:YC, :].rearrange("c (g t h) -> c g t h", g=4, t=CH), ACT.Copy).then_inc(s["y_blk"], 1)
        for j in range(6):
            n = min(6, MT * CH - 6 * j)
            act.wait_ge(s["yt_psum"], j + 1)
            nc.scalar.activation(y_ch[:, 6 * j * YC:(6 * j + n) * YC], bank[4 + j % 2][:, 0:n * YC], ACT.Copy).then_inc(s["y_ch"], 1)
        act.wait_ge(s["gel_in"], 1)
        nc.scalar.activation(gel, gel, ACT.Sigmoid, scale=2 * math.sqrt(2 / math.pi)).then_inc(s["gel_sig"], 1)
        for m in range(MT):
            act.wait_ge(s["glu_psum"], m + 1)
            for h in range(2):
                nc.scalar.activation(gel_v(gel)[:, m, 4 * h:4 * h + 4, :],
                                     bank[2 * (m % 2) + h][:, 0:4 * YC].rearrange("p (t c) -> p t c", t=4), ACT.Sigmoid,
                                     bias=pcol[:, BG + m:BG + m + 1]).then_inc(s["glu_sig"], 1)

    @block.gpsimd
    def _(pool):
        nc.gpsimd.memset(ident[:], 0.0).then_inc(pool_step, 1)
        pool.wait_ge(pool_step, 1)
        nc.gpsimd.affine_select(out=ident[:], in_=ident[:], compare_op=ALU.not_equal, fill=1.0, base=0,
                                pattern=[[-1, P]], channel_multiplier=1).then_inc(s["ident"], 1)
        for r, n in enumerate(("ssm_b_re", "ssm_b_im")):
            for g2 in range(2):
                pool.dma_start(bt[g2 * NS:(g2 + 1) * NS, r], a[n][0].rearrange("(g a) n h -> a n g h", a=2)[g2]).then_inc(s["b_in"], 16)
        for r, n in enumerate(("ssm_c_re", "ssm_c_im")):
            for half in range(2):
                for g in range(8):
                    pool.dma_start(ctl[g * GCH:(g + 1) * GCH, r, half, :].rearrange("h (a n) -> h a n", a=2),
                                   a[n][0].rearrange("(g a) h n -> g h a n", a=2)[half * 8 + g]).then_inc(s["c_in"], 16)
        for r, n in enumerate(("state_ssm_re", "state_ssm_im")):
            pool.dma_start(s0l[:, r, :], a[n][0].rearrange("b (g a) n -> (b g) (a n)", a=2)).then_inc(s["cb_in"], 16)
        pool.dma_start(cbl, a["state_conv"][0].rearrange("b k c -> (b k) c")).then_inc(s["cb_in"], 16)
        nc.gpsimd.memset(u_flat, 0.0)
        nc.gpsimd.memset(zg[:, :, 0:2], 0.0).then_inc(s["zeroed"], 1)
        nc.gpsimd.memset(cz[:], 0.0).then_inc(s["cz"], 1)
        pool.wait_ge(s["xT_psum"], NT)
        pool.wait_ge(s["cb_psum"], 1)
        nc.gpsimd.memset(u_blk[:, :, YC:UC], 0.0).then_inc(s["ublk_zero"], 1)
        pool.wait_ge(s["apow"], 1)
        pool.wait_ge(s["ct"], 1)
        steps = pool_step
        n = 1
        for t in range(CH):
            ar = apow[:, 0, t + 1, :].unsqueeze(2).to_broadcast([P, GP, GCH])
            ai = apow[:, 1, t + 1, :].unsqueeze(2).to_broadcast([P, GP, GCH])
            nc.gpsimd.tensor_tensor(q_sb[:, 0, :, t, :], ct[:, 0], ar, ALU.mult)
            nc.gpsimd.tensor_tensor(tpool[:, 0], ct[:, 1], ai, ALU.mult)
            nc.gpsimd.tensor_tensor(q_sb[:, 1, :, t, :], ct[:, 0], ai, ALU.mult)
            nc.gpsimd.tensor_tensor(tpool[:, 1], ct[:, 1], ar, ALU.mult).then_inc(steps, 1)
            n += 1
            pool.wait_ge(steps, n)
            nc.gpsimd.tensor_tensor(q_sb[:, 0, :, t, :], q_sb[:, 0, :, t, :], tpool[:, 0], ALU.subtract)
            nc.gpsimd.tensor_tensor(tpool[:, 1], q_sb[:, 1, :, t, :], tpool[:, 1], ALU.add).then_inc(steps, 1)
            n += 1
            pool.wait_ge(steps, n)
            nc.gpsimd.tensor_scalar(q_sb[:, 1, :, t, :], tpool[:, 1], -1.0, None, ALU.mult).then_inc(steps, 1)
            n += 1
            pool.wait_ge(steps, n)
        nc.gpsimd.memset(tpool[:, 0, 0, 0:1], 0.0).then_inc(s["q_ready"], 1)
        pool.wait_ge(s["proj"], 16)
        nc.gpsimd.memset(toep, 0.0).then_inc(s["toep_zero"], 1)

    @block.tensor
    def _(pe):
        pe.wait_ge(s["ident"], 1)
        pe.wait_ge(s["prow_in"], 16 * 8)
        nc.tensor.transpose(bank[0][:, 0:36], prow[:], ident[0:36, 0:36]).then_inc(s["prow_psum"], 1)

        def x_transposes(i):
            n = rows(i)
            pe.wait_ge(s["xs"], i + 1)
            if i >= 2:
                pe.wait_ge(s["hT"], 2 * (i - 1))
            for k in range(KD):
                last = nc.tensor.transpose(bank[4 + 2 * (i % 2) + k // 4][:, (k % 4) * P:(k % 4) * P + n],
                                           xs[i % 2][0:n, k * P:(k + 1) * P], ident[0:n, 0:n])
            last.then_inc(s["xT_psum"], 1)

        for i in range(NT):
            x_transposes(i)
        pe.wait_ge(s["arow"], 1)
        for j in range(4):
            last = nc.tensor.transpose(bank[1][:, j * GP:(j + 1) * GP], arow[:, j, :], ident[0:GP, 0:GP])
        last.then_inc(s["a_psum"], 1)
        pe.wait_ge(s["hT"], 2 * NT)
        pe.wait_ge(s["pcol"], 1)
        pe.wait_ge(s["par"], 1)
        for n, m in enumerate(ORDER):
            pe.wait_ge(w_in_in[m // 4], 16)
            if n >= 2:
                taken(pe, n - 2)
            for k in range(KD):
                wk = w_in[:, m // 4, k, (m % 4) * P:(m % 4 + 1) * P]
                nc.tensor.matmul(bank[2 * (n % 2)][:, 0:HALF], wk, hT[:, k, 0:HALF], start=(k == 0), stop=(k == KD - 1))
                last = nc.tensor.matmul(bank[2 * (n % 2) + 1][:, 0:REST], wk, hT[:, k, HALF:TOK], start=(k == 0), stop=(k == KD - 1))
            last.then_inc(s["proj"], 1)
            if n == 3:
                pe.wait_ge(s["c_in"], 16 * 32)
                for r in range(2):
                    for half in range(2):
                        last = nc.tensor.transpose(bank[7][:, (2 * r + half) * P:(2 * r + half + 1) * P], ctl[:, r, half, :], ident[:])
                last.then_inc(s["c_psum"], 1)
                pe.wait_ge(s["cb_in"], 48)
                for r in range(2):
                    last = nc.tensor.transpose(bank[6][:, r * P:(r + 1) * P], s0l[:, r, :], ident[:])
                last.then_inc(s["s0_psum"], 1)
                for m4 in range(MT):
                    last = nc.tensor.transpose(bank[5][:, m4 * 16:(m4 + 1) * 16], cbl[:, m4 * P:(m4 + 1) * P], ident[0:16, 0:16])
                last.then_inc(s["cb_psum"], 1)
        pe.wait_ge(s["p_ready"], 1)
        pe.wait_ge(s["cz"], 2)
        pe.wait_ge(s["s0_done"], 1)
        for g in range(GP):
            for r in range(2):
                last = nc.tensor.matmul(bank[6][:, g * 32:(g + 1) * 32], p_sb[:, r, g].rearrange("p i h -> p (i h)"),
                                        cz[:, r, g].rearrange("p a h -> p (a h)"), start=(r == 0), stop=(r == 1))
        last.then_inc(s["k_psum"], 1)
        for j in range(8):
            r, q = j // 4, j % 4
            if j >= 2:
                pe.wait_ge(s["wb"], j - 1)
            else:
                pe.wait_ge(s["cbt"], 1)
            for g in range(4):
                last = nc.tensor.transpose(bank[4 + j % 2][:, g * P:(g + 1) * P],
                                           p_sb[:, r, 4 * q + g].rearrange("p i h -> p (i h)"), ident[:])
            last.then_inc(s["pt_psum"], 1)
        pe.wait_ge(s["u_blk_in"], 16 * (CH + 1))
        pe.wait_ge(s["wb"], 8)
        for j in range(8):
            if j >= 2:
                pe.wait_ge(s["v"], j - 1)
            for gg in range(2):
                for r in range(2):
                    for g2 in range(2):
                        gp = 2 * j + gg
                        last = nc.tensor.matmul(bank[4 + j % 2][g2 * NS:(g2 + 1) * NS, (2 * gg + r) * UC:(2 * gg + r + 1) * UC],
                                                wb[:, r, gp, g2 * NS:(g2 + 1) * NS], u_blk[:, 2 * gp + g2, :], start=True, stop=True)
            last.then_inc(s["v_psum"], 1)
        pe.wait_ge(s["conv_z"], MT)
        for m in range(MT):
            last = nc.tensor.transpose(bank[7][0:2 + NDEC, m * P:(m + 1) * P], zg[:, m, NPROMPT:NPROMPT + 2 + NDEC], ident[:])
        last.then_inc(s["crow_psum"], 1)
        pe.wait_ge(s["toep"], 16 * CH)
        pe.wait_ge(s["state_in"], 1)
        pe.wait_ge(s["q_ready"], 1)
        pe.wait_ge(s["v"], 8)
        for j in range(8):
            odd = j % 2
            if j >= 2:
                pe.wait_ge(s["y_blk"], j - 1)
            for i in range(4):
                g = odd + 8 * (j // 2) + 2 * i
                o = bank[4 + odd][0:YC, i * P:(i + 1) * P]
                nc.tensor.matmul(o, u_blk[:, g, 0:YC], toep[:, :, g * GCH:(g + 1) * GCH], start=True, stop=False)
                for r in range(2):
                    last = nc.tensor.matmul(o, s_sb[odd * NS:(odd + 1) * NS, r, g // 2, :],
                                            q_sb[odd * NS:(odd + 1) * NS, r, g // 2].rearrange("p t h -> p (t h)"), start=False, stop=(r == 1))
            last.then_inc(s["y_psum"], 1)
        for j in range(6):
            if j < 2:
                pe.wait_ge(s["y_blk"], 8)
            else:
                pe.wait_ge(s["y_ch"], j - 1)
            for i in range(6 * j, min(6 * j + 6, MT * CH)):
                m, t = i // CH, i % CH
                last = nc.tensor.transpose(bank[4 + j % 2][:, (i - 6 * j) * YC:(i - 6 * j + 1) * YC], y_blk[:, t, m * P:(m + 1) * P], ident[0:YC, 0:YC])
            last.then_inc(s["yt_psum"], 1)
        pe.wait_ge(s["st_ready"], 1)
        nc.tensor.transpose(bank[6][0:2 * GP, 0:P], stout[:, 0:2 * GP], ident[:])
        for r in range(2):
            last = nc.tensor.transpose(bank[6][:, (1 + r) * P:(2 + r) * P], stout[:, 2 * GP + r * P:2 * GP + (r + 1) * P], ident[:])
        last.then_inc(s["st_psum"], 1)
        pe.wait_ge(s["y_gelu"], 1)
        pe.wait_ge(wglu_in, 16)
        yv = gel_v(y_ch)
        for m in range(MT):
            if m >= 2:
                pe.wait_ge(s["glu_sig"], 2 * (m - 1))
            for k in range(MT):
                for h in range(2):
                    last = nc.tensor.matmul(bank[2 * (m % 2) + h][:, 0:4 * YC], w_glu[:, k, m * P:(m + 1) * P],
                                            yv[:, k, 4 * h:4 * h + 4, :].rearrange("p t c -> p (t c)"),
                                            start=(k == 0), stop=(k == MT - 1))
            last.then_inc(s["glu_psum"], 1)

    @block.vector
    def _(dve):
        count = [0]

        def done(ins):
            count[0] += 1
            ins.then_inc(dve_step, 1)
            dve.wait_ge(dve_step, count[0])

        def tt(o, x0, x1, op):
            return nc.vector.tensor_tensor(o, x0, x1, op)

        def ts(o, x0, s1, op0, s2=None, op1=None):
            if op1 is None:
                return nc.vector.tensor_scalar(o, x0, s1, None, op0)
            return nc.vector.tensor_scalar(o, x0, s1, s2, op0, op1)

        def stt(o, x0, sc, x1, op0, op1):
            return nc.vector.scalar_tensor_tensor(out=o, in0=x0, scalar=sc, in1=x1, op0=op0, op1=op1)

        def cmul(o_re, o_im, a_re, a_im, b_re, b_im, t0, t1):
            tt(o_re, a_re, b_re, ALU.mult)
            tt(t0, a_im, b_im, ALU.mult)
            tt(o_im, a_re, b_im, ALU.mult)
            done(tt(t1, a_im, b_re, ALU.mult))
            tt(o_re, o_re, t0, ALU.subtract)
            done(tt(o_im, o_im, t1, ALU.add))

        dve.wait_ge(s["prow_psum"], 1)
        nc.vector.tensor_copy(pcol[:], bank[0][:, 0:36]).then_inc(s["pcol"], 1)
        dve.wait_ge(s["pcol"], 1)
        dve.wait_ge(s["dt_exp"], 1)
        for j in range(2):
            last = tt(arow[:, 2 + j, :].rearrange("g (a n) -> g a n", a=2), arow[:, j, :].rearrange("g (a n) -> g a n", a=2),
                      dtrow[:].unsqueeze(2).to_broadcast([GP, 2, NS]), ALU.mult)
        last.then_inc(s["arow"], 1)

        def take_hT(i):
            n = rows(i)
            dve.wait_ge(s["xT_psum"], i + 1)
            for q in range(2):
                tt(hT[:, 4 * q:4 * q + 4, i * P:i * P + n],
                   bank[4 + 2 * (i % 2) + q][:].rearrange("p (k t) -> p k t", k=4)[:, :, 0:n],
                   pcol[:, NM + 4 * q:NM + 4 * q + 4].unsqueeze(2).to_broadcast([P, 4, n]), ALU.mult).then_inc(s["hT"], 1)

        for i in range(NT):
            n = rows(i)
            dve.wait_ge(s["ss"], i + 1)
            ts(ss[0:n, i:i + 1], ss[0:n, i:i + 1], 1.0 / D, ALU.mult, EPS, ALU.add).then_inc(s["var"], 1)
            dve.wait_ge(s["root"], i + 1)
            refine_rsqrt(nc, done, ss[0:n, NT + i:NT + i + 1], ss[0:n, 2 * NT + i:2 * NT + i + 1], ss[0:n, i:i + 1]).then_inc(s["rstd"], 1)
            if i >= 1:
                take_hT(i - 1)
        take_hT(NT - 1)

        dve.wait_ge(s["a_psum"], 1)
        nc.vector.tensor_copy(par[:].rearrange("p a g -> p (a g)"), bank[1][:, 0:4 * GP]).then_inc(s["par"], 1)
        dve.wait_ge(s["par"], 1)
        mag, rho, kk, r, hh, h2, sn, vs, t0, t1, cs, er, ei, er2, ei2, nr, den, cr, ci = (sm[:, i, :] for i in range(19))
        are, aim, dre, dim = (par[:, i, :] for i in range(4))
        BIG = 12582912.0
        c1 = 6.28125
        c2 = float(math.floor((2 * math.pi - c1) * 2 ** 20) / 2 ** 20)
        c3 = 2 * math.pi - c1 - c2
        done(ts(kk, dim, 1 / (2 * math.pi), ALU.mult))
        done(ts(kk, kk, BIG, ALU.add))
        done(ts(kk, kk, BIG, ALU.subtract))
        done(stt(r, kk, -c1, dim, ALU.mult, ALU.add))
        done(stt(r, kk, -c2, r, ALU.mult, ALU.add))
        done(stt(r, kk, -c3, r, ALU.mult, ALU.add))
        done(ts(hh, r, 0.125, ALU.mult))
        done(tt(h2, hh, hh, ALU.mult))
        done(ts(t0, h2, -1 / 72, ALU.mult, 1.0, ALU.add))
        done(tt(t0, t0, h2, ALU.mult))
        done(ts(t0, t0, -1 / 42, ALU.mult, 1.0, ALU.add))
        done(tt(t0, t0, h2, ALU.mult))
        done(ts(t0, t0, -1 / 20, ALU.mult, 1.0, ALU.add))
        done(tt(t0, t0, h2, ALU.mult))
        done(ts(t0, t0, -1 / 6, ALU.mult, 1.0, ALU.add))
        tt(sn, t0, hh, ALU.mult)
        done(ts(t1, h2, -1 / 56, ALU.mult, 1.0, ALU.add))
        done(tt(t1, t1, h2, ALU.mult))
        done(ts(t1, t1, -1 / 30, ALU.mult, 1.0, ALU.add))
        done(tt(t1, t1, h2, ALU.mult))
        done(ts(t1, t1, -1 / 12, ALU.mult, 1.0, ALU.add))
        done(tt(t1, t1, h2, ALU.mult))
        done(ts(vs, t1, 0.5, ALU.mult))
        for _ in range(3):
            tt(t0, sn, vs, ALU.mult)
            done(tt(t1, sn, sn, ALU.mult))
            done(tt(t0, sn, t0, ALU.subtract))
            ts(vs, t1, 2.0, ALU.mult)
            done(ts(sn, t0, 2.0, ALU.mult))
        done(ts(cs, vs, -1.0, ALU.mult, 1.0, ALU.add))
        dve.wait_ge(s["exps"], 1)
        nc.vector.memset(apow[:, 0, 0, :], 1.0)
        nc.vector.memset(apow[:, 1, 0, :], 0.0)
        tt(apow[:, 0, 1, :], mag, cs, ALU.mult)
        done(tt(apow[:, 1, 1, :], mag, sn, ALU.mult))
        for h in (1, 2, 4):
            hi = [apow[:, c, h, :].unsqueeze(1).to_broadcast([P, h, GP]) for c in range(2)]
            tv = [tmp[:, c * 64:c * 64 + h * GP].rearrange("p (k g) -> p k g", k=h) for c in range(2)]
            cmul(apow[:, 0, h + 1:2 * h + 1, :], apow[:, 1, h + 1:2 * h + 1, :],
                 apow[:, 0, 1:h + 1, :], apow[:, 1, 1:h + 1, :], hi[0], hi[1], tv[0], tv[1])
        nc.vector.tensor_copy(cr, cs).then_inc(s["apow"], 1)
        cmul(er, ei, cs, sn, cs, sn, t0, t1)
        cmul(er2, ei2, er, ei, er, ei, t0, t1)
        cmul(rot[:, 0, :, 0], rot[:, 1, :, 0], er2, ei2, er2, ei2, t0, t1)
        have = 1
        while have < NCH:
            n = min(have, NCH - have)
            hi = [rot[:, c, :, have - 1:have].to_broadcast([P, GP, n]) for c in range(2)]
            tv = [tmp[:, c * GP * 32:c * GP * 32 + GP * n].rearrange("p (g c) -> p g c", g=GP) for c in range(2)]
            cmul(rot[:, 0, :, have:have + n], rot[:, 1, :, have:have + n],
                 rot[:, 0, :, 0:n], rot[:, 1, :, 0:n], hi[0], hi[1], tv[0], tv[1])
            have += n
        ts(nr, apow[:, 0, 1, :], -1.0, ALU.add)
        tt(t0, are, are, ALU.mult)
        done(tt(t1, aim, aim, ALU.mult))
        done(tt(den, t0, t1, ALU.add))
        done(nc.vector.reciprocal(den, den))
        ni = apow[:, 1, 1, :]
        tt(cr, nr, are, ALU.mult)
        tt(t0, ni, aim, ALU.mult)
        tt(ci, ni, are, ALU.mult)
        done(tt(t1, nr, aim, ALU.mult))
        tt(cr, cr, t0, ALU.add)
        done(tt(ci, ci, t1, ALU.subtract))
        tt(cr, cr, den, ALU.mult)
        done(tt(ci, ci, den, ALU.mult))
        tv = [tmp[:, c * GP * GCH:(c + 1) * GP * GCH].rearrange("p (g h) -> p g h", g=GP) for c in range(2)]
        dve.wait_ge(s["b_in"], 64)
        cmul(bbar[:, 0], bbar[:, 1], cr.unsqueeze(2).to_broadcast([P, GP, GCH]), ci.unsqueeze(2).to_broadcast([P, GP, GCH]),
             bt[:, 0], bt[:, 1], tv[0], tv[1])
        dve.wait_ge(s["c_psum"], 1)
        nc.vector.tensor_copy(ct[:].rearrange("p r g h -> p (r g h)"), bank[7][:]).then_inc(s["ct"], 1)
        dve.wait_ge(s["ct"], 1)
        dve.wait_ge(s["cz"], 1)
        for g2 in range(2):
            q = slice(g2 * NS, (g2 + 1) * NS)
            nc.vector.tensor_copy(cz[q, 0, :, g2, :], ct[q, 0])
            last = ts(cz[q, 1, :, g2, :], ct[q, 1], -1.0, ALU.mult)
        last.then_inc(s["cz"], 1)
        dve.wait_ge(s["cb_psum"], 1)
        nc.vector.tensor_copy(cbt[:].rearrange("p m b -> p (m b)"), bank[5][:, 0:MT * 16]).then_inc(s["cbt"], 1)
        for i in range(CH):
            ar = apow[:, 0, CH - 1 - i, :].unsqueeze(2).to_broadcast([P, GP, GCH])
            ai = apow[:, 1, CH - 1 - i, :].unsqueeze(2).to_broadcast([P, GP, GCH])
            cmul(p_sb[:, 0, :, i, :], p_sb[:, 1, :, i, :], bbar[:, 0], bbar[:, 1], ar, ai, tv[0], tv[1])
        nc.vector.memset(t0, 0.0).then_inc(s["p_ready"], 1)

        for m in range(MT):
            n = 8 + m
            taken(dve, 4 + m)
            dve.wait_ge(s["proj"], n + 1)
            tt(zg[:, m, 2:2 + HALF], zg[:, m, 2:2 + HALF], bank[2 * (n % 2)][:, 0:HALF], ALU.mult)
            tt(zg[:, m, 2 + HALF:2 + TOK], zg[:, m, 2 + HALF:2 + TOK], bank[2 * (n % 2) + 1][:, 0:REST], ALU.mult).then_inc(proj_free[n % 2], 1)
        dve.wait_ge(s["cbt"], 1)
        for m in range(MT):
            taken(dve, 8 + m)
            nc.vector.memset(sm[:, 20, 0:1], 0.0).then_inc(s["conv_z"], 1)
            w = [pcol[:, CW + 4 * k + m:CW + 4 * k + m + 1] for k in range(3)]
            acc, accd = tmp[:, 0:NPROMPT], tmp[:, NPROMPT:TOK]
            old = cbt[:, m, :].rearrange("p (b k) -> p k b", k=2)
            ts(acc, zg[:, m, 0:NPROMPT], w[0], ALU.mult)
            done(ts(accd, old[:, 0], w[0], ALU.mult))
            stt(acc, zg[:, m, 1:1 + NPROMPT], w[1], acc, ALU.mult, ALU.add)
            done(stt(accd, old[:, 1], w[1], accd, ALU.mult, ALU.add))
            done(stt(tmp[:, 0:TOK], zg[:, m, 2:2 + TOK], w[2], tmp[:, 0:TOK], ALU.mult, ALU.add))
            taken(dve, 12 + m)
            done(tt(mid["cmix"][:, m, :], mid["cmix"][:, m, :], tmp[:, 0:TOK], ALU.mult))

        dve.wait_ge(s["proj"], 16)
        nc.vector.memset(s_sb[:, :, :, 0:1], 0.0)
        dve.wait_ge(s["s0_psum"], 1)
        for c in range(2):
            nc.vector.tensor_copy(s_sb[:, c, :, DEC0:YC], bank[6][:, c * P:(c + 1) * P].rearrange("p (b g) -> p g b", g=GP))
        nc.vector.memset(t0, 0.0).then_inc(s["s0_done"], 1)
        rho_v = rho_t.rearrange("p (g c) -> p g c", g=GP)
        nc.vector.tensor_copy(rho_v, rho.unsqueeze(2).to_broadcast([P, GP, NCH]))
        done(nc.vector.memset(t1, 0.0))
        done(nc.vector.memset(rho_v[:, :, 0:1], 0.0))
        dve.wait_ge(s["v"], 8)
        wv = [v.rearrange("p (g c) -> p g c", g=GP) for v in wz]
        vr, vi = v_sb[:, 0, :, 0:NCH], v_sb[:, 1, :, 0:NCH]
        tt(wv[0], rot[:, 0], vr, ALU.mult)
        tt(wv[2], rot[:, 1], vi, ALU.mult)
        tt(wv[1], rot[:, 0], vi, ALU.mult)
        done(tt(wv[3], rot[:, 1], vr, ALU.mult))
        tt(wv[0], wv[0], wv[2], ALU.add)
        done(tt(wv[1], wv[1], wv[3], ALU.subtract))
        nc.vector.tensor_tensor_scan(wz[2], rho_t, wz[0], 0.0, ALU.mult, ALU.add)
        done(nc.vector.tensor_tensor_scan(wz[3], rho_t, wz[1], 0.0, ALU.mult, ALU.add))
        sr, si = s_sb[:, 0, :, 1:1 + NCH], s_sb[:, 1, :, 1:1 + NCH]
        tt(sr, rot[:, 0], wv[2], ALU.mult)
        tt(wv[0], rot[:, 1], wv[3], ALU.mult)
        tt(si, rot[:, 0], wv[3], ALU.mult)
        done(tt(wv[1], rot[:, 1], wv[2], ALU.mult))
        tt(sr, sr, wv[0], ALU.subtract)
        tt(si, si, wv[1], ALU.add).then_inc(s["state_in"], 1)
        dve.wait_ge(s["state_in"], 1)
        nc.vector.tensor_copy(stout[:, 0:2 * GP].rearrange("p (r g) -> p r g", r=2), s_sb[:, :, :, NCH])
        so = [stout[:, 2 * GP + c * P:2 * GP + (c + 1) * P].rearrange("p (b g) -> p g b", g=GP) for c in range(2)]
        d0, d1 = s_sb[:, 0, :, DEC0:YC], s_sb[:, 1, :, DEC0:YC]
        ab = [apow[:, c, 1, :].unsqueeze(2).to_broadcast([P, GP, NDEC]) for c in range(2)]
        tv = [tmp[:, c * P:(c + 1) * P].rearrange("p (g b) -> p g b", g=GP) for c in range(4)]
        cmul(tv[2], tv[3], d0, d1, ab[0], ab[1], tv[0], tv[1])
        tt(so[0], tv[2], v_sb[:, 0, :, YC:UC], ALU.add)
        tt(so[1], tv[3], v_sb[:, 1, :, YC:UC], ALU.add).then_inc(s["st_ready"], 1)
        dve.wait_ge(s["crow_psum"], 1)
        dve.wait_ge(s["q_ready"], 1)
        nc.vector.tensor_copy(crow, bank[7][0:2 + NDEC, :]).then_inc(s["crow"], 1)
        dve.wait_ge(s["st_psum"], 1)
        nc.vector.tensor_copy(sttr[0:2 * GP, 0, :], bank[6][0:2 * GP, 0:P])
        nc.vector.tensor_copy(sttr[:, 1:3, :], bank[6][:, P:3 * P].rearrange("p (a c) -> p a c", a=2)).then_inc(s["sttr"], 1)

        dve.wait_ge(s["y_ch"], 6)
        yv, uv = gel_v(y_ch), u_ch
        for m in range(MT):
            last = stt(yv[:, m], uv[:, m], pcol[:, DS + m:DS + m + 1], yv[:, m], ALU.mult, ALU.add)
        done(last)
        done(tt(gel, y_ch, y_ch, ALU.mult))
        done(ts(gel, gel, 0.044715, ALU.mult, 1.0, ALU.add))
        tt(gel, gel, y_ch, ALU.mult).then_inc(s["gel_in"], 1)
        dve.wait_ge(s["gel_sig"], 1)
        tt(y_ch, y_ch, gel, ALU.mult).then_inc(s["y_gelu"], 1)
        dve.wait_ge(s["y_gelu"], 1)
        for m in range(MT):
            dve.wait_ge(s["glu_sig"], 2 * (m + 1))
            tt(mid["ymix"][:, m, 0:NPROMPT].rearrange("p (c t) -> p t c", t=CH), yv[:, m, :, 0:NCH], gel_v(gel)[:, m, :, 0:NCH], ALU.mult)
            tt(mid["ymix"][:, m, NPROMPT:TOK], yv[:, m, 0, DEC0:YC], gel_v(gel)[:, m, 0, DEC0:YC], ALU.mult)

def loop_tables(stack, sb):
    return {
        "rank": sb(stack, "rank", [P, NT, E + 1]),
        "slotval": sb(stack, "slotval", [P, NT, E + 1, 3]),
        "iota_s": sb(stack, "iota_s", [P, P]),
        "pick_row": sb(stack, "pick_row", [96, E, P], BF16),
        "bias": sb(stack, "bias", [96, 3 * FF], BF16),
        "over_i": sb(stack, "over_i", [P, 2, NOVER], I32),
        "over_base": sb(stack, "over_base", [P, NOVER]),
    }


def weight_load(eng, a, keep, mid, e, j):
    if j < 8:
        half, k = j // 4, 2 * (j % 4)
        src = a["w_gate_up"][0].rearrange("e (p k) (u f n) -> e f p (k u) n", p=P, u=2, f=2)[e, half, :, 2 * k:2 * k + 4]
        dst = keep["ring_lo"][:, 2 * j:2 * j + 2, :].rearrange("p k (u n) -> p (k u) n", u=2)
    else:
        k = 2 * (j - 8)
        src = a["w_down"][0].rearrange("e (k p) n -> e p k n", p=P)[e, :, k:k + 2]
        dst = mid["w_out"][:, k:k + 2, :]
    return eng.dma_start(dst, src)


def router(nc, a, scratch, stack, sb, sem, bank, keep, mid, tb):
    def buf(name, shape, dt=F32):
        return sb(stack, name, shape, dt)

    x, ident, pcol = keep["x"], keep["ident"], keep["pcol"]
    NOS, NOC = 20, 24
    ymix, cmix, w_out = mid["ymix"], mid["cmix"], mid["w_out"]
    sq = buf("sq", [P, 2, MT, TOK])
    gffn = buf("gffn", [P, D])
    hf = buf("hf", [P, 2, D])
    hfT = buf("hfT", [P, 2, KD, P])
    w_r = buf("w_r", [P, KD, E])
    b_r = buf("b_r", [1, E])
    ones = buf("ones", [P, P])
    ones_b = buf("ones_b", [P, P], BF16)
    tri = buf("tri", [P, P], BF16)
    trif = sq[:, 0, 0, 0:P]
    ssq = buf("ssq", [P, 3, 2 * NT])
    ss2 = buf("ss2", [P, 3, NT])
    jk = buf("jk", [P, D], BF16)
    lg = buf("lg", [P, NT, E])
    top = buf("top", [P, NT, 8])
    topi = buf("topi", [P, NT, 8], U32)
    topf = buf("topf", [P, NT, 8])
    iota_i = buf("iota_i", [P, P], I32)
    eqk = buf("eqk", [P, NT, E, TOPK])
    mask = buf("mask", [P, NT, E])
    mask_b = buf("mask_b", [P, NT, E], BF16)
    gate = buf("gate", [P, NT, E])
    gsum = buf("gsum", [P, NT])
    cum = buf("cum", [P, NT, E])
    tokv = buf("tokv", [P, NT])
    tok_i = buf("tok_i", [P, NT], I32)
    valid = buf("valid", [P, NT])
    cnt = buf("cnt", [P, 4, E])
    om = buf("om", [P, 2, NOVER, E])
    of = buf("of", [P, 4, NOVER])
    NB = 4
    HB = 3 * FF // NB
    bf = buf("bf", [96, HB])

    s = {n: sem("r_" + n) for n in (
        "consts gffn_in wr_in br_in bias_in sq sums rows scaled mix_var mix_root mm x_new xsq x_var x_root hf hfT_psum hfT logits "
        "sub exp mask rank_psum step pool_step done tabs".split())}
    hf_stored = [sem("r_hf_stored0"), sem("r_hf_stored1")]
    mm_free = [sem("r_mm_free0"), sem("r_mm_free1")]
    keep["landed"] = [sem(f"landed{j}") for j in range(PAIRS)]
    block = stack.enter_context(nc.Block())

    @block.sync
    def _(sp):
        sp.dma_start(w_r[:], a["w_router"][0].rearrange("(p k) e -> p k e", p=P)).then_inc(s["wr_in"], 16)
        sp.dma_start(b_r[:], a["b_router"]).then_inc(s["br_in"], 16)
        sp.dma_start(gffn[:], a["norm_ffn"].to_broadcast([P, D])).then_inc(s["gffn_in"], 16)
        for j in range(8):
            weight_load(sp, a, keep, mid, 0, j).then_inc(keep["landed"][j], 16)
        for i in range(NT):
            sp.wait_ge(s["hf"], i + 1)
            sp.dma_start(scratch["hf"][i * P:i * P + rows(i), :], hf[0:rows(i), i % 2, :]).then_inc(hf_stored[i % 2], 16)
        for c in range(2):
            sp.wait_ge(hf_stored[c], 16 * len(range(c, NT, 2)))

    @block.gpsimd
    def _(pool):
        g = nc.gpsimd
        steps = [0]

        def done(ins):
            steps[0] += 1
            ins.then_inc(s["pool_step"], 1)
            pool.wait_ge(s["pool_step"], steps[0])

        g.iota(iota_i[:], pattern=[[1, P]], base=0, channel_multiplier=0)
        g.iota(tok_i[:], pattern=[[P, NT]], base=0, channel_multiplier=1).then_inc(s["tabs"], 1)
        loads = 0
        bsrc = (a["b_gate_up"][0], a["b_down"][0])
        for h in range(NB):
            lo, hi, split = h * HB, (h + 1) * HB, 2 * FF
            pieces = [(bsrc[0][:, lo:min(hi, split)], 0)] if lo < split else []
            if hi > split:
                pieces.append((bsrc[1][:, max(lo - split, 0):hi - split], max(split - lo, 0)))
            for src, c in pieces:
                for q in range(3):
                    pool.dma_start(bf[q * 32:(q + 1) * 32, c:c + src.shape[1]], src).then_inc(s["bias_in"], 16)
                    loads += 1
            pool.wait_ge(s["bias_in"], 16 * loads)
            out_b = tb["bias"][:, h * HB:(h + 1) * HB]
            done(g.tensor_copy(out_b, bf[:]))
            done(g.tensor_tensor(bf[32:64, :], bf[32:64, :], out_b[32:64, :], ALU.subtract))
            done(g.tensor_tensor(bf[64:96, :], bf[64:96, :], out_b[64:96, :], ALU.subtract))
            done(g.tensor_copy(out_b[32:64, :], bf[32:64, :]))
            done(g.tensor_copy(out_b[64:96, :], bf[64:96, :]))
            done(g.tensor_tensor(bf[64:96, :], bf[64:96, :], out_b[64:96, :], ALU.subtract))
            done(g.tensor_copy(out_b[64:96, :], bf[64:96, :]))

        done(g.memset(tb["pick_row"][:], 0.0))
        for q in range(3):
            v = tb["pick_row"][q * 32:(q + 1) * 32]
            done(g.affine_select(out=v, in_=v, compare_op=ALU.not_equal, fill=1.0, base=0,
                                 pattern=[[-1, E], [0, P]], channel_multiplier=1))

    @block.scalar
    def _(act):
        nc.scalar.activation(sq[:, 0], ymix[:], ACT.Square).then_inc(s["sq"], 1)
        nc.scalar.activation(sq[:, 1], cmix[:], ACT.Square).then_inc(s["sq"], 1)
        act.wait_ge(s["mix_var"], 1)
        nc.scalar.activation(ssq[:, 0], ssq[:, 2], ACT.Sqrt).then_inc(s["mix_root"], 1)
        for i in range(NT):
            n = rows(i)
            act.wait_ge(s["x_new"], 2 * (i + 1))
            nc.scalar.activation(jk[0:n], x[0:n, i, :], ACT.Square, accum_out=ss2[0:n, 2, i:i + 1]).then_inc(s["xsq"], 1)
            act.wait_ge(s["x_var"], i + 1)
            nc.scalar.activation(ss2[0:n, 0, i:i + 1], ss2[0:n, 2, i:i + 1], ACT.Sqrt).then_inc(s["x_root"], 1)
            act.wait_ge(s["hfT_psum"], i + 1)
            for q in range(2):
                last = nc.scalar.activation(hfT[:, i % 2, 4 * q:4 * q + 4, 0:n],
                                            bank[4 + q][:].rearrange("p (k t) -> p k t", k=4)[:, :, 0:n], ACT.Copy)
            last.then_inc(s["hfT"], 1)
        act.wait_ge(s["sub"], 1)
        nc.scalar.activation(gate[:], gate[:], ACT.Exp).then_inc(s["exp"], 1)

    @block.tensor
    def _(pe):
        pe.wait_ge(s["sq"], 2)
        pe.wait_ge(s["consts"], 1)
        for i in range(NT):
            for c in range(2):
                for m in range(MT):
                    last = nc.tensor.matmul(bank[7][0:rows(i), 2 * i + c:2 * i + c + 1], sq[:, c, m, i * P:i * P + rows(i)],
                                            ones[:, 0:1], start=(m == 0), stop=(m == MT - 1))
        last.then_inc(s["sums"], 1)
        pe.wait_ge(s["scaled"], 1)
        pe.wait_ge(keep["wout_in"], 16)

        def route(i):
            n = rows(i)
            pe.wait_ge(s["hf"], i + 1)
            if i >= 1:
                pe.wait_ge(s["hfT"], i)
            for k in range(KD):
                last = nc.tensor.transpose(bank[4 + k // 4][:, (k % 4) * P:(k % 4) * P + n],
                                           hf[0:n, i % 2, k * P:(k + 1) * P], ident[0:n, 0:n])
            last.then_inc(s["hfT_psum"], 1)
            pe.wait_ge(s["hfT"], i + 1)
            o = bank[6][0:n, i * E:(i + 1) * E]
            for k in range(KD):
                nc.tensor.matmul(o, hfT[:, i % 2, k, 0:n], w_r[:, k, :], start=(k == 0), stop=False)
            nc.tensor.matmul(o, ones[0:1, 0:n], b_r[:], start=False, stop=True).then_inc(s["logits"], 1)

        pe.wait_ge(s["wr_in"], 16)
        pe.wait_ge(s["br_in"], 16)
        for i in range(NT):
            n = rows(i)
            for h in range(2):
                if i >= 1:
                    pe.wait_ge(mm_free[h], i)
                for c, src in enumerate((ymix, cmix)):
                    for m in range(MT):
                        last = nc.tensor.matmul(bank[2 * h + c][0:n, :], src[:, m, i * P:i * P + n],
                                                w_out[:, MT * c + m, h * 512:(h + 1) * 512], start=(m == 0), stop=(m == MT - 1))
                last.then_inc(s["mm"], 1)
            if i >= 1:
                route(i - 1)
        route(NT - 1)
        pe.wait_ge(s["mask"], 1)
        pe.wait_ge(s["rows"], 1)
        for i in range(NT):
            for j in range(i):
                nc.tensor.matmul(bank[7][:, i * E:(i + 1) * E], ones_b[:], mask_b[:, j, :], start=(j == 0), stop=False)
            nc.tensor.matmul(bank[7][:, i * E:(i + 1) * E], tri[:], mask_b[:, i, :], start=(i == 0), stop=True)
        for j in range(NT):
            last = nc.tensor.matmul(bank[7][:, NT * E:(NT + 1) * E], ones_b[:], mask_b[:, j, :], start=(j == 0), stop=(j == NT - 1))
        last.then_inc(s["rank_psum"], 1)

    @block.vector
    def _(dve):
        v = nc.vector
        steps = [0]

        def done(ins):
            steps[0] += 1
            ins.then_inc(s["step"], 1)
            dve.wait_ge(s["step"], steps[0])

        v.memset(ones[:], 1.0)
        v.memset(ones_b[:], 1.0)
        v.memset(lg[:], 0.0).then_inc(s["consts"], 1)
        dve.wait_ge(s["sums"], 1)
        v.memset(ssq[:], 1.0)
        done(v.memset(ss2[:], 1.0))
        for i in range(NT):
            n = rows(i)
            last = v.tensor_scalar(ssq[0:n, 2, 2 * i:2 * i + 2], bank[7][0:n, 2 * i:2 * i + 2], 1.0 / W, EPS, ALU.mult, ALU.add)
        last.then_inc(s["mix_var"], 1)
        dve.wait_ge(s["mix_root"], 1)
        refine_rsqrt(nc, done, ssq[:, 0], ssq[:, 1], ssq[:, 2]).then_inc(s["rows"], 1)
        dve.wait_ge(s["rows"], 1)
        for m in range(MT):
            v.tensor_scalar(ymix[:, m, :], ymix[:, m, :], pcol[:, NOS + m:NOS + m + 1], None, ALU.mult)
            last = v.tensor_scalar(cmix[:, m, :], cmix[:, m, :], pcol[:, NOC + m:NOC + m + 1], None, ALU.mult)
        last.then_inc(s["scaled"], 1)
        dve.wait_ge(s["gffn_in"], 16)
        for i in range(NT):
            n = rows(i)
            for h in range(2):
                dve.wait_ge(s["mm"], 2 * i + h + 1)
                xv = x[0:n, i, h * 512:(h + 1) * 512]
                done(v.scalar_tensor_tensor(out=xv, in0=bank[2 * h][0:n, :], scalar=ssq[0:n, 0, 2 * i:2 * i + 1], in1=xv, op0=ALU.mult, op1=ALU.add))
                done(v.scalar_tensor_tensor(out=xv, in0=bank[2 * h + 1][0:n, :], scalar=ssq[0:n, 0, 2 * i + 1:2 * i + 2], in1=xv, op0=ALU.mult, op1=ALU.add))
                dve.sem_inc(mm_free[h], 1)
                dve.sem_inc(s["x_new"], 1)
            dve.wait_ge(s["xsq"], i + 1)
            v.tensor_scalar(ss2[0:n, 2, i:i + 1], ss2[0:n, 2, i:i + 1], 1.0 / D, EPS, ALU.mult, ALU.add).then_inc(s["x_var"], 1)
            dve.wait_ge(s["x_root"], i + 1)
            done(refine_rsqrt(nc, done, ss2[0:n, 0, i:i + 1], ss2[0:n, 1, i:i + 1], ss2[0:n, 2, i:i + 1]))
            if i >= 2:
                dve.wait_ge(s["hfT_psum"], i - 1)
                dve.wait_ge(hf_stored[i % 2], 16 * (i // 2))
            v.scalar_tensor_tensor(out=hf[0:n, i % 2, :].rearrange("t (k p) -> t p k", p=P), in0=x[0:n, i, :].rearrange("t (p k) -> t p k", p=P),
                                   scalar=ss2[0:n, 0, i:i + 1], in1=gffn[0:n, :].rearrange("t (p k) -> t p k", p=P),
                                   op0=ALU.mult, op1=ALU.mult).then_inc(s["hf"], 1)
        dve.wait_ge(s["tabs"], 1)
        v.tensor_copy(tb["iota_s"][:], iota_i[:])
        done(v.tensor_copy(tokv[:], tok_i[:]))
        v.tensor_scalar(valid[:], tokv[:], float(TOK), None, ALU.is_lt)
        v.tensor_scalar(tri[:], tb["iota_s"][:], tokv[:, 0:1], None, ALU.is_gt)
        dve.wait_ge(s["logits"], NT)
        for i in range(NT):
            done(v.tensor_copy(lg[0:rows(i), i, :], bank[6][0:rows(i), i * E:(i + 1) * E]))
            done(v.max(out=top[:, i, :], in_=lg[:, i, :]))
            done(v.max_index(out=topi[:, i, :], in_max=top[:, i, :], in_values=lg[:, i, :]))
        done(v.tensor_copy(topf[:], topi[:]))
        v.tensor_tensor(gate[:], lg[:], top[:, :, 0:1].to_broadcast([P, NT, E]), ALU.subtract).then_inc(s["sub"], 1)
        iota_e = tb["iota_s"][:, 0:E]
        for i in range(NT):
            last = v.tensor_tensor(eqk[:, i], iota_e.unsqueeze(2).to_broadcast([P, E, TOPK]),
                                   topf[:, i, 0:TOPK].unsqueeze(1).to_broadcast([P, E, TOPK]), ALU.is_equal)
        done(last)
        done(v.tensor_reduce(mask[:], eqk[:], AX_X, ALU.add))
        done(v.tensor_tensor(mask[:], mask[:], valid[:].unsqueeze(2).to_broadcast([P, NT, E]), ALU.mult))
        v.tensor_copy(mask_b[:], mask[:]).then_inc(s["mask"], 1)
        dve.wait_ge(s["exp"], 1)
        done(v.tensor_tensor(gate[:], gate[:], mask[:], ALU.mult))
        done(v.tensor_reduce(gsum[:], gate[:], AX_X, ALU.add))
        done(v.tensor_scalar(gsum[:], gsum[:], 1e-30, None, ALU.max))
        done(v.reciprocal(gsum[:], gsum[:]))
        rank, slotval = tb["rank"], tb["slotval"]
        v.memset(rank[:], -1.0)
        done(v.memset(slotval[:], 0.0))
        v.tensor_tensor(slotval[:, :, 0:E, 2], gate[:], gsum[:].unsqueeze(2).to_broadcast([P, NT, E]), ALU.mult)
        v.tensor_copy(slotval[:, :, 0:E, 0], tokv[:].unsqueeze(2).to_broadcast([P, NT, E]))
        for i in range(NT):
            last = v.tensor_tensor_scan(cum[:, i, :], ones[:, 0:E], mask[:, i, :], 0.0, ALU.mult, ALU.add)
        done(last)
        done(v.tensor_scalar(tokv[:], tokv[:], 4.0, None, ALU.mult))
        v.tensor_tensor(slotval[:, :, 0:E, 1], cum[:], tokv[:].unsqueeze(2).to_broadcast([P, NT, E]), ALU.add)
        done(v.memset(cnt[:, 3, :], 0.0))
        v.tensor_scalar(slotval[:, :, :, 0], slotval[:, :, :, 0], -MISS, None, ALU.add)
        v.tensor_scalar(slotval[:, :, :, 1], slotval[:, :, :, 1], -1.0 - MISS, None, ALU.add)
        dve.wait_ge(s["rank_psum"], 1)
        done(v.tensor_scalar(cum[:], bank[7][:, 0:NT * E].rearrange("p (i e) -> p i e", i=NT), 1.0, None, ALU.add))
        done(v.tensor_tensor(cum[:], cum[:], mask[:], ALU.mult))
        v.tensor_scalar(rank[:, :, 0:E], cum[:], -1.0, None, ALU.add)
        c, extra, upto = cnt[:, 0, :], cnt[:, 1, :], cnt[:, 2, :]
        done(v.tensor_copy(c, bank[7][:, NT * E:(NT + 1) * E]))
        done(v.tensor_scalar(extra, c, float(P), None, ALU.is_gt))
        for t in range(2, NT):
            done(v.scalar_tensor_tensor(out=extra, in0=c, scalar=float(t * P), in1=extra, op0=ALU.is_gt, op1=ALU.add))
        done(v.tensor_tensor_scan(upto, ones[:, 0:E], extra, 0.0, ALU.mult, ALU.add))
        b_no = tb["iota_s"][:, 0:NOVER]
        done(v.tensor_tensor(om[:, 0], upto.unsqueeze(1).to_broadcast([P, NOVER, E]),
                             b_no.unsqueeze(2).to_broadcast([P, NOVER, E]), ALU.is_le))
        v.tensor_reduce(of[:, 0, :], om[:, 0], AX_X, ALU.add)
        done(v.tensor_tensor(om[:, 1], om[:, 0], extra.unsqueeze(1).to_broadcast([P, NOVER, E]), ALU.mult))
        done(v.tensor_reduce(of[:, 1, :], om[:, 1], AX_X, ALU.add))
        done(v.tensor_tensor(of[:, 2, :], b_no, of[:, 1, :], ALU.subtract))
        v.tensor_scalar(tb["over_base"][:], of[:, 2, :], 1.0, float(P), ALU.add, ALU.mult)
        v.tensor_scalar(tb["over_i"][:, 0, :], of[:, 0, :], float(E - 1), None, ALU.min)
        v.tensor_tensor(tb["over_i"][:, 1, :], upto[:, E - 1:E].to_broadcast([P, NOVER]), b_no, ALU.is_gt).then_inc(s["done"], 1)
        dve.wait_ge(s["done"], 1)

def experts(nc, a, scratch, stack, sb, sem, bank, keep, mid, tb, landed):
    def buf(name, shape, dt=F32):
        return sb(stack, name, shape, dt)

    ident = keep["ident"]
    ring_lo, ring_hi = keep["ring_lo"], mid["w_out"]
    xg = buf("xg", [P, D])
    xT = buf("xT", [P, KD, P])
    g_sb = buf("g_sb", [P, 2, 512])
    u_sb = buf("u_sb", [P, 2, 512])
    sg = buf("sg", [P, 2, 512])
    h_sb = buf("h_sb", [P, 2, 512])
    hT = buf("hT_e", [P, KD, P])
    yo = buf("yo", [P, D])
    onehot = buf("onehot", [P, NT, P])
    idx_next = buf("idx_next", [P, 2], I32)
    gate_next = buf("gate_next", [P, 1])
    row_cur = buf("row_cur", [P, 1], I32)
    gate_cur = buf("gate_cur", [P, 1])
    zero = buf("zero", [P, 1])

    s = {n: sem("e_" + n) for n in (
        "used onehot sel_psum idx x_in xT_psum xT_lo xT_hi gu_psum gu_read g_min sig h hT_psum hT y_psum y_sb "
        "y_stored y_out y_free step curd clean turns".split())}
    block = stack.enter_context(nc.Block())

    def unit(j):
        return ring_lo[:, j, :] if j < 16 else ring_hi[:, j - 16, :]


    @block.sync
    def _(sp):
        for j in range(8, PAIRS):
            weight_load(sp, a, keep, mid, 0, j).then_inc(landed[j], 16)

        def load(e, q):
            for j in range(PAIRS):
                sp.wait_ge(s["used"], PAIRS * q + (j + 1 - PAIRS))
                weight_load(sp, a, keep, mid, e, j).then_inc(landed[j], 16)

        with sp.Fori(1, E) as e:
            load(e, e)
        with sp.Fori(0, NOVER) as b:
            active = sp.value_load(tb["over_i"][0:1, 1, bass.ds(b, 1)], min_val=0, max_val=1)
            with sp.If(active > 0):
                e = sp.value_load(tb["over_i"][0:1, 0, bass.ds(b, 1)], min_val=0, max_val=E - 1)
                load(e, b + E)

    @block.gpsimd
    def _(pool):
        nc.gpsimd.memset(xg[:], 0.0).then_inc(s["clean"], 1)
        pool.sem_inc(s["y_out"], 1)
        pool.wait_ge(s["clean"], 1)

        def gather(p):
            pool.wait_ge(s["idx"], p)
            pool.sem_inc(s["turns"], 1)
            nc.gpsimd.indirect_dma_start(xg[:], None, scratch["hf"], bass.IndirectOffsetOnAxis(ap=idx_next[:, 0:1].bitcast(U32), axis=0),
                                         bounds_check=TOK - 1, oob_is_err=False).then_inc(s["x_in"], 16)

        def scatter(q):
            pool.wait_ge(s["y_sb"], q + 1)
            pool.sem_inc(s["turns"], 1)
            nc.gpsimd.indirect_dma_start(scratch["picked"], bass.IndirectOffsetOnAxis(ap=row_cur[:, 0:1].bitcast(U32), axis=0), yo[:], None,
                                         bounds_check=TOK * TOPK - 1, oob_is_err=False).then_inc(s["y_stored"], 16)
            pool.wait_ge(s["y_stored"], 16 * q + 16)
            pool.sem_inc(s["y_out"], 1)

        gather(1)
        with pool.Fori(0, E) as e:
            gather(e + 2)
            scatter(e)
        with pool.Fori(0, NOVER) as b:
            active = pool.value_load(tb["over_i"][0:1, 1, bass.ds(b, 1)], min_val=0, max_val=1)
            with pool.If(active > 0):
                gather(b + (E + 2))
                scatter(b + E)

    @block.scalar
    def _(act):
        def body(q, p, prep):
            for half in range(2):
                act.wait_ge(s["g_min"], 2 * q + half + 1)
                nc.scalar.activation(sg[:, half, :], g_sb[:, half, :], ACT.Sigmoid, scale=ALPHA).then_inc(s["sig"], 1)
                if half == 1 and prep:
                    take_x(p + 1)
                act.wait_ge(s["hT_psum"], 2 * q + half + 1)
                nc.scalar.activation(hT[:, 4 * half:4 * half + 4, :].rearrange("p k t -> p (k t)"), bank[6 + half][:], ACT.Copy).then_inc(s["hT"], 1)
            act.wait_ge(s["y_psum"], q + 1)
            act.wait_ge(s["y_out"], q + 1)
            for h in range(2):
                last = nc.scalar.activation(yo[:, h * 512:(h + 1) * 512], bank[4 + h][:], ACT.Copy, scale=gate_cur[:, 0:1])
            last.then_inc(s["y_sb"], 1)
            act.wait_ge(s["y_sb"], q + 1)
            act.sem_inc(s["y_free"], 1)

        def take_x(p):
            act.wait_ge(s["xT_psum"], p)
            nc.scalar.activation(xT[:, 4:8, :].rearrange("p k t -> p (k t)"), bank[1][:], ACT.Copy).then_inc(s["xT_hi"], 1)

        act.sem_inc(s["y_free"], 1)
        take_x(1)
        with act.Fori(0, E) as e:
            body(e, e + 1, True)
        with act.Fori(0, NOVER) as b:
            active = act.value_load(tb["over_i"][0:1, 1, bass.ds(b, 1)], min_val=0, max_val=1)
            with act.If(active > 0):
                take_x(b + (E + 2))
                body(b + E, b + (E + 2), False)

    @block.tensor
    def _(pe):
        def select(e, p):
            pe.wait_ge(s["onehot"], p)
            for i in range(NT):
                last = nc.tensor.matmul(bank[6][:, 0:3], onehot[:, i, :], tb["slotval"][:, i, bass.ds(e, 1), :].rearrange("p a c -> p (a c)"),
                                        start=(i == 0), stop=(i == NT - 1))
            last.then_inc(s["sel_psum"], 1)

        def x_transposes(p):
            pe.wait_ge(s["x_in"], p * 16)
            for k in range(KD):
                last = nc.tensor.transpose(bank[k // 4][:, (k % 4) * P:(k % 4 + 1) * P], xg[:, k * P:(k + 1) * P], ident[:])
            last.then_inc(s["xT_psum"], 1)

        def gate_up(q, half, e):
            for j in range(4):
                pe.wait_ge(landed[4 * half + j], 16 * q + 16)
                for k in (2 * j, 2 * j + 1):
                    for u in range(2):
                        last = nc.tensor.matmul(bank[2 * half + u][:], xT[:, k, :], unit(8 * half + k)[:, u * 512:(u + 1) * 512],
                                                start=(k == 0), stop=False)
                if j < 3:
                    last.then_inc(s["used"], 1)
            for u in range(2):
                c = u * FF + half * 512
                last = nc.tensor.matmul(bank[2 * half + u][:], tb["pick_row"][:, bass.ds(e, 1), :].rearrange("p a c -> p (a c)"),
                                        tb["bias"][:, c:c + 512], start=False, stop=True)
                last.then_inc(s["used"] if u == 0 else s["gu_psum"], 1)

        def down(q, half, e):
            for j in range(2):
                pe.wait_ge(landed[8 + 2 * half + j], 16 * q + 16)
                for k in (4 * half + 2 * j, 4 * half + 2 * j + 1):
                    for h in range(2):
                        last = nc.tensor.matmul(bank[4 + h][:], hT[:, k, :], unit(16 + k)[:, h * 512:(h + 1) * 512],
                                                start=(k == 0), stop=False)
                if half == 0 or j == 0:
                    last.then_inc(s["used"], 1)
            if half == 1:
                for h in range(2):
                    c = 2 * FF + h * 512
                    last = nc.tensor.matmul(bank[4 + h][:], tb["pick_row"][:, bass.ds(e, 1), :].rearrange("p a c -> p (a c)"),
                                            tb["bias"][:, c:c + 512], start=False, stop=True)
                    last.then_inc(s["used"] if h == 0 else s["y_psum"], 1)

        def h_transposes(q, half):
            pe.wait_ge(s["h"], 2 * q + half + 1)
            for k in range(4):
                last = nc.tensor.transpose(bank[6 + half][:, k * P:(k + 1) * P], h_sb[:, half, k * P:(k + 1) * P], ident[:])
            last.then_inc(s["hT_psum"], 1)

        def body(q, p, e, prep):
            pe.wait_ge(s["xT_lo"], p)
            pe.wait_ge(s["xT_hi"], p)
            pe.wait_ge(s["gu_read"], 2 * q + 1)
            gate_up(q, 0, e)
            if prep:
                select(e + 1, p + 1)
            pe.wait_ge(s["gu_read"], 2 * q + 2)
            gate_up(q, 1, e)
            if prep:
                pe.wait_ge(s["idx"], p + 1)
            h_transposes(q, 0)
            pe.wait_ge(s["hT"], 2 * q + 1)
            pe.wait_ge(s["y_free"], q + 1)
            down(q, 0, e)
            if prep:
                pe.wait_ge(s["gu_read"], 2 * q + 3)
                x_transposes(p + 1)
            h_transposes(q, 1)
            pe.wait_ge(s["hT"], 2 * q + 2)
            down(q, 1, e)

        select(0, 1)
        x_transposes(1)
        with pe.Fori(0, E) as e:
            body(e, e + 1, e, True)
        with pe.Fori(0, NOVER) as b:
            active = pe.value_load(tb["over_i"][0:1, 1, bass.ds(b, 1)], min_val=0, max_val=1)
            with pe.If(active > 0):
                e = pe.value_load(tb["over_i"][0:1, 0, bass.ds(b, 1)], min_val=0, max_val=E - 1)
                select(e, b + (E + 2))
                x_transposes(b + (E + 2))
                body(b + E, b + (E + 2), e, False)

    @block.vector
    def _(dve):
        v = nc.vector

        def pick(e, base):
            v.scalar_tensor_tensor(out=onehot[:], in0=tb["rank"][:, :, bass.ds(e, 1)].to_broadcast([P, NT, P]), scalar=base,
                                   in1=tb["iota_s"][:].unsqueeze(1).to_broadcast([P, NT, P]),
                                   op0=ALU.subtract, op1=ALU.is_equal).then_inc(s["onehot"], 1)

        def take_slots(p):
            dve.wait_ge(s["sel_psum"], p)
            v.tensor_copy(gate_next[:], bank[6][:, 2:3])
            v.tensor_scalar(idx_next[:], bank[6][:, 0:2], MISS, None, ALU.add).then_inc(s["idx"], 1)

        def take_x(p):
            dve.wait_ge(s["xT_psum"], p)
            v.tensor_copy(xT[:, 0:4, :].rearrange("p k t -> p (k t)"), bank[0][:]).then_inc(s["xT_lo"], 1)

        def swiglu(q, half):
            dve.wait_ge(s["gu_psum"], 2 * q + half + 1)
            g, u = g_sb[:, half, :], u_sb[:, half, :]
            v.tensor_scalar(g, bank[2 * half][:], LIMIT, None, ALU.min).then_inc(s["g_min"], 1)
            v.tensor_scalar(u, bank[2 * half + 1][:], LIMIT, -LIMIT, ALU.min, ALU.max).then_inc(s["gu_read"], 1)
            dve.wait_ge(s["gu_read"], 2 * q + half + 3)
            dve.wait_ge(s["g_min"], 2 * q + half + 1)
            v.scalar_tensor_tensor(out=u, in0=u, scalar=1.0, in1=g, op0=ALU.add, op1=ALU.mult).then_inc(s["step"], 1)
            dve.wait_ge(s["step"], 2 * q + half + 1)
            dve.wait_ge(s["sig"], 2 * q + half + 1)
            v.tensor_tensor(h_sb[:, half, :], u, sg[:, half, :], ALU.mult).then_inc(s["h"], 1)

        def body(q, p, e, prep):
            dve.wait_ge(s["y_out"], q + 1)
            dve.wait_ge(s["idx"], p)
            v.tensor_copy(row_cur[:], idx_next[:, 1:2])
            v.tensor_copy(gate_cur[:], gate_next[:]).then_inc(s["curd"], 1)
            dve.wait_ge(s["curd"], q + 1)
            if prep:
                pick(e + 1, zero[:, 0:1])
            swiglu(q, 0)
            if prep:
                take_slots(p + 1)
            swiglu(q, 1)
            if prep:
                take_x(p + 1)

        v.memset(zero[:], 0.0)
        v.memset(g_sb[:, 0, 0:1], 0.0).then_inc(s["gu_read"], 2)
        dve.wait_ge(s["gu_read"], 2)
        pick(0, zero[:, 0:1])
        take_slots(1)
        take_x(1)
        with dve.Fori(0, E) as e:
            body(e, e + 1, e, True)
        with dve.Fori(0, NOVER) as b:
            active = dve.value_load(tb["over_i"][0:1, 1, bass.ds(b, 1)], min_val=0, max_val=1)
            with dve.If(active > 0):
                e = dve.value_load(tb["over_i"][0:1, 0, bass.ds(b, 1)], min_val=0, max_val=E - 1)
                pick(e, tb["over_base"][:, bass.ds(b, 1)])
                take_slots(b + (E + 2))
                take_x(b + (E + 2))
                body(b + E, b + (E + 2), e, False)


def combine(nc, a, out, scratch, stack, sb, sem, keep):
    x = keep["x"]
    ring = keep["ring_lo"][:, :, :].rearrange("p (b k) n -> p b k n", k=TOPK)
    NB = 4
    gfin = sb(stack, "gfin", [P, D])
    ssf = sb(stack, "ssf", [P, 3, NT])
    jf = sb(stack, "jf", [P, D])
    of = sb(stack, "of_fin", [P, NT, D])
    g_in, summed, sq, var, root, fin, stored, step = (sem("c_" + n) for n in "g_in summed sq var root fin stored step".split())
    rows_in = [sem(f"c_rows{i}") for i in range(NB)]
    block = stack.enter_context(nc.Block())
    picked = scratch["picked"].rearrange("(t k) n -> t k n", k=TOPK)
    outs = 1 + (NT - 2) + 2

    @block.sync
    def _(sp):
        for i in range(NT):
            if i >= NB:
                sp.wait_ge(summed, i - NB + 1)
            sp.dma_start(ring[0:rows(i), i % NB], picked[i * P:i * P + rows(i)]).then_inc(rows_in[i % NB], 16)
            if i == 0:
                sp.dma_start(gfin[:], a["norm_final"].unsqueeze(0).to_broadcast([P, D])).then_inc(g_in, 16)
        y_p = out["y_p"][0]
        for i in range(NT):
            sp.wait_ge(fin, i + 1)
            if i == 0:
                sp.dma_start(y_p[0:P - NMETA, :], of[NMETA:P, 0, :]).then_inc(stored, 16)
            elif i < NT - 1:
                sp.dma_start(y_p[i * P - NMETA:(i + 1) * P - NMETA, :], of[:, i, :]).then_inc(stored, 16)
            else:
                n = LAST - NDEC
                sp.dma_start(y_p[SEQ - n:SEQ, :], of[0:n, i, :]).then_inc(stored, 16)
                sp.dma_start(out["y_s"][:, 0, :], of[n:LAST, i, :]).then_inc(stored, 16)
        sp.wait_ge(stored, 16 * outs)

    @block.scalar
    def _(act):
        for i in range(NT):
            n = rows(i)
            act.wait_ge(summed, i + 1)
            nc.scalar.activation(jf[0:n], x[0:n, i, :], ACT.Square, accum_out=ssf[0:n, 2, i:i + 1]).then_inc(sq, 1)
            act.wait_ge(var, i + 1)
            nc.scalar.activation(ssf[0:n, 0, i:i + 1], ssf[0:n, 2, i:i + 1], ACT.Sqrt).then_inc(root, 1)

    @block.vector
    def _(dve):
        v = nc.vector
        count = [0]

        def done(ins):
            count[0] += 1
            ins.then_inc(step, 1)
            dve.wait_ge(step, count[0])

        def finish(i):
            n = rows(i)
            dve.wait_ge(sq, i + 1)
            v.tensor_scalar(ssf[0:n, 2, i:i + 1], ssf[0:n, 2, i:i + 1], 1.0 / D, EPS, ALU.mult, ALU.add).then_inc(var, 1)
            dve.wait_ge(root, i + 1)
            done(refine_rsqrt(nc, done, ssf[0:n, 0, i:i + 1], ssf[0:n, 1, i:i + 1], ssf[0:n, 2, i:i + 1]))
            v.scalar_tensor_tensor(out=of[0:n, i, :], in0=x[0:n, i, :], scalar=ssf[0:n, 0, i:i + 1], in1=gfin[0:n, :],
                                   op0=ALU.mult, op1=ALU.mult).then_inc(fin, 1)

        dve.wait_ge(g_in, 16)
        for i in range(NT):
            n = rows(i)
            dve.wait_ge(rows_in[i % NB], 16 * (i // NB + 1))
            r = ring[0:n, i % NB]
            v.tensor_tensor(r[:, 0], r[:, 0], r[:, 1], ALU.add)
            done(v.tensor_tensor(r[:, 2], r[:, 2], r[:, 3], ALU.add))
            done(v.tensor_tensor(r[:, 0], r[:, 0], r[:, 2], ALU.add))
            v.tensor_tensor(x[0:n, i, :], x[0:n, i, :], r[:, 0], ALU.add).then_inc(summed, 1)
            if i >= 1:
                finish(i - 1)
        finish(NT - 1)


_INS = ["x_prompt", "x_sample", "state_ssm_re", "state_ssm_im", "state_conv", "meta_tokens", "norm_mix", "w_in",
        "ssm_a_re", "ssm_a_im", "ssm_log_dt", "ssm_b_re", "ssm_b_im", "ssm_c_re", "ssm_c_im", "ssm_d", "w_glu", "b_glu",
        "conv_w", "norm_out_ssm", "norm_out_conv", "w_out", "norm_ffn", "w_router", "b_router", "w_gate_up",
        "b_gate_up", "w_down", "b_down", "norm_final"]
_OUTS = [("y_p", (1, SEQ, D)), ("y_s", (NDEC, 1, D)), ("re_p", (1, 1, GROUPS, NS)), ("im_p", (1, 1, GROUPS, NS)),
         ("conv_p", (1, 1, 2, W)), ("re_s", (1, NDEC, GROUPS, NS)), ("im_s", (1, NDEC, GROUPS, NS)), ("conv_s", (1, NDEC, 2, W))]


def kernel(**inputs):
    import numpy as np
    import concourse.bacc as bacc
    from concourse.bass_utils import run_bass_kernel_spmd

    nc = bacc.Bacc("TRN2", target_bir_lowering=False, num_devices=1)
    arrays, a = {}, {}
    for name in _INS:
        v = np.ascontiguousarray(inputs[name])
        arrays[f"in_{name}"] = v
        a[name] = nc.dram_tensor(f"in_{name}", v.shape, mybir.dt.from_np(v.dtype), kind="ExternalInput").ap()
    out = {n: nc.dram_tensor(f"out_{n}", shape, F32, kind="ExternalOutput").ap() for n, shape in _OUTS}
    hybrid_step(nc, a, out)
    r = run_bass_kernel_spmd(nc, [arrays], core_ids=[0])
    return tuple(r.results[0][f"out_{n}"] for n, _ in _OUTS)
```

```python
import math
from contextlib import ExitStack

import concourse.bass as bass
from concourse import mybir

F32 = mybir.dt.float32
F32R = mybir.dt.float32r
BF16 = mybir.dt.bfloat16
I32 = mybir.dt.int32
U32 = mybir.dt.uint32
ALU = mybir.AluOpType
ACT = mybir.ActivationFunctionType
AX_X = mybir.AxisListType.X

P = 128
D = 1024
KD = D // P
NMETA, SEQ, NDEC = 16, 512, 8
NPROMPT = NMETA + SEQ
TOK = NPROMPT + NDEC
NT = (TOK + P - 1) // P
LAST = TOK - (NT - 1) * P
W = 512
MT = W // P
GROUPS, GCH, NS = 32, 16, 64
GP = GROUPS // 2
CH = 8
NCH = NPROMPT // CH
YC = NCH + 1 + NDEC
DEC0 = NCH + 1
UC = YC + NDEC
E = 32
TOPK = 4
FF = D
EPS = 1e-5
LIMIT = 7.0
ALPHA = 1.702
NOVER = (TOK * TOPK + E * (P - 1)) // P - E + 1
UNITS = 24
PAIRS = UNITS // 2
MISS = 4096.0
HALF = 264
REST = TOK - HALF


def rows(i):
    return P if i < NT - 1 else LAST


def refine_rsqrt(nc, done, r, t, v):
    done(nc.vector.reciprocal(r, r))
    done(nc.vector.tensor_tensor(t, r, r, ALU.mult))
    done(nc.vector.tensor_tensor(t, t, v, ALU.mult))
    done(nc.vector.tensor_scalar(t, t, -0.5, 1.5, ALU.mult, ALU.add))
    return nc.vector.tensor_tensor(r, r, t, ALU.mult)


def hybrid_step(nc, a, out):
    scratch = {
        "u": nc.dram_tensor("u_shuffle", [W, CH, YC], F32).ap(),
        "hf": nc.dram_tensor("ffn_in", [TOK, D], F32).ap(),
        "picked": nc.dram_tensor("expert_rows", [TOK * TOPK, D], F32).ap(),
    }
    with ExitStack() as ctx:
        def sb(stack, name, shape, dt=F32):
            return stack.enter_context(nc.sbuf_tensor(name, shape, dt))

        def sem(name):
            return ctx.enter_context(nc.semaphore(name))

        bank = [ctx.enter_context(nc.psum_tensor(f"bank{i}", [P, 512], F32)) for i in range(8)]
        keep = {
            "x": sb(ctx, "x", [P, NT, D]),
            "ident": sb(ctx, "ident", [P, P]),
            "pcol": sb(ctx, "pcol", [P, 36]),
            "ring_lo": sb(ctx, "ring_lo", [P, 16, 1024]),
        }
        with ExitStack() as st:
            mid = {
                "ymix": sb(st, "ymix", [P, MT, TOK]),
                "cmix": sb(st, "cmix", [P, MT, TOK]),
                "w_out": sb(st, "w_out", [P, KD, D]),
            }
            with ExitStack() as s1:
                mixer(nc, a, out, scratch, s1, sb, sem, bank, keep, mid)
            with ExitStack() as s2:
                tables = loop_tables(s2, sb)
                with ExitStack() as s3:
                    router(nc, a, scratch, s3, sb, sem, bank, keep, mid, tables)
                landed = keep["landed"]
                experts(nc, a, scratch, s2, sb, sem, bank, keep, mid, tables, landed)
        with ExitStack() as s4:
            combine(nc, a, out, scratch, s4, sb, sem, keep)


def mixer(nc, a, out, scratch, stack, sb, sem, bank, keep, mid):
    def buf(name, shape, dt=F32):
        return sb(stack, name, shape, dt)

    x, ident, pcol = keep["x"], keep["ident"], keep["pcol"]
    flat = keep["ring_lo"][:, :, :].rearrange("p a b -> p (a b)")
    BLK = KD * W
    w_in = flat.rearrange("p (blk k n) -> p blk k n", blk=4, k=KD)
    carve = [0]

    def late(n):
        v = flat[:, carve[0]:carve[0] + n]
        carve[0] += n
        return v

    toep = late(CH * W).rearrange("p (t n) -> p t n", t=CH)
    v_sb = late(2 * GP * UC).rearrange("p (r g c) -> p r g c", r=2, g=GP)
    s_sb = late(2 * GP * YC).rearrange("p (r g c) -> p r g c", r=2, g=GP)
    ZN = GP * NCH
    z0 = carve[0]
    y_ch = late(4 * ZN)[:, 0:MT * CH * YC]
    wz = [flat[:, z0 + i * ZN:z0 + (i + 1) * ZN] for i in range(4)]
    w_glu = late(MT * W).rearrange("p (k n) -> p k n", k=MT)
    wo_flat = mid["w_out"][:, :, :].rearrange("p a b -> p (a b)")
    PW = 2 * GP * CH * GCH
    p_sb = wo_flat[:, 0:PW].rearrange("p (r g i h) -> p r g i h", r=2, g=GP, i=CH)
    q_sb = wo_flat[:, PW:2 * PW].rearrange("p (r g t h) -> p r g t h", r=2, g=GP, t=CH)
    y_blk = wo_flat[0:YC, 0:PW].rearrange("c (t n) -> c t n", t=CH)
    rot = mid["ymix"][:, :, :].rearrange("p m t -> p (m t)")[:, 0:2 * ZN].rearrange("p (r g c) -> p r g c", r=2, g=GP)

    hT = buf("hT", [P, KD, TOK])
    hflat = hT[:, :, :].rearrange("p k t -> p (k t)")
    wb = hflat[:, 0:2 * GP * P].rearrange("p (r g n) -> p r g n", r=2, g=GP)
    YN = MT * CH * YC
    gel = hflat[:, 0:YN]
    u_ch = buf("u_ch", [P, MT, CH, YC])
    u_flat = u_ch[:, :, :, :].rearrange("p m t c -> p (m t c)")
    zg = buf("zg", [P, MT, TOK + 2])
    u_blk = buf("u_blk", [P, GROUPS, UC])
    ublk_flat = u_blk[:, :, :].rearrange("p g c -> p (g c)")
    xs0 = buf("xs0", [P, ZN])
    xs = [xs0[:, 0:D], ublk_flat[:, 0:D]]
    junk = ublk_flat[:, D:2 * D]
    rho_t = xs0[:, :]
    prow = buf("prow", [36, P])
    arow = buf("arow", [GP, 4, P])
    dtrow = buf("dtrow", [GP, 2])
    par = buf("par", [P, 4, GP])
    bt = buf("bt", [P, 2, GP, GCH])
    bbar = buf("bbar", [P, 2, GP, GCH])
    ctl = buf("ctl", [P, 2, 2, P])
    ct = buf("ct", [P, 2, GP, GCH])
    cz = buf("cz", [P, 2, GP, 2, GCH])
    apow = buf("apow", [P, 2, CH + 1, GP])
    sm = buf("sm", [P, 24, GP])
    tmp = buf("tmp", [P, 2 * TOK])
    tpool = buf("tpool", [P, 2, GP, GCH])
    ss = buf("ss", [P, 3 * NT])
    s0l = buf("s0l", [P, 2, P])
    stout = bt[:, :, :, :].rearrange("p r g h -> p (r g h)")[:, 0:2 * GP + 2 * P]
    sttr = ctl[:, :, :, :].rearrange("p a b c -> p (a b) c")[:, 0:3, :]
    cbl = ublk_flat[0:2 * NDEC, 2 * D:2 * D + W]
    cbt = buf("cbt", [P, MT, 2 * NDEC])
    crow = ct[:, :, :, :].rearrange("p r g h -> p (r g h)")[0:2 + NDEC, :]
    tkern = bbar[:, :, :, :].rearrange("p r g h -> p (r g h)")
    NM, CW, NOS, NOC, DS, BG = 0, 8, 20, 24, 28, 32
    ORDER = [0, 1, 2, 3, 4, 5, 6, 7, 12, 13, 14, 15, 8, 9, 10, 11]

    names = ("ident zeroed prow_in prow_psum pcol a_in dt_exp arow a_psum par exps b_in c_in c_psum ct "
             "s0_psum s0_done cb_in cb_psum cbt ss var root rstd xs xT_psum hT proj u_stored u_blk_in apow "
             "p_ready q_ready pt_psum wb k_psum k_sb toep_zero toep v_psum v ublk_zero "
             "state_in y_psum y_blk yt_psum y_ch st_ready st_psum sttr conv_z crow_psum crow "
             "gel_in gel_sig y_gelu glu_psum glu_sig out_done cz").split()
    s = {n: sem("m_" + n) for n in names}
    x_in = [sem(f"m_x_in{i}") for i in range(NT)]
    w_in_in = [sem(f"m_w_in{i}") for i in range(4)]
    wglu_in = sem("m_wglu")
    proj_free = [sem("m_proj_free0"), sem("m_proj_free1")]
    dve_step, pool_step = sem("m_dve_step"), sem("m_pool_step")
    keep["wout_in"] = sem("wout_in")

    def taken(eng, n):
        eng.wait_ge(proj_free[n % 2], n // 2 + 1)

    def gel_v(v):
        return v.rearrange("p (m t c) -> p m t c", m=MT, t=CH)

    block = stack.enter_context(nc.Block())

    @block.sync
    def _(sp):
        for i in range(NT):
            if i == 0:
                sp.dma_start(x[0:NMETA, 0, :], a["meta_tokens"]).then_inc(x_in[0], 16)
                sp.dma_start(x[NMETA:P, 0, :], a["x_prompt"][0, 0:P - NMETA, :]).then_inc(x_in[0], 16)
            elif i < NT - 1:
                sp.dma_start(x[:, i, :], a["x_prompt"][0, i * P - NMETA:(i + 1) * P - NMETA, :]).then_inc(x_in[i], 16)
            else:
                n = LAST - NDEC
                sp.dma_start(x[0:n, i, :], a["x_prompt"][0, SEQ - n:SEQ, :]).then_inc(x_in[i], 16)
                sp.dma_start(x[n:LAST, i, :], a["x_sample"][:, 0, :]).then_inc(x_in[i], 16)
        w_src = a["w_in"][0].rearrange("(k p) (b n) -> b p k n", p=P, b=4)
        for blk in (0, 1, 3, 2):
            sp.dma_start(w_in[:, blk], w_src[blk]).then_inc(w_in_in[blk], 16)
        for n in range(MT):
            taken(sp, n)
        sp.dma_start(scratch["u"].rearrange("(m p) t c -> p m (t c)", p=P),
                     u_ch[:, :, :, :].rearrange("p m t c -> p m (t c)")).then_inc(s["u_stored"], 16)
        sp.wait_ge(s["u_stored"], 16)
        sp.wait_ge(s["ublk_zero"], 1)
        u_src = scratch["u"].rearrange("(g h) t c -> t h g c", h=GCH)
        for t in range(CH):
            sp.dma_start(u_blk[t * GCH:(t + 1) * GCH, :, 0:YC], u_src[t]).then_inc(s["u_blk_in"], 16)
        sp.dma_start(u_blk[(CH - 1) * GCH:P, :, YC:UC], u_src[0, :, :, DEC0:YC]).then_inc(s["u_blk_in"], 16)
        sp.wait_ge(s["proj"], 16)
        sp.dma_start(w_glu, a["w_glu"][0].rearrange("(k p) n -> p k n", p=P)).then_inc(wglu_in, 16)
        sp.wait_ge(s["k_sb"], 1)
        sp.wait_ge(s["toep_zero"], 1)
        for t in range(CH):
            sp.dma_start(toep[0:(t + 1) * GCH, t, :], tkern[(CH - 1 - t) * GCH:P, :]).then_inc(s["toep"], 16)
        sp.wait_ge(s["y_ch"], 6)
        sp.dma_start(mid["w_out"][:], a["w_out"][0].rearrange("(k p) n -> p k n", p=P)).then_inc(keep["wout_in"], 16)
        sp.wait_ge(s["sttr"], 1)
        for r, (p_out, s_out) in enumerate((("re_p", "re_s"), ("im_p", "im_s"))):
            sp.dma_start(out[p_out][0, 0].rearrange("(g a) n -> g (a n)", a=2), sttr[r * GP:(r + 1) * GP, 0, :]).then_inc(s["out_done"], 16)
            sp.dma_start(out[s_out][0].rearrange("b (g a) n -> (b g) (a n)", a=2), sttr[:, 1 + r, :]).then_inc(s["out_done"], 16)
        sp.wait_ge(s["crow"], 1)
        sp.dma_start(out["conv_p"][0, 0], crow[0:2, :]).then_inc(s["out_done"], 16)
        sp.dma_start(out["conv_s"][0, :, 1, :], crow[2:2 + NDEC, :]).then_inc(s["out_done"], 16)
        sp.dma_start(out["conv_s"][0, :, 0, :], a["state_conv"][0, :, 1, :]).then_inc(s["out_done"], 16)
        sp.wait_ge(s["out_done"], 7 * 16)

    @block.scalar
    def _(act):
        act.dma_start(prow[NM:NM + 8, :], a["norm_mix"][0].rearrange("(k p) -> k p", p=P)).then_inc(s["prow_in"], 16)
        for k in range(3):
            act.dma_start(prow[CW + 4 * k:CW + 4 * k + 4, :], a["conv_w"][0, k].rearrange("(m p) -> m p", p=P)).then_inc(s["prow_in"], 16)
        for o, n in ((NOS, "norm_out_ssm"), (NOC, "norm_out_conv"), (DS, "ssm_d"), (BG, "b_glu")):
            act.dma_start(prow[o:o + 4, :], a[n][0].rearrange("(m p) -> m p", p=P)).then_inc(s["prow_in"], 16)
        act.dma_start(arow[:, 0, :], a["ssm_a_re"][0].rearrange("(g a) n -> g (a n)", a=2)).then_inc(s["a_in"], 16)
        act.dma_start(arow[:, 1, :], a["ssm_a_im"][0].rearrange("(g a) n -> g (a n)", a=2)).then_inc(s["a_in"], 16)
        act.dma_start(dtrow[:], a["ssm_log_dt"][0].rearrange("(g a) -> g a", a=2)).then_inc(s["a_in"], 16)
        act.wait_ge(s["a_in"], 48)
        nc.scalar.activation(dtrow[:], dtrow[:], ACT.Exp).then_inc(s["dt_exp"], 1)
        for i in range(NT):
            n = rows(i)
            act.wait_ge(x_in[i], 32 if i in (0, NT - 1) else 16)
            nc.scalar.activation(junk[0:n], x[0:n, i, :], ACT.Square, accum_out=ss[0:n, i:i + 1]).then_inc(s["ss"], 1)
            act.wait_ge(s["var"], i + 1)
            nc.scalar.activation(ss[0:n, NT + i:NT + i + 1], ss[0:n, i:i + 1], ACT.Sqrt).then_inc(s["root"], 1)
            act.wait_ge(s["rstd"], i + 1)
            if i >= 2:
                act.wait_ge(s["xT_psum"], i - 1)
            nc.scalar.activation(xs[i % 2][0:n], x[0:n, i, :], ACT.Copy, scale=ss[0:n, NT + i:NT + i + 1]).then_inc(s["xs"], 1)
        act.wait_ge(s["par"], 1)
        nc.scalar.activation(sm[:, 0, :], par[:, 2, :], ACT.Exp)
        nc.scalar.activation(sm[:, 1, :], par[:, 2, :], ACT.Exp, scale=float(CH)).then_inc(s["exps"], 1)
        act.wait_ge(s["zeroed"], 1)
        for n, m in enumerate(ORDER):
            if m >= 12:
                continue
            act.wait_ge(s["proj"], n + 1)
            b0, b1 = bank[2 * (n % 2)], bank[2 * (n % 2) + 1]
            if m < MT:
                c0 = HALF // CH
                nc.scalar.activation(u_ch[:, m, :, 0:c0], b0[:, 0:HALF].rearrange("p (c t) -> p t c", t=CH), ACT.Copy)
                nc.scalar.activation(u_ch[:, m, :, c0:NCH], b1[:, 0:NPROMPT - HALF].rearrange("p (c t) -> p t c", t=CH), ACT.Copy)
                nc.scalar.activation(u_ch[:, m, 0, DEC0:YC], b1[:, NPROMPT - HALF:REST], ACT.Copy).then_inc(proj_free[n % 2], 1)
            else:
                dst = zg[:, m - 4, 2:2 + TOK] if m < 8 else mid["cmix"][:, m - 8, :]
                nc.scalar.activation(dst[:, 0:HALF], b0[:, 0:HALF], ACT.Copy)
                nc.scalar.activation(dst[:, HALF:TOK], b1[:, 0:REST], ACT.Copy).then_inc(proj_free[n % 2], 1)
        act.wait_ge(s["k_psum"], 1)
        nc.scalar.activation(tkern, bank[6][:], ACT.Copy).then_inc(s["k_sb"], 1)
        for j in range(8):
            act.wait_ge(s["pt_psum"], j + 1)
            r, q = j // 4, j % 4
            nc.scalar.activation(wb[:, r, 4 * q:4 * q + 4, :], bank[4 + j % 2][:].rearrange("p (g n) -> p g n", g=4), ACT.Copy).then_inc(s["wb"], 1)
        for j in range(8):
            act.wait_ge(s["v_psum"], j + 1)
            nc.scalar.activation(v_sb[:, :, 2 * j:2 * j + 2, :],
                                 bank[4 + j % 2][:, 0:4 * UC].rearrange("p (g r c) -> p r g c", g=2, r=2), ACT.Copy).then_inc(s["v"], 1)
        for j in range(8):
            g0 = j % 2 + 8 * (j // 2)
            act.wait_ge(s["y_psum"], j + 1)
            nc.scalar.activation(y_blk[:, :, :].rearrange("c t (g h) -> c g t h", h=GCH)[:, g0:g0 + 7:2],
                                 bank[4 + j % 2][0:YC, :].rearrange("c (g t h) -> c g t h", g=4, t=CH), ACT.Copy).then_inc(s["y_blk"], 1)
        for j in range(6):
            n = min(6, MT * CH - 6 * j)
            act.wait_ge(s["yt_psum"], j + 1)
            nc.scalar.activation(y_ch[:, 6 * j * YC:(6 * j + n) * YC], bank[4 + j % 2][:, 0:n * YC], ACT.Copy).then_inc(s["y_ch"], 1)
        act.wait_ge(s["gel_in"], 1)
        nc.scalar.activation(gel, gel, ACT.Sigmoid, scale=2 * math.sqrt(2 / math.pi)).then_inc(s["gel_sig"], 1)
        for m in range(MT):
            act.wait_ge(s["glu_psum"], m + 1)
            for h in range(2):
                nc.scalar.activation(gel_v(gel)[:, m, 4 * h:4 * h + 4, :],
                                     bank[2 * (m % 2) + h][:, 0:4 * YC].rearrange("p (t c) -> p t c", t=4), ACT.Sigmoid,
                                     bias=pcol[:, BG + m:BG + m + 1]).then_inc(s["glu_sig"], 1)

    @block.gpsimd
    def _(pool):
        nc.gpsimd.memset(ident[:], 0.0).then_inc(pool_step, 1)
        pool.wait_ge(pool_step, 1)
        nc.gpsimd.affine_select(out=ident[:], in_=ident[:], compare_op=ALU.not_equal, fill=1.0, base=0,
                                pattern=[[-1, P]], channel_multiplier=1).then_inc(s["ident"], 1)
        for r, n in enumerate(("ssm_b_re", "ssm_b_im")):
            for g2 in range(2):
                pool.dma_start(bt[g2 * NS:(g2 + 1) * NS, r], a[n][0].rearrange("(g a) n h -> a n g h", a=2)[g2]).then_inc(s["b_in"], 16)
        for r, n in enumerate(("ssm_c_re", "ssm_c_im")):
            for half in range(2):
                for g in range(8):
                    pool.dma_start(ctl[g * GCH:(g + 1) * GCH, r, half, :].rearrange("h (a n) -> h a n", a=2),
                                   a[n][0].rearrange("(g a) h n -> g h a n", a=2)[half * 8 + g]).then_inc(s["c_in"], 16)
        for r, n in enumerate(("state_ssm_re", "state_ssm_im")):
            pool.dma_start(s0l[:, r, :], a[n][0].rearrange("b (g a) n -> (b g) (a n)", a=2)).then_inc(s["cb_in"], 16)
        pool.dma_start(cbl, a["state_conv"][0].rearrange("b k c -> (b k) c")).then_inc(s["cb_in"], 16)
        nc.gpsimd.memset(u_flat, 0.0)
        nc.gpsimd.memset(zg[:, :, 0:2], 0.0).then_inc(s["zeroed"], 1)
        nc.gpsimd.memset(cz[:], 0.0).then_inc(s["cz"], 1)
        pool.wait_ge(s["xT_psum"], NT)
        pool.wait_ge(s["cb_psum"], 1)
        nc.gpsimd.memset(u_blk[:, :, YC:UC], 0.0).then_inc(s["ublk_zero"], 1)
        pool.wait_ge(s["apow"], 1)
        pool.wait_ge(s["ct"], 1)
        steps = pool_step
        n = 1
        for t in range(CH):
            ar = apow[:, 0, t + 1, :].unsqueeze(2).to_broadcast([P, GP, GCH])
            ai = apow[:, 1, t + 1, :].unsqueeze(2).to_broadcast([P, GP, GCH])
            nc.gpsimd.tensor_tensor(q_sb[:, 0, :, t, :], ct[:, 0], ar, ALU.mult)
            nc.gpsimd.tensor_tensor(tpool[:, 0], ct[:, 1], ai, ALU.mult)
            nc.gpsimd.tensor_tensor(q_sb[:, 1, :, t, :], ct[:, 0], ai, ALU.mult)
            nc.gpsimd.tensor_tensor(tpool[:, 1], ct[:, 1], ar, ALU.mult).then_inc(steps, 1)
            n += 1
            pool.wait_ge(steps, n)
            nc.gpsimd.tensor_tensor(q_sb[:, 0, :, t, :], q_sb[:, 0, :, t, :], tpool[:, 0], ALU.subtract)
            nc.gpsimd.tensor_tensor(tpool[:, 1], q_sb[:, 1, :, t, :], tpool[:, 1], ALU.add).then_inc(steps, 1)
            n += 1
            pool.wait_ge(steps, n)
            nc.gpsimd.tensor_scalar(q_sb[:, 1, :, t, :], tpool[:, 1], -1.0, None, ALU.mult).then_inc(steps, 1)
            n += 1
            pool.wait_ge(steps, n)
        nc.gpsimd.memset(tpool[:, 0, 0, 0:1], 0.0).then_inc(s["q_ready"], 1)
        pool.wait_ge(s["proj"], 16)
        nc.gpsimd.memset(toep, 0.0).then_inc(s["toep_zero"], 1)

    @block.tensor
    def _(pe):
        pe.wait_ge(s["ident"], 1)
        pe.wait_ge(s["prow_in"], 16 * 8)
        nc.tensor.transpose(bank[0][:, 0:36], prow[:], ident[0:36, 0:36]).then_inc(s["prow_psum"], 1)

        def x_transposes(i):
            n = rows(i)
            pe.wait_ge(s["xs"], i + 1)
            if i >= 2:
                pe.wait_ge(s["hT"], 2 * (i - 1))
            for k in range(KD):
                last = nc.tensor.transpose(bank[4 + 2 * (i % 2) + k // 4][:, (k % 4) * P:(k % 4) * P + n],
                                           xs[i % 2][0:n, k * P:(k + 1) * P], ident[0:n, 0:n])
            last.then_inc(s["xT_psum"], 1)

        for i in range(NT):
            x_transposes(i)
        pe.wait_ge(s["arow"], 1)
        for j in range(4):
            last = nc.tensor.transpose(bank[1][:, j * GP:(j + 1) * GP], arow[:, j, :], ident[0:GP, 0:GP])
        last.then_inc(s["a_psum"], 1)
        pe.wait_ge(s["hT"], 2 * NT)
        pe.wait_ge(s["pcol"], 1)
        pe.wait_ge(s["par"], 1)
        for n, m in enumerate(ORDER):
            pe.wait_ge(w_in_in[m // 4], 16)
            if n >= 2:
                taken(pe, n - 2)
            for k in range(KD):
                wk = w_in[:, m // 4, k, (m % 4) * P:(m % 4 + 1) * P]
                nc.tensor.matmul(bank[2 * (n % 2)][:, 0:HALF], wk, hT[:, k, 0:HALF], start=(k == 0), stop=(k == KD - 1))
                last = nc.tensor.matmul(bank[2 * (n % 2) + 1][:, 0:REST], wk, hT[:, k, HALF:TOK], start=(k == 0), stop=(k == KD - 1))
            last.then_inc(s["proj"], 1)
            if n == 3:
                pe.wait_ge(s["c_in"], 16 * 32)
                for r in range(2):
                    for half in range(2):
                        last = nc.tensor.transpose(bank[7][:, (2 * r + half) * P:(2 * r + half + 1) * P], ctl[:, r, half, :], ident[:])
                last.then_inc(s["c_psum"], 1)
                pe.wait_ge(s["cb_in"], 48)
                for r in range(2):
                    last = nc.tensor.transpose(bank[6][:, r * P:(r + 1) * P], s0l[:, r, :], ident[:])
                last.then_inc(s["s0_psum"], 1)
                for m4 in range(MT):
                    last = nc.tensor.transpose(bank[5][:, m4 * 16:(m4 + 1) * 16], cbl[:, m4 * P:(m4 + 1) * P], ident[0:16, 0:16])
                last.then_inc(s["cb_psum"], 1)
        pe.wait_ge(s["p_ready"], 1)
        pe.wait_ge(s["cz"], 2)
        pe.wait_ge(s["s0_done"], 1)
        for g in range(GP):
            for r in range(2):
                last = nc.tensor.matmul(bank[6][:, g * 32:(g + 1) * 32], p_sb[:, r, g].rearrange("p i h -> p (i h)"),
                                        cz[:, r, g].rearrange("p a h -> p (a h)"), start=(r == 0), stop=(r == 1))
        last.then_inc(s["k_psum"], 1)
        for j in range(8):
            r, q = j // 4, j % 4
            if j >= 2:
                pe.wait_ge(s["wb"], j - 1)
            else:
                pe.wait_ge(s["cbt"], 1)
            for g in range(4):
                last = nc.tensor.transpose(bank[4 + j % 2][:, g * P:(g + 1) * P],
                                           p_sb[:, r, 4 * q + g].rearrange("p i h -> p (i h)"), ident[:])
            last.then_inc(s["pt_psum"], 1)
        pe.wait_ge(s["u_blk_in"], 16 * (CH + 1))
        pe.wait_ge(s["wb"], 8)
        for j in range(8):
            if j >= 2:
                pe.wait_ge(s["v"], j - 1)
            for gg in range(2):
                for r in range(2):
                    for g2 in range(2):
                        gp = 2 * j + gg
                        last = nc.tensor.matmul(bank[4 + j % 2][g2 * NS:(g2 + 1) * NS, (2 * gg + r) * UC:(2 * gg + r + 1) * UC],
                                                wb[:, r, gp, g2 * NS:(g2 + 1) * NS], u_blk[:, 2 * gp + g2, :], start=True, stop=True)
            last.then_inc(s["v_psum"], 1)
        pe.wait_ge(s["conv_z"], MT)
        for m in range(MT):
            last = nc.tensor.transpose(bank[7][0:2 + NDEC, m * P:(m + 1) * P], zg[:, m, NPROMPT:NPROMPT + 2 + NDEC], ident[:])
        last.then_inc(s["crow_psum"], 1)
        pe.wait_ge(s["toep"], 16 * CH)
        pe.wait_ge(s["state_in"], 1)
        pe.wait_ge(s["q_ready"], 1)
        pe.wait_ge(s["v"], 8)
        for j in range(8):
            odd = j % 2
            if j >= 2:
                pe.wait_ge(s["y_blk"], j - 1)
            for i in range(4):
                g = odd + 8 * (j // 2) + 2 * i
                o = bank[4 + odd][0:YC, i * P:(i + 1) * P]
                nc.tensor.matmul(o, u_blk[:, g, 0:YC], toep[:, :, g * GCH:(g + 1) * GCH], start=True, stop=False)
                for r in range(2):
                    last = nc.tensor.matmul(o, s_sb[odd * NS:(odd + 1) * NS, r, g // 2, :],
                                            q_sb[odd * NS:(odd + 1) * NS, r, g // 2].rearrange("p t h -> p (t h)"), start=False, stop=(r == 1))
            last.then_inc(s["y_psum"], 1)
        for j in range(6):
            if j < 2:
                pe.wait_ge(s["y_blk"], 8)
            else:
                pe.wait_ge(s["y_ch"], j - 1)
            for i in range(6 * j, min(6 * j + 6, MT * CH)):
                m, t = i // CH, i % CH
                last = nc.tensor.transpose(bank[4 + j % 2][:, (i - 6 * j) * YC:(i - 6 * j + 1) * YC], y_blk[:, t, m * P:(m + 1) * P], ident[0:YC, 0:YC])
            last.then_inc(s["yt_psum"], 1)
        pe.wait_ge(s["st_ready"], 1)
        nc.tensor.transpose(bank[6][0:2 * GP, 0:P], stout[:, 0:2 * GP], ident[:])
        for r in range(2):
            last = nc.tensor.transpose(bank[6][:, (1 + r) * P:(2 + r) * P], stout[:, 2 * GP + r * P:2 * GP + (r + 1) * P], ident[:])
        last.then_inc(s["st_psum"], 1)
        pe.wait_ge(s["y_gelu"], 1)
        pe.wait_ge(wglu_in, 16)
        yv = gel_v(y_ch)
        for m in range(MT):
            if m >= 2:
                pe.wait_ge(s["glu_sig"], 2 * (m - 1))
            for k in range(MT):
                for h in range(2):
                    last = nc.tensor.matmul(bank[2 * (m % 2) + h][:, 0:4 * YC], w_glu[:, k, m * P:(m + 1) * P],
                                            yv[:, k, 4 * h:4 * h + 4, :].rearrange("p t c -> p (t c)"),
                                            start=(k == 0), stop=(k == MT - 1))
            last.then_inc(s["glu_psum"], 1)

    @block.vector
    def _(dve):
        count = [0]

        def done(ins):
            count[0] += 1
            ins.then_inc(dve_step, 1)
            dve.wait_ge(dve_step, count[0])

        def tt(o, x0, x1, op):
            return nc.vector.tensor_tensor(o, x0, x1, op)

        def ts(o, x0, s1, op0, s2=None, op1=None):
            if op1 is None:
                return nc.vector.tensor_scalar(o, x0, s1, None, op0)
            return nc.vector.tensor_scalar(o, x0, s1, s2, op0, op1)

        def stt(o, x0, sc, x1, op0, op1):
            return nc.vector.scalar_tensor_tensor(out=o, in0=x0, scalar=sc, in1=x1, op0=op0, op1=op1)

        def cmul(o_re, o_im, a_re, a_im, b_re, b_im, t0, t1):
            tt(o_re, a_re, b_re, ALU.mult)
            tt(t0, a_im, b_im, ALU.mult)
            tt(o_im, a_re, b_im, ALU.mult)
            done(tt(t1, a_im, b_re, ALU.mult))
            tt(o_re, o_re, t0, ALU.subtract)
            done(tt(o_im, o_im, t1, ALU.add))

        dve.wait_ge(s["prow_psum"], 1)
        nc.vector.tensor_copy(pcol[:], bank[0][:, 0:36]).then_inc(s["pcol"], 1)
        dve.wait_ge(s["pcol"], 1)
        dve.wait_ge(s["dt_exp"], 1)
        for j in range(2):
            last = tt(arow[:, 2 + j, :].rearrange("g (a n) -> g a n", a=2), arow[:, j, :].rearrange("g (a n) -> g a n", a=2),
                      dtrow[:].unsqueeze(2).to_broadcast([GP, 2, NS]), ALU.mult)
        last.then_inc(s["arow"], 1)

        def take_hT(i):
            n = rows(i)
            dve.wait_ge(s["xT_psum"], i + 1)
            for q in range(2):
                tt(hT[:, 4 * q:4 * q + 4, i * P:i * P + n],
                   bank[4 + 2 * (i % 2) + q][:].rearrange("p (k t) -> p k t", k=4)[:, :, 0:n],
                   pcol[:, NM + 4 * q:NM + 4 * q + 4].unsqueeze(2).to_broadcast([P, 4, n]), ALU.mult).then_inc(s["hT"], 1)

        for i in range(NT):
            n = rows(i)
            dve.wait_ge(s["ss"], i + 1)
            ts(ss[0:n, i:i + 1], ss[0:n, i:i + 1], 1.0 / D, ALU.mult, EPS, ALU.add).then_inc(s["var"], 1)
            dve.wait_ge(s["root"], i + 1)
            refine_rsqrt(nc, done, ss[0:n, NT + i:NT + i + 1], ss[0:n, 2 * NT + i:2 * NT + i + 1], ss[0:n, i:i + 1]).then_inc(s["rstd"], 1)
            if i >= 1:
                take_hT(i - 1)
        take_hT(NT - 1)

        dve.wait_ge(s["a_psum"], 1)
        nc.vector.tensor_copy(par[:].rearrange("p a g -> p (a g)"), bank[1][:, 0:4 * GP]).then_inc(s["par"], 1)
        dve.wait_ge(s["par"], 1)
        mag, rho, kk, r, hh, h2, sn, vs, t0, t1, cs, er, ei, er2, ei2, nr, den, cr, ci = (sm[:, i, :] for i in range(19))
        are, aim, dre, dim = (par[:, i, :] for i in range(4))
        BIG = 12582912.0
        c1 = 6.28125
        c2 = float(math.floor((2 * math.pi - c1) * 2 ** 20) / 2 ** 20)
        c3 = 2 * math.pi - c1 - c2
        done(ts(kk, dim, 1 / (2 * math.pi), ALU.mult))
        done(ts(kk, kk, BIG, ALU.add))
        done(ts(kk, kk, BIG, ALU.subtract))
        done(stt(r, kk, -c1, dim, ALU.mult, ALU.add))
        done(stt(r, kk, -c2, r, ALU.mult, ALU.add))
        done(stt(r, kk, -c3, r, ALU.mult, ALU.add))
        done(ts(hh, r, 0.125, ALU.mult))
        done(tt(h2, hh, hh, ALU.mult))
        done(ts(t0, h2, -1 / 72, ALU.mult, 1.0, ALU.add))
        done(tt(t0, t0, h2, ALU.mult))
        done(ts(t0, t0, -1 / 42, ALU.mult, 1.0, ALU.add))
        done(tt(t0, t0, h2, ALU.mult))
        done(ts(t0, t0, -1 / 20, ALU.mult, 1.0, ALU.add))
        done(tt(t0, t0, h2, ALU.mult))
        done(ts(t0, t0, -1 / 6, ALU.mult, 1.0, ALU.add))
        tt(sn, t0, hh, ALU.mult)
        done(ts(t1, h2, -1 / 56, ALU.mult, 1.0, ALU.add))
        done(tt(t1, t1, h2, ALU.mult))
        done(ts(t1, t1, -1 / 30, ALU.mult, 1.0, ALU.add))
        done(tt(t1, t1, h2, ALU.mult))
        done(ts(t1, t1, -1 / 12, ALU.mult, 1.0, ALU.add))
        done(tt(t1, t1, h2, ALU.mult))
        done(ts(vs, t1, 0.5, ALU.mult))
        for _ in range(3):
            tt(t0, sn, vs, ALU.mult)
            done(tt(t1, sn, sn, ALU.mult))
            done(tt(t0, sn, t0, ALU.subtract))
            ts(vs, t1, 2.0, ALU.mult)
            done(ts(sn, t0, 2.0, ALU.mult))
        done(ts(cs, vs, -1.0, ALU.mult, 1.0, ALU.add))
        dve.wait_ge(s["exps"], 1)
        nc.vector.memset(apow[:, 0, 0, :], 1.0)
        nc.vector.memset(apow[:, 1, 0, :], 0.0)
        tt(apow[:, 0, 1, :], mag, cs, ALU.mult)
        done(tt(apow[:, 1, 1, :], mag, sn, ALU.mult))
        for h in (1, 2, 4):
            hi = [apow[:, c, h, :].unsqueeze(1).to_broadcast([P, h, GP]) for c in range(2)]
            tv = [tmp[:, c * 64:c * 64 + h * GP].rearrange("p (k g) -> p k g", k=h) for c in range(2)]
            cmul(apow[:, 0, h + 1:2 * h + 1, :], apow[:, 1, h + 1:2 * h + 1, :],
                 apow[:, 0, 1:h + 1, :], apow[:, 1, 1:h + 1, :], hi[0], hi[1], tv[0], tv[1])
        nc.vector.tensor_copy(cr, cs).then_inc(s["apow"], 1)
        cmul(er, ei, cs, sn, cs, sn, t0, t1)
        cmul(er2, ei2, er, ei, er, ei, t0, t1)
        cmul(rot[:, 0, :, 0], rot[:, 1, :, 0], er2, ei2, er2, ei2, t0, t1)
        have = 1
        while have < NCH:
            n = min(have, NCH - have)
            hi = [rot[:, c, :, have - 1:have].to_broadcast([P, GP, n]) for c in range(2)]
            tv = [tmp[:, c * GP * 32:c * GP * 32 + GP * n].rearrange("p (g c) -> p g c", g=GP) for c in range(2)]
            cmul(rot[:, 0, :, have:have + n], rot[:, 1, :, have:have + n],
                 rot[:, 0, :, 0:n], rot[:, 1, :, 0:n], hi[0], hi[1], tv[0], tv[1])
            have += n
        ts(nr, apow[:, 0, 1, :], -1.0, ALU.add)
        tt(t0, are, are, ALU.mult)
        done(tt(t1, aim, aim, ALU.mult))
        done(tt(den, t0, t1, ALU.add))
        done(nc.vector.reciprocal(den, den))
        ni = apow[:, 1, 1, :]
        tt(cr, nr, are, ALU.mult)
        tt(t0, ni, aim, ALU.mult)
        tt(ci, ni, are, ALU.mult)
        done(tt(t1, nr, aim, ALU.mult))
        tt(cr, cr, t0, ALU.add)
        done(tt(ci, ci, t1, ALU.subtract))
        tt(cr, cr, den, ALU.mult)
        done(tt(ci, ci, den, ALU.mult))
        tv = [tmp[:, c * GP * GCH:(c + 1) * GP * GCH].rearrange("p (g h) -> p g h", g=GP) for c in range(2)]
        dve.wait_ge(s["b_in"], 64)
        cmul(bbar[:, 0], bbar[:, 1], cr.unsqueeze(2).to_broadcast([P, GP, GCH]), ci.unsqueeze(2).to_broadcast([P, GP, GCH]),
             bt[:, 0], bt[:, 1], tv[0], tv[1])
        dve.wait_ge(s["c_psum"], 1)
        nc.vector.tensor_copy(ct[:].rearrange("p r g h -> p (r g h)"), bank[7][:]).then_inc(s["ct"], 1)
        dve.wait_ge(s["ct"], 1)
        dve.wait_ge(s["cz"], 1)
        for g2 in range(2):
            q = slice(g2 * NS, (g2 + 1) * NS)
            nc.vector.tensor_copy(cz[q, 0, :, g2, :], ct[q, 0])
            last = ts(cz[q, 1, :, g2, :], ct[q, 1], -1.0, ALU.mult)
        last.then_inc(s["cz"], 1)
        dve.wait_ge(s["cb_psum"], 1)
        nc.vector.tensor_copy(cbt[:].rearrange("p m b -> p (m b)"), bank[5][:, 0:MT * 16]).then_inc(s["cbt"], 1)
        for i in range(CH):
            ar = apow[:, 0, CH - 1 - i, :].unsqueeze(2).to_broadcast([P, GP, GCH])
            ai = apow[:, 1, CH - 1 - i, :].unsqueeze(2).to_broadcast([P, GP, GCH])
            cmul(p_sb[:, 0, :, i, :], p_sb[:, 1, :, i, :], bbar[:, 0], bbar[:, 1], ar, ai, tv[0], tv[1])
        nc.vector.memset(t0, 0.0).then_inc(s["p_ready"], 1)

        for m in range(MT):
            n = 8 + m
            taken(dve, 4 + m)
            dve.wait_ge(s["proj"], n + 1)
            tt(zg[:, m, 2:2 + HALF], zg[:, m, 2:2 + HALF], bank[2 * (n % 2)][:, 0:HALF], ALU.mult)
            tt(zg[:, m, 2 + HALF:2 + TOK], zg[:, m, 2 + HALF:2 + TOK], bank[2 * (n % 2) + 1][:, 0:REST], ALU.mult).then_inc(proj_free[n % 2], 1)
        dve.wait_ge(s["cbt"], 1)
        for m in range(MT):
            taken(dve, 8 + m)
            nc.vector.memset(sm[:, 20, 0:1], 0.0).then_inc(s["conv_z"], 1)
            w = [pcol[:, CW + 4 * k + m:CW + 4 * k + m + 1] for k in range(3)]
            acc, accd = tmp[:, 0:NPROMPT], tmp[:, NPROMPT:TOK]
            old = cbt[:, m, :].rearrange("p (b k) -> p k b", k=2)
            ts(acc, zg[:, m, 0:NPROMPT], w[0], ALU.mult)
            done(ts(accd, old[:, 0], w[0], ALU.mult))
            stt(acc, zg[:, m, 1:1 + NPROMPT], w[1], acc, ALU.mult, ALU.add)
            done(stt(accd, old[:, 1], w[1], accd, ALU.mult, ALU.add))
            done(stt(tmp[:, 0:TOK], zg[:, m, 2:2 + TOK], w[2], tmp[:, 0:TOK], ALU.mult, ALU.add))
            taken(dve, 12 + m)
            done(tt(mid["cmix"][:, m, :], mid["cmix"][:, m, :], tmp[:, 0:TOK], ALU.mult))

        dve.wait_ge(s["proj"], 16)
        nc.vector.memset(s_sb[:, :, :, 0:1], 0.0)
        dve.wait_ge(s["s0_psum"], 1)
        for c in range(2):
            nc.vector.tensor_copy(s_sb[:, c, :, DEC0:YC], bank[6][:, c * P:(c + 1) * P].rearrange("p (b g) -> p g b", g=GP))
        nc.vector.memset(t0, 0.0).then_inc(s["s0_done"], 1)
        rho_v = rho_t.rearrange("p (g c) -> p g c", g=GP)
        nc.vector.tensor_copy(rho_v, rho.unsqueeze(2).to_broadcast([P, GP, NCH]))
        done(nc.vector.memset(t1, 0.0))
        done(nc.vector.memset(rho_v[:, :, 0:1], 0.0))
        dve.wait_ge(s["v"], 8)
        wv = [v.rearrange("p (g c) -> p g c", g=GP) for v in wz]
        vr, vi = v_sb[:, 0, :, 0:NCH], v_sb[:, 1, :, 0:NCH]
        tt(wv[0], rot[:, 0], vr, ALU.mult)
        tt(wv[2], rot[:, 1], vi, ALU.mult)
        tt(wv[1], rot[:, 0], vi, ALU.mult)
        done(tt(wv[3], rot[:, 1], vr, ALU.mult))
        tt(wv[0], wv[0], wv[2], ALU.add)
        done(tt(wv[1], wv[1], wv[3], ALU.subtract))
        nc.vector.tensor_tensor_scan(wz[2], rho_t, wz[0], 0.0, ALU.mult, ALU.add)
        done(nc.vector.tensor_tensor_scan(wz[3], rho_t, wz[1], 0.0, ALU.mult, ALU.add))
        sr, si = s_sb[:, 0, :, 1:1 + NCH], s_sb[:, 1, :, 1:1 + NCH]
        tt(sr, rot[:, 0], wv[2], ALU.mult)
        tt(wv[0], rot[:, 1], wv[3], ALU.mult)
        tt(si, rot[:, 0], wv[3], ALU.mult)
        done(tt(wv[1], rot[:, 1], wv[2], ALU.mult))
        tt(sr, sr, wv[0], ALU.subtract)
        tt(si, si, wv[1], ALU.add).then_inc(s["state_in"], 1)
        dve.wait_ge(s["state_in"], 1)
        nc.vector.tensor_copy(stout[:, 0:2 * GP].rearrange("p (r g) -> p r g", r=2), s_sb[:, :, :, NCH])
        so = [stout[:, 2 * GP + c * P:2 * GP + (c + 1) * P].rearrange("p (b g) -> p g b", g=GP) for c in range(2)]
        d0, d1 = s_sb[:, 0, :, DEC0:YC], s_sb[:, 1, :, DEC0:YC]
        ab = [apow[:, c, 1, :].unsqueeze(2).to_broadcast([P, GP, NDEC]) for c in range(2)]
        tv = [tmp[:, c * P:(c + 1) * P].rearrange("p (g b) -> p g b", g=GP) for c in range(4)]
        cmul(tv[2], tv[3], d0, d1, ab[0], ab[1], tv[0], tv[1])
        tt(so[0], tv[2], v_sb[:, 0, :, YC:UC], ALU.add)
        tt(so[1], tv[3], v_sb[:, 1, :, YC:UC], ALU.add).then_inc(s["st_ready"], 1)
        dve.wait_ge(s["crow_psum"], 1)
        dve.wait_ge(s["q_ready"], 1)
        nc.vector.tensor_copy(crow, bank[7][0:2 + NDEC, :]).then_inc(s["crow"], 1)
        dve.wait_ge(s["st_psum"], 1)
        nc.vector.tensor_copy(sttr[0:2 * GP, 0, :], bank[6][0:2 * GP, 0:P])
        nc.vector.tensor_copy(sttr[:, 1:3, :], bank[6][:, P:3 * P].rearrange("p (a c) -> p a c", a=2)).then_inc(s["sttr"], 1)

        dve.wait_ge(s["y_ch"], 6)
        yv, uv = gel_v(y_ch), u_ch
        for m in range(MT):
            last = stt(yv[:, m], uv[:, m], pcol[:, DS + m:DS + m + 1], yv[:, m], ALU.mult, ALU.add)
        done(last)
        done(tt(gel, y_ch, y_ch, ALU.mult))
        done(ts(gel, gel, 0.044715, ALU.mult, 1.0, ALU.add))
        tt(gel, gel, y_ch, ALU.mult).then_inc(s["gel_in"], 1)
        dve.wait_ge(s["gel_sig"], 1)
        tt(y_ch, y_ch, gel, ALU.mult).then_inc(s["y_gelu"], 1)
        dve.wait_ge(s["y_gelu"], 1)
        for m in range(MT):
            dve.wait_ge(s["glu_sig"], 2 * (m + 1))
            tt(mid["ymix"][:, m, 0:NPROMPT].rearrange("p (c t) -> p t c", t=CH), yv[:, m, :, 0:NCH], gel_v(gel)[:, m, :, 0:NCH], ALU.mult)
            tt(mid["ymix"][:, m, NPROMPT:TOK], yv[:, m, 0, DEC0:YC], gel_v(gel)[:, m, 0, DEC0:YC], ALU.mult)

def loop_tables(stack, sb):
    return {
        "rank": sb(stack, "rank", [P, NT, E + 1]),
        "slotval": sb(stack, "slotval", [P, NT, E + 1, 3]),
        "iota_s": sb(stack, "iota_s", [P, P]),
        "pick_row": sb(stack, "pick_row", [96, E, P], BF16),
        "bias": sb(stack, "bias", [96, 3 * FF], BF16),
        "over_i": sb(stack, "over_i", [P, 2, NOVER], I32),
        "over_base": sb(stack, "over_base", [P, NOVER]),
    }


def weight_load(eng, a, keep, mid, e, j):
    if j < 8:
        half, k = j // 4, 2 * (j % 4)
        src = a["w_gate_up"][0].rearrange("e (p k) (u f n) -> e f p (k u) n", p=P, u=2, f=2)[e, half, :, 2 * k:2 * k + 4]
        dst = keep["ring_lo"][:, 2 * j:2 * j + 2, :].rearrange("p k (u n) -> p (k u) n", u=2)
    else:
        k = 2 * (j - 8)
        src = a["w_down"][0].rearrange("e (k p) n -> e p k n", p=P)[e, :, k:k + 2]
        dst = mid["w_out"][:, k:k + 2, :]
    return eng.dma_start(dst, src)


def router(nc, a, scratch, stack, sb, sem, bank, keep, mid, tb):
    def buf(name, shape, dt=F32):
        return sb(stack, name, shape, dt)

    x, ident, pcol = keep["x"], keep["ident"], keep["pcol"]
    NOS, NOC = 20, 24
    ymix, cmix, w_out = mid["ymix"], mid["cmix"], mid["w_out"]
    sq = buf("sq", [P, 2, MT, TOK])
    gffn = buf("gffn", [P, D])
    hf = buf("hf", [P, 2, D])
    hfT = buf("hfT", [P, 2, KD, P])
    w_r = buf("w_r", [P, KD, E])
    b_r = buf("b_r", [1, E])
    ones = buf("ones", [P, P])
    ones_b = buf("ones_b", [P, P], BF16)
    tri = buf("tri", [P, P], BF16)
    trif = sq[:, 0, 0, 0:P]
    ssq = buf("ssq", [P, 3, 2 * NT])
    ss2 = buf("ss2", [P, 3, NT])
    jk = buf("jk", [P, D], BF16)
    lg = buf("lg", [P, NT, E])
    top = buf("top", [P, NT, 8])
    topi = buf("topi", [P, NT, 8], U32)
    topf = buf("topf", [P, NT, 8])
    iota_i = buf("iota_i", [P, P], I32)
    eqk = buf("eqk", [P, NT, E, TOPK])
    mask = buf("mask", [P, NT, E])
    mask_b = buf("mask_b", [P, NT, E], BF16)
    gate = buf("gate", [P, NT, E])
    gsum = buf("gsum", [P, NT])
    cum = buf("cum", [P, NT, E])
    tokv = buf("tokv", [P, NT])
    tok_i = buf("tok_i", [P, NT], I32)
    valid = buf("valid", [P, NT])
    cnt = buf("cnt", [P, 4, E])
    om = buf("om", [P, 2, NOVER, E])
    of = buf("of", [P, 4, NOVER])
    NB = 4
    HB = 3 * FF // NB
    bf = buf("bf", [96, HB])

    s = {n: sem("r_" + n) for n in (
        "consts gffn_in wr_in br_in bias_in sq sums rows scaled mix_var mix_root mm x_new xsq x_var x_root hf hfT_psum hfT logits "
        "sub exp mask rank_psum step pool_step done tabs".split())}
    hf_stored = [sem("r_hf_stored0"), sem("r_hf_stored1")]
    mm_free = [sem("r_mm_free0"), sem("r_mm_free1")]
    keep["landed"] = [sem(f"landed{j}") for j in range(PAIRS)]
    block = stack.enter_context(nc.Block())

    @block.sync
    def _(sp):
        sp.dma_start(w_r[:], a["w_router"][0].rearrange("(p k) e -> p k e", p=P)).then_inc(s["wr_in"], 16)
        sp.dma_start(b_r[:], a["b_router"]).then_inc(s["br_in"], 16)
        sp.dma_start(gffn[:], a["norm_ffn"].to_broadcast([P, D])).then_inc(s["gffn_in"], 16)
        for j in range(8):
            weight_load(sp, a, keep, mid, 0, j).then_inc(keep["landed"][j], 16)
        for i in range(NT):
            sp.wait_ge(s["hf"], i + 1)
            sp.dma_start(scratch["hf"][i * P:i * P + rows(i), :], hf[0:rows(i), i % 2, :]).then_inc(hf_stored[i % 2], 16)
        for c in range(2):
            sp.wait_ge(hf_stored[c], 16 * len(range(c, NT, 2)))

    @block.gpsimd
    def _(pool):
        g = nc.gpsimd
        steps = [0]

        def done(ins):
            steps[0] += 1
            ins.then_inc(s["pool_step"], 1)
            pool.wait_ge(s["pool_step"], steps[0])

        g.iota(iota_i[:], pattern=[[1, P]], base=0, channel_multiplier=0)
        g.iota(tok_i[:], pattern=[[P, NT]], base=0, channel_multiplier=1).then_inc(s["tabs"], 1)
        loads = 0
        bsrc = (a["b_gate_up"][0], a["b_down"][0])
        for h in range(NB):
            lo, hi, split = h * HB, (h + 1) * HB, 2 * FF
            pieces = [(bsrc[0][:, lo:min(hi, split)], 0)] if lo < split else []
            if hi > split:
                pieces.append((bsrc[1][:, max(lo - split, 0):hi - split], max(split - lo, 0)))
            for src, c in pieces:
                for q in range(3):
                    pool.dma_start(bf[q * 32:(q + 1) * 32, c:c + src.shape[1]], src).then_inc(s["bias_in"], 16)
                    loads += 1
            pool.wait_ge(s["bias_in"], 16 * loads)
            out_b = tb["bias"][:, h * HB:(h + 1) * HB]
            done(g.tensor_copy(out_b, bf[:]))
            done(g.tensor_tensor(bf[32:64, :], bf[32:64, :], out_b[32:64, :], ALU.subtract))
            done(g.tensor_tensor(bf[64:96, :], bf[64:96, :], out_b[64:96, :], ALU.subtract))
            done(g.tensor_copy(out_b[32:64, :], bf[32:64, :]))
            done(g.tensor_copy(out_b[64:96, :], bf[64:96, :]))
            done(g.tensor_tensor(bf[64:96, :], bf[64:96, :], out_b[64:96, :], ALU.subtract))
            done(g.tensor_copy(out_b[64:96, :], bf[64:96, :]))

        done(g.memset(tb["pick_row"][:], 0.0))
        for q in range(3):
            v = tb["pick_row"][q * 32:(q + 1) * 32]
            done(g.affine_select(out=v, in_=v, compare_op=ALU.not_equal, fill=1.0, base=0,
                                 pattern=[[-1, E], [0, P]], channel_multiplier=1))

    @block.scalar
    def _(act):
        nc.scalar.activation(sq[:, 0], ymix[:], ACT.Square).then_inc(s["sq"], 1)
        nc.scalar.activation(sq[:, 1], cmix[:], ACT.Square).then_inc(s["sq"], 1)
        act.wait_ge(s["mix_var"], 1)
        nc.scalar.activation(ssq[:, 0], ssq[:, 2], ACT.Sqrt).then_inc(s["mix_root"], 1)
        for i in range(NT):
            n = rows(i)
            act.wait_ge(s["x_new"], 2 * (i + 1))
            nc.scalar.activation(jk[0:n], x[0:n, i, :], ACT.Square, accum_out=ss2[0:n, 2, i:i + 1]).then_inc(s["xsq"], 1)
            act.wait_ge(s["x_var"], i + 1)
            nc.scalar.activation(ss2[0:n, 0, i:i + 1], ss2[0:n, 2, i:i + 1], ACT.Sqrt).then_inc(s["x_root"], 1)
            act.wait_ge(s["hfT_psum"], i + 1)
            for q in range(2):
                last = nc.scalar.activation(hfT[:, i % 2, 4 * q:4 * q + 4, 0:n],
                                            bank[4 + q][:].rearrange("p (k t) -> p k t", k=4)[:, :, 0:n], ACT.Copy)
            last.then_inc(s["hfT"], 1)
        act.wait_ge(s["sub"], 1)
        nc.scalar.activation(gate[:], gate[:], ACT.Exp).then_inc(s["exp"], 1)

    @block.tensor
    def _(pe):
        pe.wait_ge(s["sq"], 2)
        pe.wait_ge(s["consts"], 1)
        for i in range(NT):
            for c in range(2):
                for m in range(MT):
                    last = nc.tensor.matmul(bank[7][0:rows(i), 2 * i + c:2 * i + c + 1], sq[:, c, m, i * P:i * P + rows(i)],
                                            ones[:, 0:1], start=(m == 0), stop=(m == MT - 1))
        last.then_inc(s["sums"], 1)
        pe.wait_ge(s["scaled"], 1)
        pe.wait_ge(keep["wout_in"], 16)

        def route(i):
            n = rows(i)
            pe.wait_ge(s["hf"], i + 1)
            if i >= 1:
                pe.wait_ge(s["hfT"], i)
            for k in range(KD):
                last = nc.tensor.transpose(bank[4 + k // 4][:, (k % 4) * P:(k % 4) * P + n],
                                           hf[0:n, i % 2, k * P:(k + 1) * P], ident[0:n, 0:n])
            last.then_inc(s["hfT_psum"], 1)
            pe.wait_ge(s["hfT"], i + 1)
            o = bank[6][0:n, i * E:(i + 1) * E]
            for k in range(KD):
                nc.tensor.matmul(o, hfT[:, i % 2, k, 0:n], w_r[:, k, :], start=(k == 0), stop=False)
            nc.tensor.matmul(o, ones[0:1, 0:n], b_r[:], start=False, stop=True).then_inc(s["logits"], 1)

        pe.wait_ge(s["wr_in"], 16)
        pe.wait_ge(s["br_in"], 16)
        for i in range(NT):
            n = rows(i)
            for h in range(2):
                if i >= 1:
                    pe.wait_ge(mm_free[h], i)
                for c, src in enumerate((ymix, cmix)):
                    for m in range(MT):
                        last = nc.tensor.matmul(bank[2 * h + c][0:n, :], src[:, m, i * P:i * P + n],
                                                w_out[:, MT * c + m, h * 512:(h + 1) * 512], start=(m == 0), stop=(m == MT - 1))
                last.then_inc(s["mm"], 1)
            if i >= 1:
                route(i - 1)
        route(NT - 1)
        pe.wait_ge(s["mask"], 1)
        pe.wait_ge(s["rows"], 1)
        for i in range(NT):
            for j in range(i):
                nc.tensor.matmul(bank[7][:, i * E:(i + 1) * E], ones_b[:], mask_b[:, j, :], start=(j == 0), stop=False)
            nc.tensor.matmul(bank[7][:, i * E:(i + 1) * E], tri[:], mask_b[:, i, :], start=(i == 0), stop=True)
        for j in range(NT):
            last = nc.tensor.matmul(bank[7][:, NT * E:(NT + 1) * E], ones_b[:], mask_b[:, j, :], start=(j == 0), stop=(j == NT - 1))
        last.then_inc(s["rank_psum"], 1)

    @block.vector
    def _(dve):
        v = nc.vector
        steps = [0]

        def done(ins):
            steps[0] += 1
            ins.then_inc(s["step"], 1)
            dve.wait_ge(s["step"], steps[0])

        v.memset(ones[:], 1.0)
        v.memset(ones_b[:], 1.0)
        v.memset(lg[:], 0.0).then_inc(s["consts"], 1)
        dve.wait_ge(s["sums"], 1)
        v.memset(ssq[:], 1.0)
        done(v.memset(ss2[:], 1.0))
        for i in range(NT):
            n = rows(i)
            last = v.tensor_scalar(ssq[0:n, 2, 2 * i:2 * i + 2], bank[7][0:n, 2 * i:2 * i + 2], 1.0 / W, EPS, ALU.mult, ALU.add)
        last.then_inc(s["mix_var"], 1)
        dve.wait_ge(s["mix_root"], 1)
        refine_rsqrt(nc, done, ssq[:, 0], ssq[:, 1], ssq[:, 2]).then_inc(s["rows"], 1)
        dve.wait_ge(s["rows"], 1)
        for m in range(MT):
            v.tensor_scalar(ymix[:, m, :], ymix[:, m, :], pcol[:, NOS + m:NOS + m + 1], None, ALU.mult)
            last = v.tensor_scalar(cmix[:, m, :], cmix[:, m, :], pcol[:, NOC + m:NOC + m + 1], None, ALU.mult)
        last.then_inc(s["scaled"], 1)
        dve.wait_ge(s["gffn_in"], 16)
        for i in range(NT):
            n = rows(i)
            for h in range(2):
                dve.wait_ge(s["mm"], 2 * i + h + 1)
                xv = x[0:n, i, h * 512:(h + 1) * 512]
                done(v.scalar_tensor_tensor(out=xv, in0=bank[2 * h][0:n, :], scalar=ssq[0:n, 0, 2 * i:2 * i + 1], in1=xv, op0=ALU.mult, op1=ALU.add))
                done(v.scalar_tensor_tensor(out=xv, in0=bank[2 * h + 1][0:n, :], scalar=ssq[0:n, 0, 2 * i + 1:2 * i + 2], in1=xv, op0=ALU.mult, op1=ALU.add))
                dve.sem_inc(mm_free[h], 1)
                dve.sem_inc(s["x_new"], 1)
            dve.wait_ge(s["xsq"], i + 1)
            v.tensor_scalar(ss2[0:n, 2, i:i + 1], ss2[0:n, 2, i:i + 1], 1.0 / D, EPS, ALU.mult, ALU.add).then_inc(s["x_var"], 1)
            dve.wait_ge(s["x_root"], i + 1)
            done(refine_rsqrt(nc, done, ss2[0:n, 0, i:i + 1], ss2[0:n, 1, i:i + 1], ss2[0:n, 2, i:i + 1]))
            if i >= 2:
                dve.wait_ge(s["hfT_psum"], i - 1)
                dve.wait_ge(hf_stored[i % 2], 16 * (i // 2))
            v.scalar_tensor_tensor(out=hf[0:n, i % 2, :].rearrange("t (k p) -> t p k", p=P), in0=x[0:n, i, :].rearrange("t (p k) -> t p k", p=P),
                                   scalar=ss2[0:n, 0, i:i + 1], in1=gffn[0:n, :].rearrange("t (p k) -> t p k", p=P),
                                   op0=ALU.mult, op1=ALU.mult).then_inc(s["hf"], 1)
        dve.wait_ge(s["tabs"], 1)
        v.tensor_copy(tb["iota_s"][:], iota_i[:])
        done(v.tensor_copy(tokv[:], tok_i[:]))
        v.tensor_scalar(valid[:], tokv[:], float(TOK), None, ALU.is_lt)
        v.tensor_scalar(tri[:], tb["iota_s"][:], tokv[:, 0:1], None, ALU.is_gt)
        dve.wait_ge(s["logits"], NT)
        for i in range(NT):
            done(v.tensor_copy(lg[0:rows(i), i, :], bank[6][0:rows(i), i * E:(i + 1) * E]))
            done(v.max(out=top[:, i, :], in_=lg[:, i, :]))
            done(v.max_index(out=topi[:, i, :], in_max=top[:, i, :], in_values=lg[:, i, :]))
        done(v.tensor_copy(topf[:], topi[:]))
        v.tensor_tensor(gate[:], lg[:], top[:, :, 0:1].to_broadcast([P, NT, E]), ALU.subtract).then_inc(s["sub"], 1)
        iota_e = tb["iota_s"][:, 0:E]
        for i in range(NT):
            last = v.tensor_tensor(eqk[:, i], iota_e.unsqueeze(2).to_broadcast([P, E, TOPK]),
                                   topf[:, i, 0:TOPK].unsqueeze(1).to_broadcast([P, E, TOPK]), ALU.is_equal)
        done(last)
        done(v.tensor_reduce(mask[:], eqk[:], AX_X, ALU.add))
        done(v.tensor_tensor(mask[:], mask[:], valid[:].unsqueeze(2).to_broadcast([P, NT, E]), ALU.mult))
        v.tensor_copy(mask_b[:], mask[:]).then_inc(s["mask"], 1)
        dve.wait_ge(s["exp"], 1)
        done(v.tensor_tensor(gate[:], gate[:], mask[:], ALU.mult))
        done(v.tensor_reduce(gsum[:], gate[:], AX_X, ALU.add))
        done(v.tensor_scalar(gsum[:], gsum[:], 1e-30, None, ALU.max))
        done(v.reciprocal(gsum[:], gsum[:]))
        rank, slotval = tb["rank"], tb["slotval"]
        v.memset(rank[:], -1.0)
        done(v.memset(slotval[:], 0.0))
        v.tensor_tensor(slotval[:, :, 0:E, 2], gate[:], gsum[:].unsqueeze(2).to_broadcast([P, NT, E]), ALU.mult)
        v.tensor_copy(slotval[:, :, 0:E, 0], tokv[:].unsqueeze(2).to_broadcast([P, NT, E]))
        for i in range(NT):
            last = v.tensor_tensor_scan(cum[:, i, :], ones[:, 0:E], mask[:, i, :], 0.0, ALU.mult, ALU.add)
        done(last)
        done(v.tensor_scalar(tokv[:], tokv[:], 4.0, None, ALU.mult))
        v.tensor_tensor(slotval[:, :, 0:E, 1], cum[:], tokv[:].unsqueeze(2).to_broadcast([P, NT, E]), ALU.add)
        done(v.memset(cnt[:, 3, :], 0.0))
        v.tensor_scalar(slotval[:, :, :, 0], slotval[:, :, :, 0], -MISS, None, ALU.add)
        v.tensor_scalar(slotval[:, :, :, 1], slotval[:, :, :, 1], -1.0 - MISS, None, ALU.add)
        dve.wait_ge(s["rank_psum"], 1)
        done(v.tensor_scalar(cum[:], bank[7][:, 0:NT * E].rearrange("p (i e) -> p i e", i=NT), 1.0, None, ALU.add))
        done(v.tensor_tensor(cum[:], cum[:], mask[:], ALU.mult))
        v.tensor_scalar(rank[:, :, 0:E], cum[:], -1.0, None, ALU.add)
        c, extra, upto = cnt[:, 0, :], cnt[:, 1, :], cnt[:, 2, :]
        done(v.tensor_copy(c, bank[7][:, NT * E:(NT + 1) * E]))
        done(v.tensor_scalar(extra, c, float(P), None, ALU.is_gt))
        for t in range(2, NT):
            done(v.scalar_tensor_tensor(out=extra, in0=c, scalar=float(t * P), in1=extra, op0=ALU.is_gt, op1=ALU.add))
        done(v.tensor_tensor_scan(upto, ones[:, 0:E], extra, 0.0, ALU.mult, ALU.add))
        b_no = tb["iota_s"][:, 0:NOVER]
        done(v.tensor_tensor(om[:, 0], upto.unsqueeze(1).to_broadcast([P, NOVER, E]),
                             b_no.unsqueeze(2).to_broadcast([P, NOVER, E]), ALU.is_le))
        v.tensor_reduce(of[:, 0, :], om[:, 0], AX_X, ALU.add)
        done(v.tensor_tensor(om[:, 1], om[:, 0], extra.unsqueeze(1).to_broadcast([P, NOVER, E]), ALU.mult))
        done(v.tensor_reduce(of[:, 1, :], om[:, 1], AX_X, ALU.add))
        done(v.tensor_tensor(of[:, 2, :], b_no, of[:, 1, :], ALU.subtract))
        v.tensor_scalar(tb["over_base"][:], of[:, 2, :], 1.0, float(P), ALU.add, ALU.mult)
        v.tensor_scalar(tb["over_i"][:, 0, :], of[:, 0, :], float(E - 1), None, ALU.min)
        v.tensor_tensor(tb["over_i"][:, 1, :], upto[:, E - 1:E].to_broadcast([P, NOVER]), b_no, ALU.is_gt).then_inc(s["done"], 1)
        dve.wait_ge(s["done"], 1)

def experts(nc, a, scratch, stack, sb, sem, bank, keep, mid, tb, landed):
    def buf(name, shape, dt=F32):
        return sb(stack, name, shape, dt)

    ident = keep["ident"]
    ring_lo, ring_hi = keep["ring_lo"], mid["w_out"]
    SPLIT = 4
    w_hi = buf("w_hi", [P, SPLIT, 1024], F32R)
    w_lo = buf("w_lo", [P, SPLIT, 1024], F32R)
    x_hi = buf("x_hi", [P, KD, P], F32R)
    x_lo = buf("x_lo", [P, KD, P], F32R)
    h_hi = buf("h_hi", [P, KD, P], F32R)
    h_lo = buf("h_lo", [P, KD, P], F32R)
    yflat = mid["ymix"][:, :, :].rearrange("p m t -> p (m t)")
    cflat = mid["cmix"][:, :, :].rearrange("p m t -> p (m t)")
    xg, yo = yflat[:, 0:D], yflat[:, D:2 * D]
    g_sb = cflat[:, 0:1024].rearrange("p (h n) -> p h n", h=2)
    u_sb = cflat[:, 1024:2048].rearrange("p (h n) -> p h n", h=2)
    h_sb = buf("h_sb", [P, 2, 512])
    onehot = buf("onehot", [P, NT, P])
    idx_next = buf("idx_next", [P, 2], I32)
    gate_next = buf("gate_next", [P, 1])
    row_cur = buf("row_cur", [P, 1], I32)
    gate_cur = buf("gate_cur", [P, 1])
    zero = buf("zero", [P, 1])

    s = {n: sem("e_" + n) for n in (
        "w_hi w_lo w_used onehot sel_psum idx x_in xT_psum x_hi x_lo gu_psum gu_read g_min sig h hT_psum h_hi h_lo "
        "y_psum y_sb y_stored y_out y_free step curd turns".split())}
    block = stack.enter_context(nc.Block())

    def unit(j):
        return ring_lo[:, j, :] if j < 16 else ring_hi[:, j - 16, :]

    def overflow(eng, work):
        with eng.Fori(0, NOVER) as b:
            active = eng.value_load(tb["over_i"][0:1, 1, bass.ds(b, 1)], min_val=0, max_val=1)
            with eng.If(active > 0):
                work(b)

    def over_expert(eng, b):
        return eng.value_load(tb["over_i"][0:1, 0, bass.ds(b, 1)], min_val=0, max_val=E - 1)


    @block.sync
    def _(sp):
        for j in range(8, PAIRS):
            weight_load(sp, a, keep, mid, 0, j).then_inc(landed[j], 16)

        def load(e, q):
            for j in range(PAIRS):
                sp.wait_ge(s["w_lo"], UNITS * q + (2 * j + 2 - UNITS))
                weight_load(sp, a, keep, mid, e, j).then_inc(landed[j], 16)

        with sp.Fori(1, E) as e:
            load(e, e)
        overflow(sp, lambda b: load(over_expert(sp, b), b + E))

    @block.gpsimd
    def _(pool):
        nc.gpsimd.memset(xg, 0.0).then_inc(s["turns"], 1)
        pool.sem_inc(s["y_out"], 1)
        pool.wait_ge(s["turns"], 1)

        def gather(q):
            pool.wait_ge(s["idx"], q + 1)
            pool.sem_inc(s["turns"], 1)
            nc.gpsimd.indirect_dma_start(xg, None, scratch["hf"], bass.IndirectOffsetOnAxis(ap=idx_next[:, 0:1].bitcast(U32), axis=0),
                                         bounds_check=TOK - 1, oob_is_err=False).then_inc(s["x_in"], 16)

        def scatter(q):
            pool.wait_ge(s["y_sb"], q + 1)
            pool.sem_inc(s["turns"], 1)
            nc.gpsimd.indirect_dma_start(scratch["picked"], bass.IndirectOffsetOnAxis(ap=row_cur[:, 0:1].bitcast(U32), axis=0), yo, None,
                                         bounds_check=TOK * TOPK - 1, oob_is_err=False).then_inc(s["y_stored"], 16)
            pool.wait_ge(s["y_stored"], 16 * q + 16)
            pool.sem_inc(s["y_out"], 1)

        def over(b):
            gather(b + E)
            scatter(b + E)

        gather(0)
        with pool.Fori(0, E - 1) as e:
            gather(e + 1)
            scatter(e)
        scatter(E - 1)
        overflow(pool, over)

    @block.scalar
    def _(act):
        def split(q, j, first=False):
            if j % 2 == 0:
                act.wait_ge(landed[j // 2], 16 * q + 16)
            if not first:
                act.wait_ge(s["w_used"], UNITS * q + (j + 1 - SPLIT))
            nc.scalar.activation(w_hi[:, j % SPLIT, :], unit(j), ACT.Copy).then_inc(s["w_hi"], 1)

        def take_x(q):
            act.wait_ge(s["xT_psum"], q + 1)
            for h in range(2):
                nc.scalar.activation(x_hi[:, 4 * h:4 * h + 4, :].rearrange("p k t -> p (k t)"), bank[h][:], ACT.Copy).then_inc(s["x_hi"], 1)

        def sigmoid(q, half):
            act.wait_ge(s["g_min"], 2 * q + half + 1)
            nc.scalar.activation(h_sb[:, half, :], g_sb[:, half, :], ACT.Sigmoid, scale=ALPHA).then_inc(s["sig"], 1)

        def take_h(q, half):
            act.wait_ge(s["hT_psum"], 2 * q + half + 1)
            nc.scalar.activation(h_hi[:, 4 * half:4 * half + 4, :].rearrange("p k t -> p (k t)"), bank[6 + half][:], ACT.Copy).then_inc(s["h_hi"], 1)

        def body(q, nxt):
            for j in range(SPLIT, UNITS):
                split(q, j)
                if j == 11:
                    sigmoid(q, 0)
                elif j == 14:
                    take_h(q, 0)
                elif j == 19:
                    sigmoid(q, 1)
                elif j == 21:
                    take_h(q, 1)
            if nxt:
                take_x(q + 1)
                for j in range(SPLIT):
                    split(q + 1, j)
            act.wait_ge(s["y_psum"], q + 1)
            act.wait_ge(s["y_out"], q + 1)
            act.wait_ge(s["curd"], q + 1)
            for h in range(2):
                last = nc.scalar.activation(yo[:, h * 512:(h + 1) * 512], bank[4 + h][:], ACT.Copy, scale=gate_cur[:, 0:1])
            last.then_inc(s["y_sb"], 1)
            act.wait_ge(s["y_sb"], q + 1)
            act.sem_inc(s["y_free"], 1)

        def over(b):
            take_x(b + E)
            for j in range(SPLIT):
                split(b + E, j)
            body(b + E, False)

        act.sem_inc(s["y_free"], 1)
        for j in range(SPLIT):
            split(0, j, first=True)
        take_x(0)
        with act.Fori(0, E - 1) as e:
            body(e, True)
        body(E - 1, False)
        overflow(act, over)

    @block.tensor
    def _(pe):
        def select(e, q):
            pe.wait_ge(s["onehot"], q + 1)
            for i in range(NT):
                last = nc.tensor.matmul(bank[6][:, 0:3], onehot[:, i, :], tb["slotval"][:, i, bass.ds(e, 1), :].rearrange("p a c -> p (a c)"),
                                        start=(i == 0), stop=(i == NT - 1))
            last.then_inc(s["sel_psum"], 1)

        def x_transposes(q):
            pe.wait_ge(s["x_in"], 16 * q + 16)
            for k in range(KD):
                last = nc.tensor.transpose(bank[k // 4][:, (k % 4) * P:(k % 4 + 1) * P], xg[:, k * P:(k + 1) * P], ident[:])
            last.then_inc(s["xT_psum"], 1)

        def h_transposes(q, half):
            pe.wait_ge(s["h"], 2 * q + half + 1)
            for k in range(4):
                last = nc.tensor.transpose(bank[6 + half][:, k * P:(k + 1) * P], h_sb[:, half, k * P:(k + 1) * P], ident[:])
            last.then_inc(s["hT_psum"], 1)

        def products(q, j):
            v_hi, v_lo, k, b = (x_hi, x_lo, j % 8, 2 * (j // 8)) if j < 16 else (h_hi, h_lo, j - 16, 4)
            pe.wait_ge(s["w_lo"], UNITS * q + (j + 1))
            for first, (v, w) in ((True, (v_hi, w_hi)), (False, (v_hi, w_lo)), (False, (v_lo, w_hi))):
                for u in range(2):
                    last = nc.tensor.matmul(bank[b + u][:], v[:, k, :], w[:, j % SPLIT, u * 512:(u + 1) * 512],
                                            start=(k == 0 and first), stop=False)
            last.then_inc(s["w_used"], 1)

        def add_bias(e, b, cols, done):
            for u in range(2):
                last = nc.tensor.matmul(bank[b + u][:], tb["pick_row"][:, bass.ds(e, 1), :].rearrange("p a c -> p (a c)"),
                                        tb["bias"][:, cols[u]:cols[u] + 512], start=False, stop=True)
            last.then_inc(done, 1)

        def body(q, e, nxt):
            pe.wait_ge(s["x_lo"], q + 1)
            for j in range(UNITS):
                if j in (0, 8):
                    pe.wait_ge(s["gu_read"], 2 * q + j // 8 + 1)
                if j == 8 and nxt:
                    select(e + 1, q + 1)
                if j == 12:
                    if nxt:
                        pe.wait_ge(s["idx"], q + 2)
                    h_transposes(q, 0)
                if j == 16:
                    pe.wait_ge(s["h_lo"], 2 * q + 1)
                    pe.wait_ge(s["y_free"], q + 1)
                if j == 19:
                    h_transposes(q, 1)
                if j == 20:
                    if nxt:
                        pe.wait_ge(s["gu_read"], 2 * q + 3)
                        x_transposes(q + 1)
                    pe.wait_ge(s["h_lo"], 2 * q + 2)
                products(q, j)
                if j in (7, 15):
                    half = j // 8
                    add_bias(e, 2 * half, (half * 512, FF + half * 512), s["gu_psum"])
            add_bias(e, 4, (2 * FF, 2 * FF + 512), s["y_psum"])

        def over(b):
            e = over_expert(pe, b)
            select(e, b + E)
            x_transposes(b + E)
            body(b + E, e, False)

        select(0, 0)
        x_transposes(0)
        with pe.Fori(0, E - 1) as e:
            body(e, e, True)
        body(E - 1, E - 1, False)
        overflow(pe, over)

    @block.vector
    def _(dve):
        v = nc.vector

        def pick(e, base):
            v.scalar_tensor_tensor(out=onehot[:], in0=tb["rank"][:, :, bass.ds(e, 1)].to_broadcast([P, NT, P]), scalar=base,
                                   in1=tb["iota_s"][:].unsqueeze(1).to_broadcast([P, NT, P]),
                                   op0=ALU.subtract, op1=ALU.is_equal).then_inc(s["onehot"], 1)

        def take_slots(q):
            dve.wait_ge(s["sel_psum"], q + 1)
            v.tensor_copy(gate_next[:], bank[6][:, 2:3])
            v.tensor_scalar(idx_next[:], bank[6][:, 0:2], MISS, None, ALU.add).then_inc(s["idx"], 1)

        def keep_slots(q):
            dve.wait_ge(s["y_out"], q + 1)
            v.tensor_copy(row_cur[:], idx_next[:, 1:2])
            v.tensor_copy(gate_cur[:], gate_next[:]).then_inc(s["curd"], 1)
            dve.wait_ge(s["curd"], q + 1)

        def split(q, j):
            dve.wait_ge(s["w_hi"], UNITS * q + (j + 1))
            v.tensor_tensor(w_lo[:, j % SPLIT, :], unit(j), w_hi[:, j % SPLIT, :].bitcast(F32), ALU.subtract).then_inc(s["w_lo"], 1)

        def take_x(q):
            for h in range(2):
                dve.wait_ge(s["x_hi"], 2 * q + h + 1)
                c = slice(4 * h, 4 * h + 4)
                last = v.tensor_tensor(x_lo[:, c, :].rearrange("p k t -> p (k t)"), bank[h][:],
                                       x_hi[:, c, :].rearrange("p k t -> p (k t)").bitcast(F32), ALU.subtract)
            last.then_inc(s["x_lo"], 1)

        def take_h(q, half):
            dve.wait_ge(s["h_hi"], 2 * q + half + 1)
            c = slice(4 * half, 4 * half + 4)
            v.tensor_tensor(h_lo[:, c, :].rearrange("p k t -> p (k t)"), bank[6 + half][:],
                            h_hi[:, c, :].rearrange("p k t -> p (k t)").bitcast(F32), ALU.subtract).then_inc(s["h_lo"], 1)

        def swiglu(q, half):
            dve.wait_ge(s["gu_psum"], 2 * q + half + 1)
            g, u = g_sb[:, half, :], u_sb[:, half, :]
            v.tensor_scalar(g, bank[2 * half][:], LIMIT, None, ALU.min).then_inc(s["g_min"], 1)
            v.tensor_scalar(u, bank[2 * half + 1][:], LIMIT, -LIMIT, ALU.min, ALU.max).then_inc(s["gu_read"], 1)
            dve.wait_ge(s["gu_read"], 2 * q + half + 3)
            dve.wait_ge(s["g_min"], 2 * q + half + 1)
            v.scalar_tensor_tensor(out=u, in0=u, scalar=1.0, in1=g, op0=ALU.add, op1=ALU.mult).then_inc(s["step"], 1)
            dve.wait_ge(s["step"], 2 * q + half + 1)
            dve.wait_ge(s["sig"], 2 * q + half + 1)
            v.tensor_tensor(h_sb[:, half, :], u, h_sb[:, half, :], ALU.mult).then_inc(s["h"], 1)

        def body(q, e, nxt):
            if nxt:
                pick(e + 1, zero[:, 0:1])
            for j in range(SPLIT, UNITS):
                split(q, j)
                if j == 11:
                    swiglu(q, 0)
                    keep_slots(q)
                    if nxt:
                        take_slots(q + 1)
                elif j == 14:
                    take_h(q, 0)
                elif j == 19:
                    swiglu(q, 1)
                elif j == 21:
                    take_h(q, 1)
            if nxt:
                take_x(q + 1)
                for j in range(SPLIT):
                    split(q + 1, j)

        def over(b):
            pick(over_expert(dve, b), tb["over_base"][:, bass.ds(b, 1)])
            take_slots(b + E)
            take_x(b + E)
            for j in range(SPLIT):
                split(b + E, j)
            body(b + E, 0, False)

        v.memset(zero[:], 0.0).then_inc(s["gu_read"], 2)
        dve.wait_ge(s["gu_read"], 2)
        pick(0, zero[:, 0:1])
        take_slots(0)
        for j in range(SPLIT):
            split(0, j)
        take_x(0)
        with dve.Fori(0, E - 1) as e:
            body(e, e, True)
        body(E - 1, E - 1, False)
        overflow(dve, over)


def combine(nc, a, out, scratch, stack, sb, sem, keep):
    x = keep["x"]
    ring = keep["ring_lo"][:, :, :].rearrange("p (b k) n -> p b k n", k=TOPK)
    NB = 4
    gfin = sb(stack, "gfin", [P, D])
    ssf = sb(stack, "ssf", [P, 3, NT])
    jf = sb(stack, "jf", [P, D])
    of = sb(stack, "of_fin", [P, NT, D])
    g_in, summed, sq, var, root, fin, stored, step = (sem("c_" + n) for n in "g_in summed sq var root fin stored step".split())
    rows_in = [sem(f"c_rows{i}") for i in range(NB)]
    block = stack.enter_context(nc.Block())
    picked = scratch["picked"].rearrange("(t k) n -> t k n", k=TOPK)
    outs = 1 + (NT - 2) + 2

    @block.sync
    def _(sp):
        for i in range(NT):
            if i >= NB:
                sp.wait_ge(summed, i - NB + 1)
            sp.dma_start(ring[0:rows(i), i % NB], picked[i * P:i * P + rows(i)]).then_inc(rows_in[i % NB], 16)
            if i == 0:
                sp.dma_start(gfin[:], a["norm_final"].unsqueeze(0).to_broadcast([P, D])).then_inc(g_in, 16)
        y_p = out["y_p"][0]
        for i in range(NT):
            sp.wait_ge(fin, i + 1)
            if i == 0:
                sp.dma_start(y_p[0:P - NMETA, :], of[NMETA:P, 0, :]).then_inc(stored, 16)
            elif i < NT - 1:
                sp.dma_start(y_p[i * P - NMETA:(i + 1) * P - NMETA, :], of[:, i, :]).then_inc(stored, 16)
            else:
                n = LAST - NDEC
                sp.dma_start(y_p[SEQ - n:SEQ, :], of[0:n, i, :]).then_inc(stored, 16)
                sp.dma_start(out["y_s"][:, 0, :], of[n:LAST, i, :]).then_inc(stored, 16)
        sp.wait_ge(stored, 16 * outs)

    @block.scalar
    def _(act):
        for i in range(NT):
            n = rows(i)
            act.wait_ge(summed, i + 1)
            nc.scalar.activation(jf[0:n], x[0:n, i, :], ACT.Square, accum_out=ssf[0:n, 2, i:i + 1]).then_inc(sq, 1)
            act.wait_ge(var, i + 1)
            nc.scalar.activation(ssf[0:n, 0, i:i + 1], ssf[0:n, 2, i:i + 1], ACT.Sqrt).then_inc(root, 1)

    @block.vector
    def _(dve):
        v = nc.vector
        count = [0]

        def done(ins):
            count[0] += 1
            ins.then_inc(step, 1)
            dve.wait_ge(step, count[0])

        def finish(i):
            n = rows(i)
            dve.wait_ge(sq, i + 1)
            v.tensor_scalar(ssf[0:n, 2, i:i + 1], ssf[0:n, 2, i:i + 1], 1.0 / D, EPS, ALU.mult, ALU.add).then_inc(var, 1)
            dve.wait_ge(root, i + 1)
            done(refine_rsqrt(nc, done, ssf[0:n, 0, i:i + 1], ssf[0:n, 1, i:i + 1], ssf[0:n, 2, i:i + 1]))
            v.scalar_tensor_tensor(out=of[0:n, i, :], in0=x[0:n, i, :], scalar=ssf[0:n, 0, i:i + 1], in1=gfin[0:n, :],
                                   op0=ALU.mult, op1=ALU.mult).then_inc(fin, 1)

        dve.wait_ge(g_in, 16)
        for i in range(NT):
            n = rows(i)
            dve.wait_ge(rows_in[i % NB], 16 * (i // NB + 1))
            r = ring[0:n, i % NB]
            v.tensor_tensor(r[:, 0], r[:, 0], r[:, 1], ALU.add)
            done(v.tensor_tensor(r[:, 2], r[:, 2], r[:, 3], ALU.add))
            done(v.tensor_tensor(r[:, 0], r[:, 0], r[:, 2], ALU.add))
            v.tensor_tensor(x[0:n, i, :], x[0:n, i, :], r[:, 0], ALU.add).then_inc(summed, 1)
            if i >= 1:
                finish(i - 1)
        finish(NT - 1)


_INS = ["x_prompt", "x_sample", "state_ssm_re", "state_ssm_im", "state_conv", "meta_tokens", "norm_mix", "w_in",
        "ssm_a_re", "ssm_a_im", "ssm_log_dt", "ssm_b_re", "ssm_b_im", "ssm_c_re", "ssm_c_im", "ssm_d", "w_glu", "b_glu",
        "conv_w", "norm_out_ssm", "norm_out_conv", "w_out", "norm_ffn", "w_router", "b_router", "w_gate_up",
        "b_gate_up", "w_down", "b_down", "norm_final"]
_OUTS = [("y_p", (1, SEQ, D)), ("y_s", (NDEC, 1, D)), ("re_p", (1, 1, GROUPS, NS)), ("im_p", (1, 1, GROUPS, NS)),
         ("conv_p", (1, 1, 2, W)), ("re_s", (1, NDEC, GROUPS, NS)), ("im_s", (1, NDEC, GROUPS, NS)), ("conv_s", (1, NDEC, 2, W))]


def kernel(**inputs):
    import numpy as np
    import concourse.bacc as bacc
    from concourse.bass_utils import run_bass_kernel_spmd

    nc = bacc.Bacc("TRN2", target_bir_lowering=False, num_devices=1)
    arrays, a = {}, {}
    for name in _INS:
        v = np.ascontiguousarray(inputs[name])
        arrays[f"in_{name}"] = v
        a[name] = nc.dram_tensor(f"in_{name}", v.shape, mybir.dt.from_np(v.dtype), kind="ExternalInput").ap()
    out = {n: nc.dram_tensor(f"out_{n}", shape, F32, kind="ExternalOutput").ap() for n, shape in _OUTS}
    hybrid_step(nc, a, out)
    r = run_bass_kernel_spmd(nc, [arrays], core_ids=[0])
    return tuple(r.results[0][f"out_{n}"] for n, _ in _OUTS)
```

```python
import math
from contextlib import ExitStack

import concourse.bass as bass
from concourse import mybir

F32 = mybir.dt.float32
F32R = mybir.dt.float32r
BF16 = mybir.dt.bfloat16
I32 = mybir.dt.int32
U32 = mybir.dt.uint32
ALU = mybir.AluOpType
ACT = mybir.ActivationFunctionType
AX_X = mybir.AxisListType.X

P = 128
D = 1024
KD = D // P
NMETA, SEQ, NDEC = 16, 512, 8
NPROMPT = NMETA + SEQ
TOK = NPROMPT + NDEC
NT = (TOK + P - 1) // P
LAST = TOK - (NT - 1) * P
W = 512
MT = W // P
GROUPS, GCH, NS = 32, 16, 64
GP = GROUPS // 2
CH = 8
NCH = NPROMPT // CH
YC = NCH + 1 + NDEC
DEC0 = NCH + 1
UC = YC + NDEC
E = 32
TOPK = 4
FF = D
EPS = 1e-5
LIMIT = 7.0
ALPHA = 1.702
GROUP = 4
NOVER = ((TOK * TOPK + E * (P - 1)) // P - E + GROUP) // GROUP * GROUP
UNITS = 24
PAIRS = UNITS // 2
MISS = 4096.0
HALF = 264
REST = TOK - HALF


def rows(i):
    return P if i < NT - 1 else LAST


def refine_rsqrt(nc, done, r, t, v):
    done(nc.vector.reciprocal(r, r))
    done(nc.vector.tensor_tensor(t, r, r, ALU.mult))
    done(nc.vector.tensor_tensor(t, t, v, ALU.mult))
    done(nc.vector.tensor_scalar(t, t, -0.5, 1.5, ALU.mult, ALU.add))
    return nc.vector.tensor_tensor(r, r, t, ALU.mult)


def hybrid_step(nc, a, out):
    scratch = {
        "u": nc.dram_tensor("u_shuffle", [W, CH, YC], F32).ap(),
        "hf": nc.dram_tensor("ffn_in", [TOK, D], F32).ap(),
        "picked": nc.dram_tensor("expert_rows", [TOK * TOPK, D], F32).ap(),
    }
    with ExitStack() as ctx:
        def sb(stack, name, shape, dt=F32):
            return stack.enter_context(nc.sbuf_tensor(name, shape, dt))

        def sem(name):
            return ctx.enter_context(nc.semaphore(name))

        bank = [ctx.enter_context(nc.psum_tensor(f"bank{i}", [P, 512], F32)) for i in range(8)]
        keep = {
            "x": sb(ctx, "x", [P, NT, D]),
            "ident": sb(ctx, "ident", [P, P]),
            "ones": sb(ctx, "ones_col", [P, 1]),
            "conv_ss": sb(ctx, "conv_ss", [P, NT]),
            "pcol": sb(ctx, "pcol", [P, 36]),
            "ring_lo": sb(ctx, "ring_lo", [P, 16, 1024]),
        }
        with ExitStack() as st:
            mid = {
                "ymix": sb(st, "ymix", [P, MT, TOK]),
                "cmix": sb(st, "cmix", [P, MT, TOK]),
                "w_out": sb(st, "w_out", [P, KD, D]),
            }
            with ExitStack() as s1:
                mixer(nc, a, out, scratch, s1, sb, sem, bank, keep, mid)
            with ExitStack() as s2:
                tables = loop_tables(s2, sb)
                with ExitStack() as s3:
                    router(nc, a, scratch, s3, sb, sem, bank, keep, mid, tables)
                landed = keep["landed"]
                experts(nc, a, scratch, s2, sb, sem, bank, keep, mid, tables, landed)
        with ExitStack() as s4:
            combine(nc, a, out, scratch, s4, sb, sem, keep)


def mixer(nc, a, out, scratch, stack, sb, sem, bank, keep, mid):
    def buf(name, shape, dt=F32):
        return sb(stack, name, shape, dt)

    x, ident, pcol = keep["x"], keep["ident"], keep["pcol"]
    flat = keep["ring_lo"][:, :, :].rearrange("p a b -> p (a b)")
    BLK = KD * W
    w_in = flat.rearrange("p (blk k n) -> p blk k n", blk=4, k=KD)
    toep = flat[:, 0:CH * W].rearrange("p (t n) -> p t n", t=CH)
    ZN = GP * NCH
    wb = flat[:, BLK:BLK + 2 * GP * P].rearrange("p (r g n) -> p r g n", r=2, g=GP)
    y_ch = flat[:, BLK:BLK + MT * CH * YC]
    w_glu = flat[:, 2 * BLK:2 * BLK + MT * W].rearrange("p (k n) -> p k n", k=MT)
    v_sb = flat[:, 3 * BLK:3 * BLK + 2 * GP * UC].rearrange("p (r g c) -> p r g c", r=2, g=GP)
    x_flat = x[:, :, :].rearrange("p i d -> p (i d)")
    SN = 2 * GP * YC
    s_sb = x_flat[:, 0:SN].rearrange("p (r g c) -> p r g c", r=2, g=GP)
    wz = [flat[:, BLK + i * ZN:BLK + (i + 1) * ZN] for i in range(3)] + [x_flat[:, SN:SN + ZN]]
    wo_flat = mid["w_out"][:, :, :].rearrange("p a b -> p (a b)")
    PW = 2 * GP * CH * GCH
    p_sb = wo_flat[:, PW:2 * PW].rearrange("p (r g i h) -> p r g i h", r=2, g=GP, i=CH)
    q_sb = wo_flat[:, 0:PW].rearrange("p (r g t h) -> p r g t h", r=2, g=GP, t=CH)
    y_blk = wo_flat[0:YC, PW:2 * PW].rearrange("c (t n) -> c t n", t=CH)
    rot = mid["ymix"][:, :, :].rearrange("p m t -> p (m t)")[:, 0:2 * ZN].rearrange("p (r g c) -> p r g c", r=2, g=GP)

    hT = buf("hT", [P, KD, TOK])
    hflat = hT[:, :, :].rearrange("p k t -> p (k t)")
    csq = hflat[:, MT * TOK:2 * MT * TOK]
    YN = MT * CH * YC
    gel = hflat[:, 0:YN]
    u_ch = buf("u_ch", [P, MT, CH, YC])
    u_flat = u_ch[:, :, :, :].rearrange("p m t c -> p (m t c)")
    zg = buf("zg", [P, MT, TOK + 2])
    u_blk = buf("u_blk", [P, GROUPS, UC])
    ublk_flat = u_blk[:, :, :].rearrange("p g c -> p (g c)")
    xs0 = buf("xs0", [P, ZN])
    xs = [xs0[:, 0:D], ublk_flat[:, 0:D]]
    junk = ublk_flat[:, D:2 * D]
    rho_t = xs0[:, :]
    prow = buf("prow", [36, P])
    arow = buf("arow", [GP, 4, P])
    dtrow = buf("dtrow", [GP, 2])
    par = buf("par", [P, 4, GP])
    bt = buf("bt", [P, 2, GP, GCH])
    bbar = buf("bbar", [P, 2, GP, GCH])
    ctl = buf("ctl", [P, 2, 2, P])
    ct = buf("ct", [P, 2, GP, GCH])
    cz = buf("cz", [P, 2, GP, 2, GCH])
    apow = buf("apow", [P, 2, CH + 1, GP])
    sm = buf("sm", [P, 24, GP])
    tmp = buf("tmp", [P, 2 * TOK])
    tpool = buf("tpool", [P, 2, GP, GCH])
    ss = buf("ss", [P, 3 * NT])
    s0l = buf("s0l", [P, 2, P])
    stout = bt[:, :, :, :].rearrange("p r g h -> p (r g h)")[:, 0:2 * GP + 2 * P]
    sttr = ctl[:, :, :, :].rearrange("p a b c -> p (a b) c")[:, 0:3, :]
    cbl = ublk_flat[0:2 * NDEC, 2 * D:2 * D + W]
    cbt = buf("cbt", [P, MT, 2 * NDEC])
    crow = ct[:, :, :, :].rearrange("p r g h -> p (r g h)")[0:2 + NDEC, :]
    ones = keep["ones"][:, :]
    tkern = bbar[:, :, :, :].rearrange("p r g h -> p (r g h)")
    NM, CW, NOS, NOC, DS, BG = 0, 8, 20, 24, 28, 32
    ORDER = [0, 1, 2, 3, 4, 5, 6, 7, 12, 13, 14, 15, 8, 9, 10, 11]

    names = ("ident cleared prow_in prow_psum pcol a_in dt_exp arow a_psum par exps b_in c_in c_psum ct "
             "s0_psum s0_done cb_in cb_psum cbt ss var root rstd xs xT_psum hT proj u_stored u_blk_in apow "
             "p_ready q_ready pt_psum wb k_psum k_sb toep v_psum v "
             "state_in y_psum y_blk yt_psum y_ch st_ready st_psum sttr crow_psum crow "
             "csq gel_in gel_sig y_gelu glu_psum glu_sig out_done cz").split()
    s = {n: sem("m_" + n) for n in names}
    x_in = [sem(f"m_x_in{i}") for i in range(NT)]
    w_in_in = [sem(f"m_w_in{i}") for i in range(4)]
    wglu_in = sem("m_wglu")
    proj_free = [sem("m_proj_free0"), sem("m_proj_free1")]
    dve_step, pool_step = sem("m_dve_step"), sem("m_pool_step")
    keep["wout_in"] = [sem("wout_in0"), sem("wout_in1")]
    keep["x_again"] = sem("x_again")

    def taken(eng, n):
        eng.wait_ge(proj_free[n % 2], n // 2 + 1)

    def gel_v(v):
        return v.rearrange("p (m t c) -> p m t c", m=MT, t=CH)

    block = stack.enter_context(nc.Block())

    @block.sync
    def _(sp):
        def load_x(i, signal):
            if i == 0:
                sp.dma_start(x[0:NMETA, 0, :], a["meta_tokens"]).then_inc(signal, 16)
                sp.dma_start(x[NMETA:P, 0, :], a["x_prompt"][0, 0:P - NMETA, :]).then_inc(signal, 16)
            elif i < NT - 1:
                sp.dma_start(x[:, i, :], a["x_prompt"][0, i * P - NMETA:(i + 1) * P - NMETA, :]).then_inc(signal, 16)
            else:
                n = LAST - NDEC
                sp.dma_start(x[0:n, i, :], a["x_prompt"][0, SEQ - n:SEQ, :]).then_inc(signal, 16)
                sp.dma_start(x[n:LAST, i, :], a["x_sample"][:, 0, :]).then_inc(signal, 16)

        for i in range(NT):
            load_x(i, x_in[i])
        w_src = a["w_in"][0].rearrange("(k p) (b n) -> b p k n", p=P, b=4)
        for blk in (0, 1, 3, 2):
            sp.dma_start(w_in[:, blk], w_src[blk]).then_inc(w_in_in[blk], 16)
        for n in range(MT):
            taken(sp, n)
        sp.dma_start(scratch["u"].rearrange("(m p) t c -> p m (t c)", p=P),
                     u_ch[:, :, :, :].rearrange("p m t c -> p m (t c)")).then_inc(s["u_stored"], 16)
        sp.wait_ge(s["u_stored"], 16)
        sp.wait_ge(s["cleared"], 2)
        u_src = scratch["u"].rearrange("(g h) t c -> t h g c", h=GCH)
        for t in range(CH):
            sp.dma_start(u_blk[t * GCH:(t + 1) * GCH, :, 0:YC], u_src[t]).then_inc(s["u_blk_in"], 16)
        sp.dma_start(u_blk[(CH - 1) * GCH:P, :, YC:UC], u_src[0, :, :, DEC0:YC]).then_inc(s["u_blk_in"], 16)
        sp.wait_ge(s["k_sb"], 1)
        sp.wait_ge(s["cleared"], 3)
        for t in range(CH):
            sp.dma_start(toep[0:(t + 1) * GCH, t, :], tkern[(CH - 1 - t) * GCH:P, :]).then_inc(s["toep"], 16)
        sp.wait_ge(s["proj"], 16)
        sp.dma_start(w_glu, a["w_glu"][0].rearrange("(k p) n -> p k n", p=P)).then_inc(wglu_in, 16)
        sp.wait_ge(s["sttr"], 1)
        for r, (p_out, s_out) in enumerate((("re_p", "re_s"), ("im_p", "im_s"))):
            sp.dma_start(out[p_out][0, 0].rearrange("(g a) n -> g (a n)", a=2), sttr[r * GP:(r + 1) * GP, 0, :]).then_inc(s["out_done"], 16)
            sp.dma_start(out[s_out][0].rearrange("b (g a) n -> (b g) (a n)", a=2), sttr[:, 1 + r, :]).then_inc(s["out_done"], 16)
        sp.wait_ge(s["crow"], 1)
        sp.dma_start(out["conv_p"][0, 0], crow[0:2, :]).then_inc(s["out_done"], 16)
        sp.dma_start(out["conv_s"][0, :, 1, :], crow[2:2 + NDEC, :]).then_inc(s["out_done"], 16)
        sp.dma_start(out["conv_s"][0, :, 0, :], a["state_conv"][0, :, 1, :]).then_inc(s["out_done"], 16)
        w_out_src = a["w_out"][0].rearrange("(b k p) n -> b p k n", b=2, p=P)
        for b in range(2):
            if b == 0:
                sp.wait_ge(s["y_psum"], 8)
            else:
                sp.wait_ge(s["yt_psum"], 2 * MT)
            sp.dma_start(mid["w_out"][:, b * MT:(b + 1) * MT], w_out_src[b]).then_inc(keep["wout_in"][b], 16)
        for i in range(NT - 1):
            load_x(i, keep["x_again"])
        sp.wait_ge(s["out_done"], 7 * 16)

    @block.scalar
    def _(act):
        act.dma_start(prow[NM:NM + 8, :], a["norm_mix"][0].rearrange("(k p) -> k p", p=P)).then_inc(s["prow_in"], 16)
        act.dma_start(prow[CW:CW + 12, :], a["conv_w"][0].rearrange("k (m p) -> (k m) p", p=P)).then_inc(s["prow_in"], 16)
        for o, n in ((NOS, "norm_out_ssm"), (NOC, "norm_out_conv"), (DS, "ssm_d"), (BG, "b_glu")):
            act.dma_start(prow[o:o + 4, :], a[n][0].rearrange("(m p) -> m p", p=P)).then_inc(s["prow_in"], 16)
        act.dma_start(arow[:, 0, :], a["ssm_a_re"][0].rearrange("(g a) n -> g (a n)", a=2)).then_inc(s["a_in"], 16)
        act.dma_start(arow[:, 1, :], a["ssm_a_im"][0].rearrange("(g a) n -> g (a n)", a=2)).then_inc(s["a_in"], 16)
        act.dma_start(dtrow[:], a["ssm_log_dt"][0].rearrange("(g a) -> g a", a=2)).then_inc(s["a_in"], 16)
        for i in range(NT):
            n = rows(i)
            act.wait_ge(x_in[i], 32 if i in (0, NT - 1) else 16)
            nc.scalar.activation(junk[0:n], x[0:n, i, :], ACT.Square, accum_out=ss[0:n, i:i + 1]).then_inc(s["ss"], 1)
            act.wait_ge(s["var"], i + 1)
            nc.scalar.activation(ss[0:n, NT + i:NT + i + 1], ss[0:n, i:i + 1], ACT.Sqrt).then_inc(s["root"], 1)
            act.wait_ge(s["rstd"], i + 1)
            if i >= 2:
                act.wait_ge(s["xT_psum"], i - 1)
            nc.scalar.activation(xs[i % 2][0:n], x[0:n, i, :], ACT.Copy, scale=ss[0:n, NT + i:NT + i + 1]).then_inc(s["xs"], 1)
        act.wait_ge(s["a_in"], 48)
        nc.scalar.activation(dtrow[:], dtrow[:], ACT.Exp).then_inc(s["dt_exp"], 1)
        act.wait_ge(s["par"], 1)
        nc.scalar.activation(sm[:, 0, :], par[:, 2, :], ACT.Exp)
        nc.scalar.activation(sm[:, 1, :], par[:, 2, :], ACT.Exp, scale=float(CH)).then_inc(s["exps"], 1)
        act.wait_ge(s["cleared"], 1)
        for n, m in enumerate(ORDER):
            if m >= 8:
                break
            act.wait_ge(s["proj"], n + 1)
            b0, b1 = bank[2 * (n % 2)], bank[2 * (n % 2) + 1]
            if m < MT:
                c0 = HALF // CH
                nc.scalar.activation(u_ch[:, m, :, 0:c0], b0[:, 0:HALF].rearrange("p (c t) -> p t c", t=CH), ACT.Copy)
                nc.scalar.activation(u_ch[:, m, :, c0:NCH], b1[:, 0:NPROMPT - HALF].rearrange("p (c t) -> p t c", t=CH), ACT.Copy)
                nc.scalar.activation(u_ch[:, m, 0, DEC0:YC], b1[:, NPROMPT - HALF:REST], ACT.Copy).then_inc(proj_free[n % 2], 1)
            else:
                dst = zg[:, m - 4, 2:2 + TOK]
                nc.scalar.activation(dst[:, 0:HALF], b0[:, 0:HALF], ACT.Copy)
                nc.scalar.activation(dst[:, HALF:TOK], b1[:, 0:REST], ACT.Copy).then_inc(proj_free[n % 2], 1)
        act.wait_ge(s["k_psum"], 1)
        nc.scalar.activation(tkern, bank[6][:], ACT.Copy).then_inc(s["k_sb"], 1)
        for j in range(8):
            act.wait_ge(s["pt_psum"], j + 1)
            r, q = j // 4, j % 4
            nc.scalar.activation(wb[:, r, 4 * q:4 * q + 4, :], bank[4 + j % 2][:].rearrange("p (g n) -> p g n", g=4), ACT.Copy).then_inc(s["wb"], 1)
        for j in range(8):
            act.wait_ge(s["v_psum"], j + 1)
            nc.scalar.activation(v_sb[:, :, 2 * j:2 * j + 2, :],
                                 bank[4 + j % 2][:, 0:4 * UC].rearrange("p (g r c) -> p r g c", g=2, r=2), ACT.Copy).then_inc(s["v"], 1)
        for n in (14, 15):
            taken(act, n)
        nc.scalar.activation(csq, mid["cmix"][:, :, :].rearrange("p m t -> p (m t)"), ACT.Square).then_inc(s["csq"], 1)

        def y_out(j):
            g0 = j % 2 + 8 * (j // 2)
            act.wait_ge(s["y_psum"], j + 1)
            nc.scalar.activation(y_blk[:, :, :].rearrange("c t (g h) -> c g t h", h=GCH)[:, g0:g0 + 7:2],
                                 bank[4 + j % 2][0:YC, :].rearrange("c (g t h) -> c g t h", g=4, t=CH), ACT.Copy).then_inc(s["y_blk"], 1)

        y_out(0)
        y_out(1)
        for m in range(MT):
            if m < MT - 1:
                y_out(2 * m + 2)
            for h in range(2):
                act.wait_ge(s["yt_psum"], 2 * m + h + 1)
                c0 = (2 * m + h) * 4 * YC
                nc.scalar.activation(y_ch[:, c0:c0 + 4 * YC], bank[6 + h][:, 0:4 * YC], ACT.Copy).then_inc(s["y_ch"], 1)
            if m < MT - 1:
                y_out(2 * m + 3)
            act.wait_ge(s["gel_in"], m + 1)
            g_m = gel[:, m * CH * YC:(m + 1) * CH * YC]
            nc.scalar.activation(g_m, g_m, ACT.Sigmoid, scale=2 * math.sqrt(2 / math.pi)).then_inc(s["gel_sig"], 1)
        act.wait_ge(keep["wout_in"][0], 16)
        for m in range(MT):
            nc.scalar.activation(mid["w_out"][:, m, :], mid["w_out"][:, m, :], ACT.Copy, scale=pcol[:, NOS + m:NOS + m + 1])
            act.wait_ge(s["glu_psum"], m + 1)
            for h in range(2):
                nc.scalar.activation(gel_v(gel)[:, m, 4 * h:4 * h + 4, :],
                                     bank[2 * m + h][:, 0:4 * YC].rearrange("p (t c) -> p t c", t=4), ACT.Sigmoid,
                                     bias=pcol[:, BG + m:BG + m + 1]).then_inc(s["glu_sig"], 1)

    @block.gpsimd
    def _(pool):
        nc.gpsimd.memset(ident[:], 0.0).then_inc(pool_step, 1)
        pool.wait_ge(pool_step, 1)
        nc.gpsimd.affine_select(out=ident[:], in_=ident[:], compare_op=ALU.not_equal, fill=1.0, base=0,
                                pattern=[[-1, P]], channel_multiplier=1).then_inc(s["ident"], 1)
        for r, n in enumerate(("ssm_b_re", "ssm_b_im")):
            for g2 in range(2):
                pool.dma_start(bt[g2 * NS:(g2 + 1) * NS, r], a[n][0].rearrange("(g a) n h -> a n g h", a=2)[g2]).then_inc(s["b_in"], 16)
        for r, n in enumerate(("ssm_c_re", "ssm_c_im")):
            for half in range(2):
                for g in range(8):
                    pool.dma_start(ctl[g * GCH:(g + 1) * GCH, r, half, :].rearrange("h (a n) -> h a n", a=2),
                                   a[n][0].rearrange("(g a) h n -> g h a n", a=2)[half * 8 + g]).then_inc(s["c_in"], 16)
        for r, n in enumerate(("state_ssm_re", "state_ssm_im")):
            pool.dma_start(s0l[:, r, :], a[n][0].rearrange("b (g a) n -> (b g) (a n)", a=2)).then_inc(s["cb_in"], 16)
        pool.dma_start(cbl, a["state_conv"][0].rearrange("b k c -> (b k) c")).then_inc(s["cb_in"], 16)
        nc.gpsimd.memset(u_flat, 0.0)
        nc.gpsimd.memset(zg[:, :, 0:2], 0.0).then_inc(s["cleared"], 1)
        nc.gpsimd.memset(cz[:], 0.0).then_inc(s["cz"], 1)
        pool.wait_ge(s["xT_psum"], NT)
        pool.wait_ge(s["cb_psum"], 1)
        nc.gpsimd.memset(u_blk[:, :, YC:UC], 0.0).then_inc(s["cleared"], 1)
        pool.wait_ge(s["proj"], MT)
        nc.gpsimd.memset(toep, 0.0).then_inc(s["cleared"], 1)
        pool.wait_ge(s["apow"], 1)
        pool.wait_ge(s["ct"], 1)
        steps = pool_step
        n = 1
        for t in range(CH):
            ar = apow[:, 0, t + 1, :].unsqueeze(2).to_broadcast([P, GP, GCH])
            ai = apow[:, 1, t + 1, :].unsqueeze(2).to_broadcast([P, GP, GCH])
            nc.gpsimd.tensor_tensor(q_sb[:, 0, :, t, :], ct[:, 0], ar, ALU.mult)
            nc.gpsimd.tensor_tensor(tpool[:, 0], ct[:, 1], ai, ALU.mult)
            nc.gpsimd.tensor_tensor(q_sb[:, 1, :, t, :], ct[:, 0], ai, ALU.mult)
            nc.gpsimd.tensor_tensor(tpool[:, 1], ct[:, 1], ar, ALU.mult).then_inc(steps, 1)
            n += 1
            pool.wait_ge(steps, n)
            nc.gpsimd.tensor_tensor(q_sb[:, 0, :, t, :], q_sb[:, 0, :, t, :], tpool[:, 0], ALU.subtract)
            nc.gpsimd.tensor_tensor(tpool[:, 1], q_sb[:, 1, :, t, :], tpool[:, 1], ALU.add).then_inc(steps, 1)
            n += 1
            pool.wait_ge(steps, n)
            nc.gpsimd.tensor_scalar(q_sb[:, 1, :, t, :], tpool[:, 1], -1.0, None, ALU.mult).then_inc(steps, 1)
            n += 1
            pool.wait_ge(steps, n)
        nc.gpsimd.memset(tpool[:, 0, 0, 0:1], 0.0).then_inc(s["q_ready"], 1)

    @block.tensor
    def _(pe):
        pe.wait_ge(s["ident"], 1)
        pe.wait_ge(s["prow_in"], 16 * 6)
        nc.tensor.transpose(bank[0][:, 0:36], prow[:], ident[0:36, 0:36]).then_inc(s["prow_psum"], 1)

        def x_transposes(i):
            n = rows(i)
            pe.wait_ge(s["xs"], i + 1)
            if i >= 2:
                pe.wait_ge(s["hT"], 2 * (i - 1))
            for k in range(KD):
                last = nc.tensor.transpose(bank[4 + 2 * (i % 2) + k // 4][:, (k % 4) * P:(k % 4) * P + n],
                                           xs[i % 2][0:n, k * P:(k + 1) * P], ident[0:n, 0:n])
            last.then_inc(s["xT_psum"], 1)

        for i in range(NT):
            x_transposes(i)
        pe.wait_ge(s["hT"], 2 * NT)
        pe.wait_ge(s["pcol"], 1)
        def lag_kernel():
            pe.wait_ge(s["p_ready"], 1)
            pe.wait_ge(s["cz"], 2)
            pe.wait_ge(s["s0_done"], 1)
            for g in range(GP):
                for r in range(2):
                    last = nc.tensor.matmul(bank[6][:, g * 32:(g + 1) * 32], p_sb[:, r, g].rearrange("p i h -> p (i h)"),
                                            cz[:, r, g].rearrange("p a h -> p (a h)"), start=(r == 0), stop=(r == 1))
            last.then_inc(s["k_psum"], 1)
            for j in range(8):
                r, q = j // 4, j % 4
                if j >= 2:
                    pe.wait_ge(s["wb"], j - 1)
                else:
                    pe.wait_ge(s["cbt"], 1)
                for g in range(4):
                    last = nc.tensor.transpose(bank[4 + j % 2][:, g * P:(g + 1) * P],
                                               p_sb[:, r, 4 * q + g].rearrange("p i h -> p (i h)"), ident[:])
                last.then_inc(s["pt_psum"], 1)

        def chunk_inputs():
            pe.wait_ge(s["u_blk_in"], 16 * (CH + 1))
            pe.wait_ge(s["wb"], 8)
            for j in range(8):
                if j >= 2:
                    pe.wait_ge(s["v"], j - 1)
                for gg in range(2):
                    for r in range(2):
                        for g2 in range(2):
                            gp = 2 * j + gg
                            last = nc.tensor.matmul(bank[4 + j % 2][g2 * NS:(g2 + 1) * NS, (2 * gg + r) * UC:(2 * gg + r + 1) * UC],
                                                    wb[:, r, gp, g2 * NS:(g2 + 1) * NS], u_blk[:, 2 * gp + g2, :], start=True, stop=True)
                last.then_inc(s["v_psum"], 1)

        for n, m in enumerate(ORDER):
            pe.wait_ge(w_in_in[m // 4], 16)
            if n >= 2:
                taken(pe, n - 2)
            for k in range(KD):
                wk = w_in[:, m // 4, k, (m % 4) * P:(m % 4 + 1) * P]
                nc.tensor.matmul(bank[2 * (n % 2)][:, 0:HALF], wk, hT[:, k, 0:HALF], start=(k == 0), stop=(k == KD - 1))
                last = nc.tensor.matmul(bank[2 * (n % 2) + 1][:, 0:REST], wk, hT[:, k, HALF:TOK], start=(k == 0), stop=(k == KD - 1))
            last.then_inc(s["proj"], 1)
            if n == 0:
                pe.wait_ge(s["arow"], 1)
                for j in range(4):
                    last = nc.tensor.transpose(bank[7][:, j * GP:(j + 1) * GP], arow[:, j, :], ident[0:GP, 0:GP])
                last.then_inc(s["a_psum"], 1)
            if n == 3:
                pe.wait_ge(s["par"], 1)
                pe.wait_ge(s["c_in"], 16 * 32)
                for r in range(2):
                    for half in range(2):
                        last = nc.tensor.transpose(bank[7][:, (2 * r + half) * P:(2 * r + half + 1) * P], ctl[:, r, half, :], ident[:])
                last.then_inc(s["c_psum"], 1)
                pe.wait_ge(s["cb_in"], 48)
                for r in range(2):
                    last = nc.tensor.transpose(bank[6][:, r * P:(r + 1) * P], s0l[:, r, :], ident[:])
                last.then_inc(s["s0_psum"], 1)
                for m4 in range(MT):
                    last = nc.tensor.transpose(bank[5][:, m4 * 16:(m4 + 1) * 16], cbl[:, m4 * P:(m4 + 1) * P], ident[0:16, 0:16])
                last.then_inc(s["cb_psum"], 1)
            if n == 8:
                lag_kernel()
            if n == 11:
                chunk_inputs()

        def chunk_outputs(j):
            odd = j % 2
            if j >= 2:
                pe.wait_ge(s["y_blk"], j - 1)
            for i in range(4):
                g = odd + 8 * (j // 2) + 2 * i
                o = bank[4 + odd][0:YC, i * P:(i + 1) * P]
                nc.tensor.matmul(o, u_blk[:, g, 0:YC], toep[:, :, g * GCH:(g + 1) * GCH], start=True, stop=False)
                for r in range(2):
                    last = nc.tensor.matmul(o, s_sb[odd * NS:(odd + 1) * NS, r, g // 2, :],
                                            q_sb[odd * NS:(odd + 1) * NS, r, g // 2].rearrange("p t h -> p (t h)"), start=False, stop=(r == 1))
            last.then_inc(s["y_psum"], 1)

        def to_channels(m):
            pe.wait_ge(s["y_blk"], 2 * m + 2)
            if m == 0:
                pe.wait_ge(s["sttr"], 1)
                pe.wait_ge(s["crow"], 1)
            for h in range(2):
                if m >= 1:
                    pe.wait_ge(s["y_ch"], 2 * m - 1 + h)
                for t in range(4):
                    last = nc.tensor.transpose(bank[6 + h][:, t * YC:(t + 1) * YC], y_blk[:, 4 * h + t, m * P:(m + 1) * P], ident[0:YC, 0:YC])
                last.then_inc(s["yt_psum"], 1)

        yv = gel_v(y_ch)

        def glu(m, k):
            pe.wait_ge(s["y_gelu"], k + 1)
            for h in range(2):
                last = nc.tensor.matmul(bank[2 * m + h][:, 0:4 * YC], w_glu[:, k, m * P:(m + 1) * P],
                                        yv[:, k, 4 * h:4 * h + 4, :].rearrange("p t c -> p (t c)"),
                                        start=(k == 0), stop=(k == MT - 1))
            if k == MT - 1:
                last.then_inc(s["glu_psum"], 1)

        pe.wait_ge(s["toep"], 16 * CH)
        pe.wait_ge(s["state_in"], 1)
        pe.wait_ge(s["q_ready"], 1)
        pe.wait_ge(s["v"], 8)
        chunk_outputs(0)
        chunk_outputs(1)
        for n in (14, 15):
            taken(pe, n)
        pe.wait_ge(s["ct"], 1)
        for m in range(MT):
            last = nc.tensor.transpose(bank[7][0:2 + NDEC, m * P:(m + 1) * P], zg[:, m, NPROMPT:NPROMPT + 2 + NDEC], ident[:])
        last.then_inc(s["crow_psum"], 1)
        pe.wait_ge(s["k_sb"], 1)
        pe.wait_ge(s["csq"], 2)
        pe.wait_ge(s["st_ready"], 1)
        for i in range(NT):
            nc.tensor.matmul(bank[6][0:rows(i), 3 * P + i:3 * P + i + 1], csq[:, i * P:i * P + rows(i)], ones[:, 0:1], start=True, stop=True)
        nc.tensor.transpose(bank[6][0:2 * GP, 0:P], stout[:, 0:2 * GP], ident[:])
        for r in range(2):
            last = nc.tensor.transpose(bank[6][:, (1 + r) * P:(2 + r) * P], stout[:, 2 * GP + r * P:2 * GP + (r + 1) * P], ident[:])
        last.then_inc(s["st_psum"], 1)
        pe.wait_ge(wglu_in, 16)
        for m in range(1, MT):
            chunk_outputs(2 * m)
            to_channels(m - 1)
            chunk_outputs(2 * m + 1)
            if m >= 2:
                for mo in range(2):
                    glu(mo, m - 2)
        to_channels(MT - 1)
        for mo in range(2):
            glu(mo, MT - 2)
        pe.wait_ge(s["y_blk"], 8)
        for k in range(MT - 1):
            glu(2, k)
        for mo in range(3):
            glu(mo, MT - 1)
        pe.wait_ge(s["y_ch"], 8)
        for k in range(MT):
            glu(3, k)

    @block.vector
    def _(dve):
        count = [0]

        def done(ins):
            count[0] += 1
            ins.then_inc(dve_step, 1)
            dve.wait_ge(dve_step, count[0])

        def tt(o, x0, x1, op):
            return nc.vector.tensor_tensor(o, x0, x1, op)

        def ts(o, x0, s1, op0, s2=None, op1=None):
            if op1 is None:
                return nc.vector.tensor_scalar(o, x0, s1, None, op0)
            return nc.vector.tensor_scalar(o, x0, s1, s2, op0, op1)

        def stt(o, x0, sc, x1, op0, op1):
            return nc.vector.scalar_tensor_tensor(out=o, in0=x0, scalar=sc, in1=x1, op0=op0, op1=op1)

        def cmul(o_re, o_im, a_re, a_im, b_re, b_im, t0, t1):
            tt(o_re, a_re, b_re, ALU.mult)
            tt(t0, a_im, b_im, ALU.mult)
            tt(o_im, a_re, b_im, ALU.mult)
            done(tt(t1, a_im, b_re, ALU.mult))
            tt(o_re, o_re, t0, ALU.subtract)
            done(tt(o_im, o_im, t1, ALU.add))

        dve.wait_ge(s["prow_psum"], 1)
        nc.vector.tensor_copy(pcol[:], bank[0][:, 0:36]).then_inc(s["pcol"], 1)
        nc.vector.memset(ones, 1.0)
        dve.wait_ge(s["pcol"], 1)

        def take_hT(i):
            n = rows(i)
            dve.wait_ge(s["xT_psum"], i + 1)
            for q in range(2):
                tt(hT[:, 4 * q:4 * q + 4, i * P:i * P + n],
                   bank[4 + 2 * (i % 2) + q][:].rearrange("p (k t) -> p k t", k=4)[:, :, 0:n],
                   pcol[:, NM + 4 * q:NM + 4 * q + 4].unsqueeze(2).to_broadcast([P, 4, n]), ALU.mult).then_inc(s["hT"], 1)

        for i in range(NT):
            n = rows(i)
            dve.wait_ge(s["ss"], i + 1)
            ts(ss[0:n, i:i + 1], ss[0:n, i:i + 1], 1.0 / D, ALU.mult, EPS, ALU.add).then_inc(s["var"], 1)
            dve.wait_ge(s["root"], i + 1)
            refine_rsqrt(nc, done, ss[0:n, NT + i:NT + i + 1], ss[0:n, 2 * NT + i:2 * NT + i + 1], ss[0:n, i:i + 1]).then_inc(s["rstd"], 1)
            if i >= 1:
                take_hT(i - 1)
        take_hT(NT - 1)
        dve.wait_ge(s["dt_exp"], 1)
        for j in range(2):
            last = tt(arow[:, 2 + j, :].rearrange("g (a n) -> g a n", a=2), arow[:, j, :].rearrange("g (a n) -> g a n", a=2),
                      dtrow[:].unsqueeze(2).to_broadcast([GP, 2, NS]), ALU.mult)
        last.then_inc(s["arow"], 1)

        dve.wait_ge(s["a_psum"], 1)
        nc.vector.tensor_copy(par[:].rearrange("p a g -> p (a g)"), bank[7][:, 0:4 * GP]).then_inc(s["par"], 1)
        dve.wait_ge(s["par"], 1)
        mag, rho, kk, r, hh, h2, sn, vs, t0, t1, cs, er, ei, er2, ei2, nr, den, cr, ci = (sm[:, i, :] for i in range(19))
        are, aim, dre, dim = (par[:, i, :] for i in range(4))
        BIG = 12582912.0
        c1 = 6.28125
        c2 = float(math.floor((2 * math.pi - c1) * 2 ** 20) / 2 ** 20)
        c3 = 2 * math.pi - c1 - c2
        done(ts(kk, dim, 1 / (2 * math.pi), ALU.mult))
        done(ts(kk, kk, BIG, ALU.add))
        done(ts(kk, kk, BIG, ALU.subtract))
        done(stt(r, kk, -c1, dim, ALU.mult, ALU.add))
        done(stt(r, kk, -c2, r, ALU.mult, ALU.add))
        done(stt(r, kk, -c3, r, ALU.mult, ALU.add))
        done(ts(hh, r, 0.125, ALU.mult))
        done(tt(h2, hh, hh, ALU.mult))
        done(ts(t0, h2, -1 / 72, ALU.mult, 1.0, ALU.add))
        done(tt(t0, t0, h2, ALU.mult))
        done(ts(t0, t0, -1 / 42, ALU.mult, 1.0, ALU.add))
        done(tt(t0, t0, h2, ALU.mult))
        done(ts(t0, t0, -1 / 20, ALU.mult, 1.0, ALU.add))
        done(tt(t0, t0, h2, ALU.mult))
        done(ts(t0, t0, -1 / 6, ALU.mult, 1.0, ALU.add))
        tt(sn, t0, hh, ALU.mult)
        done(ts(t1, h2, -1 / 56, ALU.mult, 1.0, ALU.add))
        done(tt(t1, t1, h2, ALU.mult))
        done(ts(t1, t1, -1 / 30, ALU.mult, 1.0, ALU.add))
        done(tt(t1, t1, h2, ALU.mult))
        done(ts(t1, t1, -1 / 12, ALU.mult, 1.0, ALU.add))
        done(tt(t1, t1, h2, ALU.mult))
        done(ts(vs, t1, 0.5, ALU.mult))
        for _ in range(3):
            tt(t0, sn, vs, ALU.mult)
            done(tt(t1, sn, sn, ALU.mult))
            done(tt(t0, sn, t0, ALU.subtract))
            ts(vs, t1, 2.0, ALU.mult)
            done(ts(sn, t0, 2.0, ALU.mult))
        done(ts(cs, vs, -1.0, ALU.mult, 1.0, ALU.add))
        dve.wait_ge(s["exps"], 1)
        nc.vector.memset(apow[:, 0, 0, :], 1.0)
        nc.vector.memset(apow[:, 1, 0, :], 0.0)
        tt(apow[:, 0, 1, :], mag, cs, ALU.mult)
        done(tt(apow[:, 1, 1, :], mag, sn, ALU.mult))
        for h in (1, 2, 4):
            hi = [apow[:, c, h, :].unsqueeze(1).to_broadcast([P, h, GP]) for c in range(2)]
            tv = [tmp[:, c * 64:c * 64 + h * GP].rearrange("p (k g) -> p k g", k=h) for c in range(2)]
            cmul(apow[:, 0, h + 1:2 * h + 1, :], apow[:, 1, h + 1:2 * h + 1, :],
                 apow[:, 0, 1:h + 1, :], apow[:, 1, 1:h + 1, :], hi[0], hi[1], tv[0], tv[1])
        nc.vector.tensor_copy(cr, cs).then_inc(s["apow"], 1)
        cmul(er, ei, cs, sn, cs, sn, t0, t1)
        cmul(er2, ei2, er, ei, er, ei, t0, t1)
        cmul(rot[:, 0, :, 0], rot[:, 1, :, 0], er2, ei2, er2, ei2, t0, t1)
        have = 1
        while have < NCH:
            n = min(have, NCH - have)
            hi = [rot[:, c, :, have - 1:have].to_broadcast([P, GP, n]) for c in range(2)]
            tv = [tmp[:, c * GP * 32:c * GP * 32 + GP * n].rearrange("p (g c) -> p g c", g=GP) for c in range(2)]
            cmul(rot[:, 0, :, have:have + n], rot[:, 1, :, have:have + n],
                 rot[:, 0, :, 0:n], rot[:, 1, :, 0:n], hi[0], hi[1], tv[0], tv[1])
            have += n
        ts(nr, apow[:, 0, 1, :], -1.0, ALU.add)
        tt(t0, are, are, ALU.mult)
        done(tt(t1, aim, aim, ALU.mult))
        done(tt(den, t0, t1, ALU.add))
        done(nc.vector.reciprocal(den, den))
        ni = apow[:, 1, 1, :]
        tt(cr, nr, are, ALU.mult)
        tt(t0, ni, aim, ALU.mult)
        tt(ci, ni, are, ALU.mult)
        done(tt(t1, nr, aim, ALU.mult))
        tt(cr, cr, t0, ALU.add)
        done(tt(ci, ci, t1, ALU.subtract))
        tt(cr, cr, den, ALU.mult)
        done(tt(ci, ci, den, ALU.mult))
        tv = [tmp[:, c * GP * GCH:(c + 1) * GP * GCH].rearrange("p (g h) -> p g h", g=GP) for c in range(2)]
        dve.wait_ge(s["b_in"], 64)
        cmul(bbar[:, 0], bbar[:, 1], cr.unsqueeze(2).to_broadcast([P, GP, GCH]), ci.unsqueeze(2).to_broadcast([P, GP, GCH]),
             bt[:, 0], bt[:, 1], tv[0], tv[1])
        dve.wait_ge(s["c_psum"], 1)
        nc.vector.tensor_copy(ct[:].rearrange("p r g h -> p (r g h)"), bank[7][:]).then_inc(s["ct"], 1)
        dve.wait_ge(s["ct"], 1)
        dve.wait_ge(s["cz"], 1)
        for g2 in range(2):
            q = slice(g2 * NS, (g2 + 1) * NS)
            nc.vector.tensor_copy(cz[q, 0, :, g2, :], ct[q, 0])
            last = ts(cz[q, 1, :, g2, :], ct[q, 1], -1.0, ALU.mult)
        last.then_inc(s["cz"], 1)
        dve.wait_ge(s["cb_psum"], 1)
        nc.vector.tensor_copy(cbt[:].rearrange("p m b -> p (m b)"), bank[5][:, 0:MT * 16]).then_inc(s["cbt"], 1)
        dve.wait_ge(s["xs"], NT)
        nc.vector.memset(s_sb[:, :, :, 0:1], 0.0)
        dve.wait_ge(s["s0_psum"], 1)
        for c in range(2):
            nc.vector.tensor_copy(s_sb[:, c, :, DEC0:YC], bank[6][:, c * P:(c + 1) * P].rearrange("p (b g) -> p g b", g=GP))
        rho_v = rho_t.rearrange("p (g c) -> p g c", g=GP)
        done(nc.vector.tensor_copy(rho_v, rho.unsqueeze(2).to_broadcast([P, GP, NCH])))
        nc.vector.memset(rho_v[:, :, 0:1], 0.0).then_inc(s["s0_done"], 1)
        for i in range(CH):
            ar = apow[:, 0, CH - 1 - i, :].unsqueeze(2).to_broadcast([P, GP, GCH])
            ai = apow[:, 1, CH - 1 - i, :].unsqueeze(2).to_broadcast([P, GP, GCH])
            cmul(p_sb[:, 0, :, i, :], p_sb[:, 1, :, i, :], bbar[:, 0], bbar[:, 1], ar, ai, tv[0], tv[1])
        nc.vector.memset(t0, 0.0).then_inc(s["p_ready"], 1)

        dve.wait_ge(s["cbt"], 1)
        for m in range(MT):
            n = 8 + m
            taken(dve, 4 + m)
            dve.wait_ge(s["proj"], n + 1)
            tt(zg[:, m, 2:2 + HALF], zg[:, m, 2:2 + HALF], bank[2 * (n % 2)][:, 0:HALF], ALU.mult)
            tt(zg[:, m, 2 + HALF:2 + TOK], zg[:, m, 2 + HALF:2 + TOK], bank[2 * (n % 2) + 1][:, 0:REST], ALU.mult).then_inc(proj_free[n % 2], 1)
            taken(dve, n)
            w = [pcol[:, CW + 4 * k + m:CW + 4 * k + m + 1] for k in range(3)]
            conv = mid["cmix"][:, m, :]
            acc, accd = conv[:, 0:NPROMPT], conv[:, NPROMPT:TOK]
            old = cbt[:, m, :].rearrange("p (b k) -> p k b", k=2)
            ts(acc, zg[:, m, 0:NPROMPT], w[0], ALU.mult)
            done(ts(accd, old[:, 0], w[0], ALU.mult))
            stt(acc, zg[:, m, 1:1 + NPROMPT], w[1], acc, ALU.mult, ALU.add)
            done(stt(accd, old[:, 1], w[1], accd, ALU.mult, ALU.add))
            done(stt(conv, zg[:, m, 2:2 + TOK], w[2], conv, ALU.mult, ALU.add))

        def conv_gate_out(m):
            n = 12 + m
            dve.wait_ge(s["proj"], n + 1)
            tt(mid["cmix"][:, m, 0:HALF], mid["cmix"][:, m, 0:HALF], bank[2 * (n % 2)][:, 0:HALF], ALU.mult)
            tt(mid["cmix"][:, m, HALF:TOK], mid["cmix"][:, m, HALF:TOK], bank[2 * (n % 2) + 1][:, 0:REST], ALU.mult).then_inc(proj_free[n % 2], 1)

        dve.wait_ge(s["v"], 8)
        wv = [v.rearrange("p (g c) -> p g c", g=GP) for v in wz]
        vr, vi = v_sb[:, 0, :, 0:NCH], v_sb[:, 1, :, 0:NCH]
        tt(wv[0], rot[:, 0], vr, ALU.mult)
        tt(wv[2], rot[:, 1], vi, ALU.mult)
        tt(wv[1], rot[:, 0], vi, ALU.mult)
        done(tt(wv[3], rot[:, 1], vr, ALU.mult))
        tt(wv[0], wv[0], wv[2], ALU.add)
        done(tt(wv[1], wv[1], wv[3], ALU.subtract))
        conv_gate_out(0)
        nc.vector.tensor_tensor_scan(wz[2], rho_t, wz[0], 0.0, ALU.mult, ALU.add)
        done(nc.vector.tensor_tensor_scan(wz[3], rho_t, wz[1], 0.0, ALU.mult, ALU.add))
        sr, si = s_sb[:, 0, :, 1:1 + NCH], s_sb[:, 1, :, 1:1 + NCH]
        tt(sr, rot[:, 0], wv[2], ALU.mult)
        tt(wv[0], rot[:, 1], wv[3], ALU.mult)
        tt(si, rot[:, 0], wv[3], ALU.mult)
        done(tt(wv[1], rot[:, 1], wv[2], ALU.mult))
        conv_gate_out(1)
        tt(sr, sr, wv[0], ALU.subtract)
        tt(si, si, wv[1], ALU.add).then_inc(s["state_in"], 1)
        dve.wait_ge(s["state_in"], 1)
        nc.vector.tensor_copy(stout[:, 0:2 * GP].rearrange("p (r g) -> p r g", r=2), s_sb[:, :, :, NCH])
        so = [stout[:, 2 * GP + c * P:2 * GP + (c + 1) * P].rearrange("p (b g) -> p g b", g=GP) for c in range(2)]
        d0, d1 = s_sb[:, 0, :, DEC0:YC], s_sb[:, 1, :, DEC0:YC]
        ab = [apow[:, c, 1, :].unsqueeze(2).to_broadcast([P, GP, NDEC]) for c in range(2)]
        tv = [tmp[:, c * P:(c + 1) * P].rearrange("p (g b) -> p g b", g=GP) for c in range(4)]
        cmul(tv[2], tv[3], d0, d1, ab[0], ab[1], tv[0], tv[1])
        tt(so[0], tv[2], v_sb[:, 0, :, YC:UC], ALU.add)
        tt(so[1], tv[3], v_sb[:, 1, :, YC:UC], ALU.add).then_inc(s["st_ready"], 1)
        conv_gate_out(2)
        conv_gate_out(3)
        dve.wait_ge(s["csq"], 1)
        done(tt(csq[:, 0:2 * TOK], csq[:, 0:2 * TOK], csq[:, 2 * TOK:4 * TOK], ALU.add))
        tt(csq[:, 0:TOK], csq[:, 0:TOK], csq[:, TOK:2 * TOK], ALU.add).then_inc(s["csq"], 1)
        for m in range(MT):
            ts(mid["cmix"][:, m, :], mid["cmix"][:, m, :], pcol[:, NOC + m:NOC + m + 1], ALU.mult)
        dve.wait_ge(s["crow_psum"], 1)
        dve.wait_ge(s["q_ready"], 1)
        nc.vector.tensor_copy(crow, bank[7][0:2 + NDEC, :]).then_inc(s["crow"], 1)
        dve.wait_ge(s["st_psum"], 1)
        nc.vector.tensor_copy(keep["conv_ss"][:, 0:NT - 1], bank[6][:, 3 * P:3 * P + NT - 1])
        nc.vector.tensor_copy(keep["conv_ss"][0:LAST, NT - 1:NT], bank[6][0:LAST, 3 * P + NT - 1:3 * P + NT])
        nc.vector.tensor_copy(sttr[0:2 * GP, 0, :], bank[6][0:2 * GP, 0:P])
        nc.vector.tensor_copy(sttr[:, 1:3, :], bank[6][:, P:3 * P].rearrange("p (a c) -> p a c", a=2)).then_inc(s["sttr"], 1)

        yv, uv = gel_v(y_ch), u_ch
        for m in range(MT):
            dve.wait_ge(s["y_ch"], 2 * (m + 1))
            y_m, g_m = y_ch[:, m * CH * YC:(m + 1) * CH * YC], gel[:, m * CH * YC:(m + 1) * CH * YC]
            done(stt(yv[:, m], uv[:, m], pcol[:, DS + m:DS + m + 1], yv[:, m], ALU.mult, ALU.add))
            done(tt(g_m, y_m, y_m, ALU.mult))
            done(ts(g_m, g_m, 0.044715, ALU.mult, 1.0, ALU.add))
            tt(g_m, g_m, y_m, ALU.mult).then_inc(s["gel_in"], 1)
            dve.wait_ge(s["gel_sig"], m + 1)
            tt(y_m, y_m, g_m, ALU.mult).then_inc(s["y_gelu"], 1)
        dve.wait_ge(s["y_gelu"], MT)
        for m in range(MT):
            dve.wait_ge(s["glu_sig"], 2 * (m + 1))
            tt(mid["ymix"][:, m, 0:NPROMPT].rearrange("p (c t) -> p t c", t=CH), yv[:, m, :, 0:NCH], gel_v(gel)[:, m, :, 0:NCH], ALU.mult)
            tt(mid["ymix"][:, m, NPROMPT:TOK], yv[:, m, 0, DEC0:YC], gel_v(gel)[:, m, 0, DEC0:YC], ALU.mult)

def loop_tables(stack, sb):
    return {
        "rank": sb(stack, "rank", [P, NT, E + 1]),
        "slotval": sb(stack, "slotval", [P, NT, E + 1, 3]),
        "iota_s": sb(stack, "iota_s", [P, P]),
        "pick_row": sb(stack, "pick_row", [96, E, P], BF16),
        "bias": sb(stack, "bias", [96, 3 * FF], BF16),
        "over_i": sb(stack, "over_i", [P, 2, NOVER], I32),
        "over_base": sb(stack, "over_base", [P, NOVER]),
    }


def weight_load(eng, a, keep, mid, e, j):
    if j < 8:
        half, k = j // 4, 2 * (j % 4)
        src = a["w_gate_up"][0].rearrange("e (p k) (u f n) -> e f p (k u) n", p=P, u=2, f=2)[e, half, :, 2 * k:2 * k + 4]
        dst = keep["ring_lo"][:, 2 * j:2 * j + 2, :].rearrange("p k (u n) -> p (k u) n", u=2)
    else:
        k = 2 * (j - 8)
        src = a["w_down"][0].rearrange("e (k p) n -> e p k n", p=P)[e, :, k:k + 2]
        dst = mid["w_out"][:, k:k + 2, :]
    return eng.dma_start(dst, src)


def router(nc, a, scratch, stack, sb, sem, bank, keep, mid, tb):
    def buf(name, shape, dt=F32):
        return sb(stack, name, shape, dt)

    x, ident, pcol = keep["x"], keep["ident"], keep["pcol"]
    NOS, NOC = 20, 24
    ymix, cmix, w_out = mid["ymix"], mid["cmix"], mid["w_out"]
    sq = buf("sq", [P, MT, TOK])
    gffn = buf("gffn", [P, D])
    hf = buf("hf", [P, 2, D])
    hfT = buf("hfT", [P, 2, KD, P])
    w_r = buf("w_r", [P, KD, E])
    b_r = buf("b_r", [1, E])
    ones = buf("ones", [P, P])
    ones_b = buf("ones_b", [P, P], BF16)
    tri = buf("tri", [P, P], BF16)
    ssq = buf("ssq", [P, 3, 2 * NT])
    ss2 = buf("ss2", [P, 3, NT])
    jk = buf("jk", [P, D], BF16)
    lg = buf("lg", [P, NT, E])
    top = buf("top", [P, NT, 8])
    topi = buf("topi", [P, NT, 8], U32)
    topf = buf("topf", [P, NT, 8])
    iota_i = buf("iota_i", [P, P], I32)
    eqk = buf("eqk", [P, NT, E, TOPK])
    mask = buf("mask", [P, NT, E])
    mask_b = buf("mask_b", [P, NT, E], BF16)
    gate = buf("gate", [P, NT, E])
    gsum = buf("gsum", [P, NT])
    cum = buf("cum", [P, NT, E])
    tokv = buf("tokv", [P, NT])
    tok_i = buf("tok_i", [P, NT], I32)
    valid = buf("valid", [P, NT])
    cnt = buf("cnt", [P, 4, E])
    om = buf("om", [P, 2, NOVER, E])
    of = buf("of", [P, 4, NOVER])
    NB = 4
    HB = 3 * FF // NB
    bf = buf("bf", [96, HB])
    bsrc = (a["b_gate_up"][0], a["b_down"][0])
    bias_src = []
    for h in range(NB):
        lo, hi, split = h * HB, (h + 1) * HB, 2 * FF
        pieces = [(bsrc[0][:, lo:min(hi, split)], 0)] if lo < split else []
        if hi > split:
            pieces.append((bsrc[1][:, max(lo - split, 0):hi - split], max(split - lo, 0)))
        bias_src.append(pieces)
    bias_pieces = [len(p) for p in bias_src]

    s = {n: sem("r_" + n) for n in (
        "bias_done consts gffn_in wr_in bias_in sq sums rows mix_var mix_root mm x_new xsq x_var x_root hf hfT_psum hfT logits "
        "sub exp mask rank_psum step pool_step done tabs".split())}
    hf_stored = [sem("r_hf_stored0"), sem("r_hf_stored1")]
    mm_free = [sem("r_mm_free0"), sem("r_mm_free1")]
    keep["landed"] = [sem(f"landed{j}") for j in range(PAIRS)]
    TILES = [NT - 1] + list(range(NT - 1))
    block = stack.enter_context(nc.Block())

    @block.sync
    def _(sp):
        sp.dma_start(w_r[:], a["w_router"][0].rearrange("(p k) e -> p k e", p=P)).then_inc(s["wr_in"], 16)
        sp.dma_start(b_r[:], a["b_router"]).then_inc(s["wr_in"], 16)
        sp.dma_start(gffn[:], a["norm_ffn"].to_broadcast([P, D])).then_inc(s["gffn_in"], 16)
        for j in range(8):
            weight_load(sp, a, keep, mid, 0, j).then_inc(keep["landed"][j], 16)
        for q, i in enumerate(TILES):
            if q == NT - 1:
                sp.wait_ge(s["mm"], 2 * NT)
                for j in (8, 9):
                    weight_load(sp, a, keep, mid, 0, j).then_inc(keep["landed"][j], 16)
            sp.wait_ge(s["hf"], q + 1)
            sp.dma_start(scratch["hf"][i * P:i * P + rows(i), :], hf[0:rows(i), q % 2, :]).then_inc(hf_stored[q % 2], 16)
        for j in (10, 11):
            weight_load(sp, a, keep, mid, 0, j).then_inc(keep["landed"][j], 16)
        for c in range(2):
            sp.wait_ge(hf_stored[c], 16 * len(range(c, NT, 2)))

    @block.gpsimd
    def _(pool):
        g = nc.gpsimd
        steps = [0]

        def done(ins):
            steps[0] += 1
            ins.then_inc(s["pool_step"], 1)
            pool.wait_ge(s["pool_step"], steps[0])

        g.iota(iota_i[:], pattern=[[1, P]], base=0, channel_multiplier=0)
        g.iota(tok_i[:], pattern=[[P, NT]], base=0, channel_multiplier=1).then_inc(s["tabs"], 1)
        for h in range(NB):
            if h >= 1:
                pool.wait_ge(s["bias_done"], h)
            for src, c in bias_src[h]:
                for q in range(3):
                    pool.dma_start(bf[q * 32:(q + 1) * 32, c:c + src.shape[1]], src).then_inc(s["bias_in"], 16)
            if h == 0:
                done(g.memset(tb["pick_row"][:], 0.0))
                for q in range(3):
                    v = tb["pick_row"][q * 32:(q + 1) * 32]
                    done(g.affine_select(out=v, in_=v, compare_op=ALU.not_equal, fill=1.0, base=0,
                                         pattern=[[-1, E], [0, P]], channel_multiplier=1))

    @block.scalar
    def _(act):
        nc.scalar.activation(sq[:], ymix[:], ACT.Square).then_inc(s["sq"], 1)
        act.wait_ge(s["mix_var"], 1)
        nc.scalar.activation(ssq[:, 0], ssq[:, 2], ACT.Sqrt).then_inc(s["mix_root"], 1)
        for q, i in enumerate(TILES):
            n = rows(i)
            act.wait_ge(s["x_new"], 2 * (q + 1))
            nc.scalar.activation(jk[0:n], x[0:n, i, :], ACT.Square, accum_out=ss2[0:n, 2, i:i + 1]).then_inc(s["xsq"], 1)
            act.wait_ge(s["x_var"], q + 1)
            nc.scalar.activation(ss2[0:n, 0, i:i + 1], ss2[0:n, 2, i:i + 1], ACT.Sqrt).then_inc(s["x_root"], 1)
            act.wait_ge(s["hfT_psum"], q + 1)
            for c in range(2):
                last = nc.scalar.activation(hfT[:, q % 2, 4 * c:4 * c + 4, 0:n],
                                            bank[4 + c][:].rearrange("p (k t) -> p k t", k=4)[:, :, 0:n], ACT.Copy)
            last.then_inc(s["hfT"], 1)
        act.wait_ge(s["sub"], NT)
        nc.scalar.activation(gate[:], gate[:], ACT.Exp).then_inc(s["exp"], 1)

    @block.tensor
    def _(pe):

        def ssm_sums():
            pe.wait_ge(s["sq"], 2)
            for i in range(NT):
                last = nc.tensor.matmul(bank[7][0:rows(i), i:i + 1], sq[:, 0, i * P:i * P + rows(i)], keep["ones"][:, 0:1], start=True, stop=True)
            last.then_inc(s["sums"], 1)

        def route(q):
            i, n = TILES[q], rows(TILES[q])
            pe.wait_ge(s["hf"], q + 1)
            if q >= 1:
                pe.wait_ge(s["hfT"], q)
            for k in range(KD):
                last = nc.tensor.transpose(bank[4 + k // 4][:, (k % 4) * P:(k % 4) * P + n],
                                           hf[0:n, q % 2, k * P:(k + 1) * P], ident[0:n, 0:n])
            last.then_inc(s["hfT_psum"], 1)
            pe.wait_ge(s["hfT"], q + 1)
            o = bank[6 + q % 2][0:n, 0:E]
            for k in range(KD):
                nc.tensor.matmul(o, hfT[:, q % 2, k, 0:n], w_r[:, k, :], start=(k == 0), stop=False)
            nc.tensor.matmul(o, ones[0:1, 0:n], b_r[:], start=False, stop=True).then_inc(s["logits"], 1)

        for b in range(2):
            pe.wait_ge(keep["wout_in"][b], 16)
        for q, i in enumerate(TILES):
            n = rows(i)
            for h in range(2):
                if q >= 1:
                    pe.wait_ge(mm_free[h], q)
                for c, src in enumerate((ymix, cmix)):
                    for m in range(MT):
                        last = nc.tensor.matmul(bank[2 * h + c][0:n, :], src[:, m, i * P:i * P + n],
                                                w_out[:, MT * c + m, h * 512:(h + 1) * 512], start=(m == 0), stop=(m == MT - 1))
                last.then_inc(s["mm"], 1)
                if q == 0 and h == 0:
                    ssm_sums()
            if q == 0:
                pe.wait_ge(s["consts"], 1)
                pe.wait_ge(s["wr_in"], 32)
            else:
                route(q - 1)
        route(NT - 1)
        pe.wait_ge(s["mask"], NT)
        pe.wait_ge(s["rows"], 1)
        for i in range(NT):
            for j in range(i):
                nc.tensor.matmul(bank[7][:, i * E:(i + 1) * E], ones_b[:], mask_b[:, j, :], start=(j == 0), stop=False)
            nc.tensor.matmul(bank[7][:, i * E:(i + 1) * E], tri[:], mask_b[:, i, :], start=(i == 0), stop=True)
        for j in range(NT):
            last = nc.tensor.matmul(bank[7][:, NT * E:(NT + 1) * E], ones_b[:], mask_b[:, j, :], start=(j == 0), stop=(j == NT - 1))
        last.then_inc(s["rank_psum"], 1)

    @block.vector
    def _(dve):
        v = nc.vector
        steps = [0]

        def done(ins):
            steps[0] += 1
            ins.then_inc(s["step"], 1)
            dve.wait_ge(s["step"], steps[0])

        def bias_parts(h):
            dve.wait_ge(s["bias_in"], 48 * sum(bias_pieces[0:h + 1]))
            out_b = tb["bias"][:, h * HB:(h + 1) * HB]
            done(v.tensor_copy(out_b, bf[:]))
            v.tensor_tensor(bf[32:64, :], bf[32:64, :], out_b[32:64, :], ALU.subtract)
            done(v.tensor_tensor(bf[64:96, :], bf[64:96, :], out_b[64:96, :], ALU.subtract))
            v.tensor_copy(out_b[32:64, :], bf[32:64, :])
            done(v.tensor_copy(out_b[64:96, :], bf[64:96, :]))
            done(v.tensor_tensor(bf[64:96, :], bf[64:96, :], out_b[64:96, :], ALU.subtract))
            v.tensor_copy(out_b[64:96, :], bf[64:96, :]).then_inc(s["bias_done"], 1)

        v.memset(ones[:], 1.0)
        v.memset(ones_b[:], 1.0)
        v.memset(lg[:], 0.0).then_inc(s["consts"], 1)
        v.memset(ssq[:], 1.0)
        done(v.memset(ss2[:], 1.0))
        dve.wait_ge(s["sq"], 1)
        done(v.tensor_tensor(sq[:, 0:2, :], sq[:, 0:2, :], sq[:, 2:4, :], ALU.add))
        v.tensor_tensor(sq[:, 0, :], sq[:, 0, :], sq[:, 1, :], ALU.add).then_inc(s["sq"], 1)
        dve.wait_ge(s["sums"], 1)
        for i in range(NT):
            n = rows(i)
            v.tensor_scalar(ssq[0:n, 2, 2 * i:2 * i + 1], bank[7][0:n, i:i + 1], 1.0 / W, EPS, ALU.mult, ALU.add)
            last = v.tensor_scalar(ssq[0:n, 2, 2 * i + 1:2 * i + 2], keep["conv_ss"][0:n, i:i + 1], 1.0 / W, EPS, ALU.mult, ALU.add)
        last.then_inc(s["mix_var"], 1)
        dve.wait_ge(s["mix_root"], 1)
        refine_rsqrt(nc, done, ssq[:, 0], ssq[:, 1], ssq[:, 2]).then_inc(s["rows"], 1)
        dve.wait_ge(s["rows"], 1)
        dve.wait_ge(s["tabs"], 1)
        v.tensor_copy(tb["iota_s"][:], iota_i[:])
        done(v.tensor_copy(tokv[:], tok_i[:]))
        v.tensor_scalar(valid[:], tokv[:], float(TOK), None, ALU.is_lt)
        v.tensor_scalar(tri[:], tb["iota_s"][:], tokv[:, 0:1], None, ALU.is_gt)
        rank, slotval = tb["rank"], tb["slotval"]
        v.memset(rank[:], -1.0)
        v.memset(slotval[:, :, :, 0], -MISS)
        v.memset(slotval[:, :, :, 1], -1.0 - MISS)
        done(v.memset(slotval[:, :, :, 2], 0.0))
        done(v.tensor_scalar(slotval[:, :, 0:E, 0], tokv[:].unsqueeze(2).to_broadcast([P, NT, E]), -MISS, None, ALU.add))
        done(v.tensor_scalar(tokv[:], tokv[:], 4.0, None, ALU.mult))
        iota_e = tb["iota_s"][:, 0:E]

        def pick_experts(q):
            i, n = TILES[q], rows(TILES[q])
            dve.wait_ge(s["logits"], q + 1)
            done(v.tensor_copy(lg[0:n, i, :], bank[6 + q % 2][0:n, 0:E]))
            done(v.max(out=top[:, i, :], in_=lg[:, i, :]))
            done(v.max_index(out=topi[:, i, :], in_max=top[:, i, :], in_values=lg[:, i, :]))
            v.tensor_tensor(gate[:, i, :], lg[:, i, :], top[:, i, 0:1].to_broadcast([P, E]), ALU.subtract).then_inc(s["sub"], 1)
            done(v.tensor_copy(topf[:, i, :], topi[:, i, :]))
            done(v.tensor_tensor(eqk[:, i], iota_e.unsqueeze(2).to_broadcast([P, E, TOPK]),
                                 topf[:, i, 0:TOPK].unsqueeze(1).to_broadcast([P, E, TOPK]), ALU.is_equal))
            done(v.tensor_reduce(mask[:, i, :], eqk[:, i], AX_X, ALU.add))
            done(v.tensor_scalar(mask[:, i, :], mask[:, i, :], valid[:, i:i + 1], None, ALU.mult))
            v.tensor_copy(mask_b[:, i, :], mask[:, i, :]).then_inc(s["mask"], 1)
            done(v.tensor_tensor_scan(cum[:, i, :], ones[:, 0:E], mask[:, i, :], 0.0, ALU.mult, ALU.add))

        dve.wait_ge(s["gffn_in"], 16)
        dve.wait_ge(keep["x_again"], 16 * NT)
        for q, i in enumerate(TILES):
            n = rows(i)
            for h in range(2):
                dve.wait_ge(s["mm"], 2 * q + h + 1)
                xv = x[0:n, i, h * 512:(h + 1) * 512]
                done(v.scalar_tensor_tensor(out=xv, in0=bank[2 * h][0:n, :], scalar=ssq[0:n, 0, 2 * i:2 * i + 1], in1=xv, op0=ALU.mult, op1=ALU.add))
                done(v.scalar_tensor_tensor(out=xv, in0=bank[2 * h + 1][0:n, :], scalar=ssq[0:n, 0, 2 * i + 1:2 * i + 2], in1=xv, op0=ALU.mult, op1=ALU.add))
                dve.sem_inc(mm_free[h], 1)
                dve.sem_inc(s["x_new"], 1)
            dve.wait_ge(s["xsq"], q + 1)
            v.tensor_scalar(ss2[0:n, 2, i:i + 1], ss2[0:n, 2, i:i + 1], 1.0 / D, EPS, ALU.mult, ALU.add).then_inc(s["x_var"], 1)
            dve.wait_ge(s["x_root"], q + 1)
            done(refine_rsqrt(nc, done, ss2[0:n, 0, i:i + 1], ss2[0:n, 1, i:i + 1], ss2[0:n, 2, i:i + 1]))
            if q >= 2:
                dve.wait_ge(s["hfT_psum"], q - 1)
                dve.wait_ge(hf_stored[q % 2], 16 * (q // 2))
            v.scalar_tensor_tensor(out=hf[0:n, q % 2, :].rearrange("t (k p) -> t p k", p=P), in0=x[0:n, i, :].rearrange("t (p k) -> t p k", p=P),
                                   scalar=ss2[0:n, 0, i:i + 1], in1=gffn[0:n, :].rearrange("t (p k) -> t p k", p=P),
                                   op0=ALU.mult, op1=ALU.mult).then_inc(s["hf"], 1)
            if q < NB:
                bias_parts(q)
            if q >= 1:
                pick_experts(q - 1)
        pick_experts(NT - 1)
        v.scalar_tensor_tensor(out=slotval[:, :, 0:E, 1], in0=cum[:], scalar=-1.0 - MISS, in1=tokv[:].unsqueeze(2).to_broadcast([P, NT, E]),
                               op0=ALU.add, op1=ALU.add)
        dve.wait_ge(s["exp"], 1)
        done(v.tensor_tensor(gate[:], gate[:], mask[:], ALU.mult))
        done(v.tensor_reduce(gsum[:], gate[:], AX_X, ALU.add))
        done(v.tensor_scalar(gsum[:], gsum[:], 1e-30, None, ALU.max))
        done(v.reciprocal(gsum[:], gsum[:]))
        v.tensor_tensor(slotval[:, :, 0:E, 2], gate[:], gsum[:].unsqueeze(2).to_broadcast([P, NT, E]), ALU.mult)
        dve.wait_ge(s["rank_psum"], 1)
        done(v.tensor_scalar(cum[:], bank[7][:, 0:NT * E].rearrange("p (i e) -> p i e", i=NT), 1.0, None, ALU.add))
        done(v.tensor_tensor(cum[:], cum[:], mask[:], ALU.mult))
        v.tensor_scalar(rank[:, :, 0:E], cum[:], -1.0, None, ALU.add)
        c, extra, upto = cnt[:, 0, :], cnt[:, 1, :], cnt[:, 2, :]
        done(v.tensor_copy(c, bank[7][:, NT * E:(NT + 1) * E]))
        done(v.tensor_scalar(extra, c, float(P), None, ALU.is_gt))
        for t in range(2, NT):
            done(v.scalar_tensor_tensor(out=extra, in0=c, scalar=float(t * P), in1=extra, op0=ALU.is_gt, op1=ALU.add))
        done(v.tensor_tensor_scan(upto, ones[:, 0:E], extra, 0.0, ALU.mult, ALU.add))
        b_no = tb["iota_s"][:, 0:NOVER]
        done(v.tensor_tensor(om[:, 0], upto.unsqueeze(1).to_broadcast([P, NOVER, E]),
                             b_no.unsqueeze(2).to_broadcast([P, NOVER, E]), ALU.is_le))
        v.tensor_reduce(of[:, 0, :], om[:, 0], AX_X, ALU.add)
        done(v.tensor_tensor(om[:, 1], om[:, 0], extra.unsqueeze(1).to_broadcast([P, NOVER, E]), ALU.mult))
        done(v.tensor_reduce(of[:, 1, :], om[:, 1], AX_X, ALU.add))
        done(v.tensor_tensor(of[:, 2, :], b_no, of[:, 1, :], ALU.subtract))
        v.tensor_scalar(tb["over_base"][:], of[:, 2, :], 1.0, float(P), ALU.add, ALU.mult)
        v.tensor_scalar(tb["over_i"][:, 0, :], of[:, 0, :], float(E - 1), None, ALU.min)
        v.tensor_tensor(tb["over_i"][:, 1, :], upto[:, E - 1:E].to_broadcast([P, NOVER]), b_no, ALU.is_gt).then_inc(s["done"], 1)
        dve.wait_ge(s["done"], 1)

def experts(nc, a, scratch, stack, sb, sem, bank, keep, mid, tb, landed):
    def buf(name, shape, dt=F32):
        return sb(stack, name, shape, dt)

    ident = keep["ident"]
    ring_lo, ring_hi = keep["ring_lo"], mid["w_out"]
    SPLIT = 4
    w_hi = buf("w_hi", [P, SPLIT, 1024], F32R)
    w_lo = buf("w_lo", [P, SPLIT, 1024], F32R)
    x_hi = buf("x_hi", [P, KD, P], F32R)
    x_lo = buf("x_lo", [P, KD, P], F32R)
    h_hi = buf("h_hi", [P, KD, P], F32R)
    h_lo = buf("h_lo", [P, KD, P], F32R)
    yflat = mid["ymix"][:, :, :].rearrange("p m t -> p (m t)")
    cflat = mid["cmix"][:, :, :].rearrange("p m t -> p (m t)")
    xg, yo = yflat[:, 0:D], yflat[:, D:2 * D]
    g_sb = cflat[:, 0:1024].rearrange("p (h n) -> p h n", h=2)
    u_sb = cflat[:, 1024:2048].rearrange("p (h n) -> p h n", h=2)
    h_sb = buf("h_sb", [P, 2, 512])
    onehot = buf("onehot", [P, NT, P])
    idx_next = buf("idx_next", [P, 2], I32)
    gate_next = buf("gate_next", [P, 1])
    row_cur = buf("row_cur", [P, 1], I32)
    gate_cur = buf("gate_cur", [P, 1])
    zero = buf("zero", [P, 1])

    s = {n: sem("e_" + n) for n in (
        "w_hi w_lo w_used onehot sel_psum idx x_in xT_psum x_hi x_lo gu_psum gu_read g_min sig h hT_psum h_hi h_lo "
        "y_psum y_sb y_stored y_out y_free step curd turns".split())}
    block = stack.enter_context(nc.Block())

    def unit(j):
        return ring_lo[:, j, :] if j < 16 else ring_hi[:, j - 16, :]

    def overflow(eng, work):
        with eng.Fori(0, NOVER // GROUP) as g:
            some = eng.value_load(tb["over_i"][0:1, 1, bass.ds(g * GROUP, 1)], min_val=0, max_val=1)
            with eng.If(some > 0):
                with eng.Fori(0, GROUP) as i:
                    b = g * GROUP + i
                    active = eng.value_load(tb["over_i"][0:1, 1, bass.ds(b, 1)], min_val=0, max_val=1)
                    with eng.If(active > 0):
                        work(b)

    def over_expert(eng, b):
        return eng.value_load(tb["over_i"][0:1, 0, bass.ds(b, 1)], min_val=0, max_val=E - 1)


    @block.sync
    def _(sp):
        def load(e, q):
            for j in range(PAIRS):
                sp.wait_ge(s["w_lo"], UNITS * q + (2 * j + 2 - UNITS))
                weight_load(sp, a, keep, mid, e, j).then_inc(landed[j], 16)

        with sp.Fori(1, E) as e:
            load(e, e)
        overflow(sp, lambda b: load(over_expert(sp, b), b + E))

    @block.gpsimd
    def _(pool):
        nc.gpsimd.memset(xg, 0.0).then_inc(s["turns"], 1)
        pool.sem_inc(s["y_out"], 1)
        pool.wait_ge(s["turns"], 1)

        def gather(q):
            pool.wait_ge(s["idx"], q + 1)
            pool.sem_inc(s["turns"], 1)
            nc.gpsimd.indirect_dma_start(xg, None, scratch["hf"], bass.IndirectOffsetOnAxis(ap=idx_next[:, 0:1].bitcast(U32), axis=0),
                                         bounds_check=TOK - 1, oob_is_err=False).then_inc(s["x_in"], 16)

        def scatter(q):
            pool.wait_ge(s["y_sb"], q + 1)
            pool.sem_inc(s["turns"], 1)
            nc.gpsimd.indirect_dma_start(scratch["picked"], bass.IndirectOffsetOnAxis(ap=row_cur[:, 0:1].bitcast(U32), axis=0), yo, None,
                                         bounds_check=TOK * TOPK - 1, oob_is_err=False).then_inc(s["y_stored"], 16)
            pool.wait_ge(s["y_stored"], 16 * q + 16)
            pool.sem_inc(s["y_out"], 1)

        def over(b):
            gather(b + E)
            scatter(b + E)

        gather(0)
        with pool.Fori(0, E - 1) as e:
            gather(e + 1)
            scatter(e)
        scatter(E - 1)
        overflow(pool, over)

    @block.scalar
    def _(act):
        def split(q, j, first=False):
            if j % 2 == 0:
                act.wait_ge(landed[j // 2], 16 * q + 16)
            if not first:
                act.wait_ge(s["w_used"], UNITS * q + (j + 1 - SPLIT))
            nc.scalar.activation(w_hi[:, j % SPLIT, :], unit(j), ACT.Copy).then_inc(s["w_hi"], 1)

        def take_x(q):
            act.wait_ge(s["xT_psum"], q + 1)
            for h in range(2):
                nc.scalar.activation(x_hi[:, 4 * h:4 * h + 4, :].rearrange("p k t -> p (k t)"), bank[h][:], ACT.Copy).then_inc(s["x_hi"], 1)

        def sigmoid(q, half):
            act.wait_ge(s["g_min"], 2 * q + half + 1)
            nc.scalar.activation(h_sb[:, half, :], g_sb[:, half, :], ACT.Sigmoid, scale=ALPHA).then_inc(s["sig"], 1)

        def take_h(q, half):
            act.wait_ge(s["hT_psum"], 2 * q + half + 1)
            nc.scalar.activation(h_hi[:, 4 * half:4 * half + 4, :].rearrange("p k t -> p (k t)"), bank[6 + half][:], ACT.Copy).then_inc(s["h_hi"], 1)

        def body(q, nxt):
            for j in range(SPLIT, UNITS):
                split(q, j)
                if j == 11:
                    sigmoid(q, 0)
                elif j == 14:
                    take_h(q, 0)
                elif j == 19:
                    sigmoid(q, 1)
                elif j == 21:
                    take_h(q, 1)
            if nxt:
                take_x(q + 1)
                for j in range(SPLIT):
                    split(q + 1, j)
            act.wait_ge(s["y_psum"], q + 1)
            act.wait_ge(s["y_out"], q + 1)
            act.wait_ge(s["curd"], q + 1)
            for h in range(2):
                last = nc.scalar.activation(yo[:, h * 512:(h + 1) * 512], bank[4 + h][:], ACT.Copy, scale=gate_cur[:, 0:1])
            last.then_inc(s["y_sb"], 1)
            act.wait_ge(s["y_sb"], q + 1)
            act.sem_inc(s["y_free"], 1)

        def over(b):
            take_x(b + E)
            for j in range(SPLIT):
                split(b + E, j)
            body(b + E, False)

        act.sem_inc(s["y_free"], 1)
        for j in range(SPLIT):
            split(0, j, first=True)
        take_x(0)
        with act.Fori(0, E - 1) as e:
            body(e, True)
        body(E - 1, False)
        overflow(act, over)

    @block.tensor
    def _(pe):
        def select(e, q):
            pe.wait_ge(s["onehot"], q + 1)
            for i in range(NT):
                last = nc.tensor.matmul(bank[6][:, 0:3], onehot[:, i, :], tb["slotval"][:, i, bass.ds(e, 1), :].rearrange("p a c -> p (a c)"),
                                        start=(i == 0), stop=(i == NT - 1))
            last.then_inc(s["sel_psum"], 1)

        def x_transposes(q):
            pe.wait_ge(s["x_in"], 16 * q + 16)
            for k in range(KD):
                last = nc.tensor.transpose(bank[k // 4][:, (k % 4) * P:(k % 4 + 1) * P], xg[:, k * P:(k + 1) * P], ident[:])
            last.then_inc(s["xT_psum"], 1)

        def h_transposes(q, half):
            pe.wait_ge(s["h"], 2 * q + half + 1)
            for k in range(4):
                last = nc.tensor.transpose(bank[6 + half][:, k * P:(k + 1) * P], h_sb[:, half, k * P:(k + 1) * P], ident[:])
            last.then_inc(s["hT_psum"], 1)

        def products(q, j):
            v_hi, v_lo, k, b = (x_hi, x_lo, j % 8, 2 * (j // 8)) if j < 16 else (h_hi, h_lo, j - 16, 4)
            pe.wait_ge(s["w_lo"], UNITS * q + (j + 1))
            for first, (v, w) in ((True, (v_hi, w_hi)), (False, (v_hi, w_lo)), (False, (v_lo, w_hi))):
                for u in range(2):
                    last = nc.tensor.matmul(bank[b + u][:], v[:, k, :], w[:, j % SPLIT, u * 512:(u + 1) * 512],
                                            start=(k == 0 and first), stop=False)
            last.then_inc(s["w_used"], 1)

        def add_bias(e, b, cols, done):
            for u in range(2):
                last = nc.tensor.matmul(bank[b + u][:], tb["pick_row"][:, bass.ds(e, 1), :].rearrange("p a c -> p (a c)"),
                                        tb["bias"][:, cols[u]:cols[u] + 512], start=False, stop=True)
            last.then_inc(done, 1)

        def body(q, e, nxt):
            pe.wait_ge(s["x_lo"], q + 1)
            for j in range(UNITS):
                if j in (0, 8):
                    pe.wait_ge(s["gu_read"], 2 * q + j // 8 + 1)
                if j == 8 and nxt:
                    select(e + 1, q + 1)
                if j == 12:
                    if nxt:
                        pe.wait_ge(s["idx"], q + 2)
                    h_transposes(q, 0)
                if j == 16:
                    pe.wait_ge(s["h_lo"], 2 * q + 1)
                    pe.wait_ge(s["y_free"], q + 1)
                if j == 19:
                    h_transposes(q, 1)
                if j == 20:
                    if nxt:
                        pe.wait_ge(s["gu_read"], 2 * q + 3)
                        x_transposes(q + 1)
                    pe.wait_ge(s["h_lo"], 2 * q + 2)
                products(q, j)
                if j in (7, 15):
                    half = j // 8
                    add_bias(e, 2 * half, (half * 512, FF + half * 512), s["gu_psum"])
            add_bias(e, 4, (2 * FF, 2 * FF + 512), s["y_psum"])

        def over(b):
            e = over_expert(pe, b)
            select(e, b + E)
            x_transposes(b + E)
            body(b + E, e, False)

        select(0, 0)
        x_transposes(0)
        with pe.Fori(0, E - 1) as e:
            body(e, e, True)
        body(E - 1, E - 1, False)
        overflow(pe, over)

    @block.vector
    def _(dve):
        v = nc.vector

        def pick(e, base):
            v.scalar_tensor_tensor(out=onehot[:], in0=tb["rank"][:, :, bass.ds(e, 1)].to_broadcast([P, NT, P]), scalar=base,
                                   in1=tb["iota_s"][:].unsqueeze(1).to_broadcast([P, NT, P]),
                                   op0=ALU.subtract, op1=ALU.is_equal).then_inc(s["onehot"], 1)

        def take_slots(q):
            dve.wait_ge(s["sel_psum"], q + 1)
            v.tensor_copy(gate_next[:], bank[6][:, 2:3])
            v.tensor_scalar(idx_next[:], bank[6][:, 0:2], MISS, None, ALU.add).then_inc(s["idx"], 1)

        def keep_slots(q):
            dve.wait_ge(s["y_out"], q + 1)
            v.tensor_copy(row_cur[:], idx_next[:, 1:2])
            v.tensor_copy(gate_cur[:], gate_next[:]).then_inc(s["curd"], 1)
            dve.wait_ge(s["curd"], q + 1)

        def split(q, j):
            dve.wait_ge(s["w_hi"], UNITS * q + (j + 1))
            v.tensor_tensor(w_lo[:, j % SPLIT, :], unit(j), w_hi[:, j % SPLIT, :].bitcast(F32), ALU.subtract).then_inc(s["w_lo"], 1)

        def take_x(q):
            for h in range(2):
                dve.wait_ge(s["x_hi"], 2 * q + h + 1)
                c = slice(4 * h, 4 * h + 4)
                last = v.tensor_tensor(x_lo[:, c, :].rearrange("p k t -> p (k t)"), bank[h][:],
                                       x_hi[:, c, :].rearrange("p k t -> p (k t)").bitcast(F32), ALU.subtract)
            last.then_inc(s["x_lo"], 1)

        def take_h(q, half):
            dve.wait_ge(s["h_hi"], 2 * q + half + 1)
            c = slice(4 * half, 4 * half + 4)
            v.tensor_tensor(h_lo[:, c, :].rearrange("p k t -> p (k t)"), bank[6 + half][:],
                            h_hi[:, c, :].rearrange("p k t -> p (k t)").bitcast(F32), ALU.subtract).then_inc(s["h_lo"], 1)

        def swiglu(q, half):
            dve.wait_ge(s["gu_psum"], 2 * q + half + 1)
            g, u = g_sb[:, half, :], u_sb[:, half, :]
            v.tensor_scalar(g, bank[2 * half][:], LIMIT, None, ALU.min).then_inc(s["g_min"], 1)
            v.tensor_scalar(u, bank[2 * half + 1][:], LIMIT, -LIMIT, ALU.min, ALU.max).then_inc(s["gu_read"], 1)
            dve.wait_ge(s["gu_read"], 2 * q + half + 3)
            dve.wait_ge(s["g_min"], 2 * q + half + 1)
            v.scalar_tensor_tensor(out=u, in0=u, scalar=1.0, in1=g, op0=ALU.add, op1=ALU.mult).then_inc(s["step"], 1)
            dve.wait_ge(s["step"], 2 * q + half + 1)
            dve.wait_ge(s["sig"], 2 * q + half + 1)
            v.tensor_tensor(h_sb[:, half, :], u, h_sb[:, half, :], ALU.mult).then_inc(s["h"], 1)

        def body(q, e, nxt):
            if nxt:
                pick(e + 1, zero[:, 0:1])
            for j in range(SPLIT, UNITS):
                if j == 11:
                    swiglu(q, 0)
                elif j == 19:
                    swiglu(q, 1)
                elif j == 21:
                    take_h(q, 1)
                split(q, j)
                if j == 11:
                    keep_slots(q)
                    if nxt:
                        take_slots(q + 1)
                elif j == 14:
                    take_h(q, 0)
            if nxt:
                take_x(q + 1)
                for j in range(SPLIT):
                    split(q + 1, j)

        def over(b):
            pick(over_expert(dve, b), tb["over_base"][:, bass.ds(b, 1)])
            take_slots(b + E)
            take_x(b + E)
            for j in range(SPLIT):
                split(b + E, j)
            body(b + E, 0, False)

        v.memset(zero[:], 0.0).then_inc(s["gu_read"], 2)
        dve.wait_ge(s["gu_read"], 2)
        pick(0, zero[:, 0:1])
        take_slots(0)
        for j in range(SPLIT):
            split(0, j)
        take_x(0)
        with dve.Fori(0, E - 1) as e:
            body(e, e, True)
        body(E - 1, E - 1, False)
        overflow(dve, over)


def combine(nc, a, out, scratch, stack, sb, sem, keep):
    x = keep["x"]
    ring = keep["ring_lo"][:, :, :].rearrange("p (b k) n -> p b k n", k=TOPK)
    NB = 4
    gfin = sb(stack, "gfin", [P, D])
    ssf = sb(stack, "ssf", [P, 3, NT])
    jf = sb(stack, "jf", [P, D])
    of = sb(stack, "of_fin", [P, NT, D])
    g_in, summed, sq, var, root, fin, stored, step = (sem("c_" + n) for n in "g_in summed sq var root fin stored step".split())
    rows_in = [sem(f"c_rows{i}") for i in range(NB)]
    block = stack.enter_context(nc.Block())
    picked = scratch["picked"].rearrange("(t k) n -> t k n", k=TOPK)
    outs = 1 + (NT - 2) + 2

    TILES = [NT - 1] + list(range(NT - 1))

    @block.sync
    def _(sp):
        for q, i in enumerate(TILES):
            if q >= NB:
                sp.wait_ge(summed, q - NB + 1)
            sp.dma_start(ring[0:rows(i), q % NB], picked[i * P:i * P + rows(i)]).then_inc(rows_in[q % NB], 16)
            if q == 0:
                sp.dma_start(gfin[:], a["norm_final"].unsqueeze(0).to_broadcast([P, D])).then_inc(g_in, 16)
        y_p = out["y_p"][0]
        for q, i in enumerate(TILES):
            sp.wait_ge(fin, q + 1)
            if i == 0:
                sp.dma_start(y_p[0:P - NMETA, :], of[NMETA:P, 0, :]).then_inc(stored, 16)
            elif i < NT - 1:
                sp.dma_start(y_p[i * P - NMETA:(i + 1) * P - NMETA, :], of[:, i, :]).then_inc(stored, 16)
            else:
                n = LAST - NDEC
                sp.dma_start(y_p[SEQ - n:SEQ, :], of[0:n, i, :]).then_inc(stored, 16)
                sp.dma_start(out["y_s"][:, 0, :], of[n:LAST, i, :]).then_inc(stored, 16)
        sp.wait_ge(stored, 16 * outs)

    @block.scalar
    def _(act):
        for q, i in enumerate(TILES):
            n = rows(i)
            act.wait_ge(summed, q + 1)
            nc.scalar.activation(jf[0:n], x[0:n, i, :], ACT.Square, accum_out=ssf[0:n, 2, i:i + 1]).then_inc(sq, 1)
            act.wait_ge(var, q + 1)
            nc.scalar.activation(ssf[0:n, 0, i:i + 1], ssf[0:n, 2, i:i + 1], ACT.Sqrt).then_inc(root, 1)

    @block.vector
    def _(dve):
        v = nc.vector
        count = [0]

        def done(ins):
            count[0] += 1
            ins.then_inc(step, 1)
            dve.wait_ge(step, count[0])

        def variance(q):
            i, n = TILES[q], rows(TILES[q])
            dve.wait_ge(sq, q + 1)
            v.tensor_scalar(ssf[0:n, 2, i:i + 1], ssf[0:n, 2, i:i + 1], 1.0 / D, EPS, ALU.mult, ALU.add).then_inc(var, 1)

        def inverse(q):
            i, n = TILES[q], rows(TILES[q])
            dve.wait_ge(root, q + 1)
            done(refine_rsqrt(nc, done, ssf[0:n, 0, i:i + 1], ssf[0:n, 1, i:i + 1], ssf[0:n, 2, i:i + 1]))

        def output(q):
            i, n = TILES[q], rows(TILES[q])
            v.scalar_tensor_tensor(out=of[0:n, i, :], in0=x[0:n, i, :], scalar=ssf[0:n, 0, i:i + 1], in1=gfin[0:n, :],
                                   op0=ALU.mult, op1=ALU.mult).then_inc(fin, 1)

        for q, i in enumerate(TILES):
            n = rows(i)
            dve.wait_ge(rows_in[q % NB], 16 * (q // NB + 1))
            r = ring[0:n, q % NB]
            v.tensor_tensor(r[:, 0], r[:, 0], r[:, 1], ALU.add)
            if q >= 1:
                variance(q - 1)
            done(v.tensor_tensor(r[:, 2], r[:, 2], r[:, 3], ALU.add))
            done(v.tensor_tensor(r[:, 0], r[:, 0], r[:, 2], ALU.add))
            v.tensor_tensor(x[0:n, i, :], x[0:n, i, :], r[:, 0], ALU.add).then_inc(summed, 1)
            if q == 0:
                dve.wait_ge(g_in, 16)
            else:
                inverse(q - 1)
                output(q - 1)
        variance(NT - 1)
        inverse(NT - 1)
        output(NT - 1)


_INS = ["x_prompt", "x_sample", "state_ssm_re", "state_ssm_im", "state_conv", "meta_tokens", "norm_mix", "w_in",
        "ssm_a_re", "ssm_a_im", "ssm_log_dt", "ssm_b_re", "ssm_b_im", "ssm_c_re", "ssm_c_im", "ssm_d", "w_glu", "b_glu",
        "conv_w", "norm_out_ssm", "norm_out_conv", "w_out", "norm_ffn", "w_router", "b_router", "w_gate_up",
        "b_gate_up", "w_down", "b_down", "norm_final"]
_OUTS = [("y_p", (1, SEQ, D)), ("y_s", (NDEC, 1, D)), ("re_p", (1, 1, GROUPS, NS)), ("im_p", (1, 1, GROUPS, NS)),
         ("conv_p", (1, 1, 2, W)), ("re_s", (1, NDEC, GROUPS, NS)), ("im_s", (1, NDEC, GROUPS, NS)), ("conv_s", (1, NDEC, 2, W))]


def kernel(**inputs):
    import numpy as np
    import concourse.bacc as bacc
    from concourse.bass_utils import run_bass_kernel_spmd

    nc = bacc.Bacc("TRN2", target_bir_lowering=False, num_devices=1)
    arrays, a = {}, {}
    for name in _INS:
        v = np.ascontiguousarray(inputs[name])
        arrays[f"in_{name}"] = v
        a[name] = nc.dram_tensor(f"in_{name}", v.shape, mybir.dt.from_np(v.dtype), kind="ExternalInput").ap()
    out = {n: nc.dram_tensor(f"out_{n}", shape, F32, kind="ExternalOutput").ap() for n, shape in _OUTS}
    hybrid_step(nc, a, out)
    r = run_bass_kernel_spmd(nc, [arrays], core_ids=[0])
    return tuple(r.results[0][f"out_{n}"] for n, _ in _OUTS)
```
